# Optimizing a Trainium2 kernel written in Bass

```python
import math, functools
import jax, jax.numpy as jnp
from jax import lax
import numpy as np

D_MODEL = 1024
BATCH = 1
SEQ = 512
DEPTH = 1
DEC_BATCH = 8
DEC_SEQ = 8
PAST_LEN = 2048
PAGE_SIZE = 128

SSM_EXPAND = 2
D_INNER = SSM_EXPAND * D_MODEL
SSM_HEAD_DIM = 64
SSM_HEADS = D_INNER // SSM_HEAD_DIM
SSM_GROUPS = 4
SSM_HPG = SSM_HEADS // SSM_GROUPS
SSM_STATE = 128
CONV_WIDTH = 4
CONV_DIM = D_INNER + 2 * SSM_GROUPS * SSM_STATE
SSD_CHUNK = 128
ATTN_HEADS = 16
ATTN_HEAD_DIM = 64
ATTN_WIDTH = ATTN_HEADS * ATTN_HEAD_DIM
KV_HEADS = 2
HEADS_PER_KV = ATTN_HEADS // KV_HEADS
KV_WIDTH = 2 * KV_HEADS * ATTN_HEAD_DIM
CMP_BLOCK = 64
SEL_BLOCK = CMP_BLOCK
SEL_TOPK = 16
SEL_BONUS = 1000.0
WINDOW = 512
WIN_QBLOCK = 128
SEL_QBLOCK = 32
ATTN_SCALE = ATTN_HEAD_DIM ** -0.5
PEER_HEADS = 8
PEER_KEYS = 128
N_EXPERTS = PEER_KEYS * PEER_KEYS
PEER_QDIM = 256
PEER_HALF = PEER_QDIM // 2
PEER_TOPK = 16
PEER_TOKEN_CHUNK = 128
EPS = 1e-6
PROJ_SIZES = (D_INNER, CONV_DIM, SSM_HEADS, ATTN_WIDTH, KV_WIDTH, KV_WIDTH, KV_WIDTH, 3 * ATTN_HEADS, 2 * D_MODEL)
PROJ_DIM = sum(PROJ_SIZES)

kernel_name = 'mamba2_nsa_peer_hybrid_step'

def _rmsnorm(x, w):
    xf = x.astype(jnp.float32)
    y = xf * lax.rsqrt(jnp.mean(xf * xf, axis=-1, keepdims=True) + EPS)
    return (y * w.astype(jnp.float32)).astype(x.dtype)

def _masked_softmax(s, mask):
    s = jnp.where(mask, s.astype(jnp.float32), -jnp.inf)
    m = jnp.max(s, axis=-1, keepdims=True)
    m = jnp.where(jnp.isfinite(m), m, 0.0)
    p = jnp.exp(s - m)
    return p / jnp.maximum(jnp.sum(p, axis=-1, keepdims=True), 1e-30)

def _split_proj(p):
    idx = np.cumsum(PROJ_SIZES)[:-1].tolist()
    return jnp.split(p, idx, axis=-1)

def _to_blocks(a, blk):
    b, T = a.shape[:2]
    return jnp.moveaxis(a.reshape(b, T // blk, blk, *a.shape[2:]), 1, 0)

def _from_blocks(a):
    nb, b, blk = a.shape[:3]
    return jnp.moveaxis(a, 0, 1).reshape(b, nb * blk, *a.shape[3:])

def _causal_conv(xbc, conv_prev, conv_w, conv_b):
    xp = jnp.concatenate([conv_prev.astype(xbc.dtype), xbc], axis=1)
    y = lax.conv_general_dilated(xp, conv_w.astype(xbc.dtype)[:, None, :], window_strides=(1,), padding='VALID',
                                 dimension_numbers=('NWC', 'WIO', 'NWC'), feature_group_count=CONV_DIM)
    return jax.nn.silu(y + conv_b.astype(xbc.dtype)), xp[:, -(CONV_WIDTH - 1):]

def _ssd(x, dt, A, Bm, Cm, h0, chunk):
    f32 = jnp.float32
    b, L = x.shape[:2]
    nc = L // chunk
    xc = x.astype(f32).reshape(b, nc, chunk, SSM_GROUPS, SSM_HPG, SSM_HEAD_DIM)
    dtc = dt.reshape(b, nc, chunk, SSM_GROUPS, SSM_HPG)
    Bc = Bm.astype(f32).reshape(b, nc, chunk, SSM_GROUPS, SSM_STATE)
    Cc = Cm.astype(f32).reshape(b, nc, chunk, SSM_GROUPS, SSM_STATE)
    a_cum = jnp.cumsum(dtc * A.reshape(SSM_GROUPS, SSM_HPG), axis=2)
    tril = jnp.tril(jnp.ones((chunk, chunk), bool))[:, :, None, None]
    diff = a_cum[:, :, :, None] - a_cum[:, :, None]
    decay = jnp.exp(jnp.where(tril, diff, -jnp.inf))
    xdt = xc * dtc[..., None]
    cb = jnp.einsum('bclgn,bcsgn->bclsg', Cc, Bc)
    y_diag = jnp.einsum('bclsgj,bcsgjp->bclgjp', cb[..., None] * decay, xdt)
    decay_to_end = jnp.exp(a_cum[:, :, -1:] - a_cum)
    chunk_states = jnp.einsum('bclgn,bclgjp->bcgjpn', Bc, xdt * decay_to_end[..., None])
    chunk_decay = jnp.exp(a_cum[:, :, -1])

    def step(h, inp):
        s_c, d_c = inp
        return h * d_c[..., None, None] + s_c, h

    h_init = h0.astype(f32).reshape(b, SSM_GROUPS, SSM_HPG, SSM_HEAD_DIM, SSM_STATE)
    h_last, h_prev = lax.scan(step, h_init, (jnp.moveaxis(chunk_states, 1, 0), jnp.moveaxis(chunk_decay, 1, 0)))
    h_prev = jnp.moveaxis(h_prev, 0, 1)
    y_off = jnp.einsum('bclgn,bcgjpn->bclgjp', Cc, h_prev) * jnp.exp(a_cum)[..., None]
    y = (y_diag + y_off).reshape(b, L, SSM_HEADS, SSM_HEAD_DIM)
    return y, h_last.reshape(b, SSM_HEADS, SSM_HEAD_DIM, SSM_STATE)

def _mamba_branch(z, xbc, dt_raw, conv_prev, ssm_prev, conv_w, conv_b, dt_bias, a_log, d_skip, ssm_norm_w):
    f32 = jnp.float32
    b, L, _ = xbc.shape
    xbc, conv_new = _causal_conv(xbc, conv_prev, conv_w, conv_b)
    gn = SSM_GROUPS * SSM_STATE
    xs = xbc[..., :D_INNER].reshape(b, L, SSM_HEADS, SSM_HEAD_DIM)
    Bm = xbc[..., D_INNER:D_INNER + gn].reshape(b, L, SSM_GROUPS, SSM_STATE)
    Cm = xbc[..., D_INNER + gn:].reshape(b, L, SSM_GROUPS, SSM_STATE)
    dt = jax.nn.softplus(dt_raw.astype(f32) + dt_bias.astype(f32))
    A = -jnp.exp(a_log.astype(f32))
    y, ssm_new = _ssd(xs, dt, A, Bm, Cm, ssm_prev, math.gcd(L, SSD_CHUNK))
    y = y + d_skip.astype(f32)[:, None] * xs.astype(f32)
    y = y.reshape(b, L, D_INNER) * jax.nn.silu(z.astype(f32))
    y = _rmsnorm(y, ssm_norm_w).astype(z.dtype)
    return y, conv_new, ssm_new.astype(ssm_prev.dtype)

def _cmp_attend(q, cmp_kv, q_pos):
    n = cmp_kv.shape[1]
    blk_end = jnp.arange(n) * CMP_BLOCK + (CMP_BLOCK - 1)
    s = jnp.einsum('btgjd,bngd->btgjn', q, cmp_kv[..., 0, :]).astype(jnp.float32) * ATTN_SCALE
    mask = (blk_end[None, :] <= q_pos[:, None])[None, :, None, None, :]
    p = _masked_softmax(s, mask)
    o = jnp.einsum('btgjn,bngd->btgjd', p.astype(cmp_kv.dtype), cmp_kv[..., 1, :])
    return o, jnp.sum(p, axis=3)

def _select_blocks(imp, q_pos, n_sel):
    imp = jnp.pad(imp, ((0, 0), (0, 0), (0, 0), (0, n_sel - imp.shape[-1])))
    j = jnp.arange(n_sel)[None, :]
    cur = (q_pos // SEL_BLOCK)[:, None]
    forced = ((j == 0) | (j == cur) | (j == cur - 1)).astype(jnp.float32)
    score = jnp.where((j <= cur)[None, :, None, :], imp + SEL_BONUS * forced[None, :, None, :], -jnp.inf)
    _, idx = lax.top_k(score, min(SEL_TOPK, n_sel))
    return idx

def _block_positions(idx):
    pos = idx[..., None] * SEL_BLOCK + jnp.arange(SEL_BLOCK)
    return pos.reshape(*idx.shape[:-1], -1)

def _sel_attend(q, rows, pos, q_pos):
    s = jnp.einsum('btgjd,btgsd->btgjs', q, rows[..., 0, :]).astype(jnp.float32) * ATTN_SCALE
    mask = (pos <= q_pos[None, :, None, None])[:, :, :, None, :]
    p = _masked_softmax(s, mask)
    return jnp.einsum('btgjs,btgsd->btgjd', p.astype(rows.dtype), rows[..., 1, :])

def _band_attend(q, kv, q_pos, k_pos):
    s = jnp.einsum('btgjd,bsgd->btgjs', q, kv[..., 0, :]).astype(jnp.float32) * ATTN_SCALE
    rel = q_pos[:, None] - k_pos[None, :]
    mask = ((rel >= 0) & (rel <= WINDOW) & (k_pos[None, :] >= 0))[None, :, None, None, :]
    p = _masked_softmax(s, mask)
    return jnp.einsum('btgjs,bsgd->btgjd', p.astype(kv.dtype), kv[..., 1, :])

def _combine(gates, o_cmp, o_sel, o_win):
    o = gates[..., 0:1] * o_cmp.astype(jnp.float32) + gates[..., 1:2] * o_sel.astype(jnp.float32) \
        + gates[..., 2:3] * o_win.astype(jnp.float32)
    return o.astype(o_cmp.dtype)

def _nsa_prompt(q, kv_cmp, kv_sel, kv_win, gates):
    b, T = q.shape[:2]
    q_pos = jnp.arange(T)
    n_blk = T // CMP_BLOCK
    cmp_kv = kv_cmp.reshape(b, n_blk, CMP_BLOCK, KV_HEADS, 2, ATTN_HEAD_DIM).mean(axis=2)
    o_cmp, imp = _cmp_attend(q, cmp_kv, q_pos)
    idx = _select_blocks(imp, q_pos, n_blk)
    bidx = jnp.arange(b)[:, None, None, None]
    gidx = jnp.arange(KV_HEADS)[None, None, :, None]

    def sel_block(args):
        qb, ib, pb = args
        pos = _block_positions(ib)
        return _sel_attend(qb, kv_sel[bidx, pos, gidx], pos, pb)

    o_sel = _from_blocks(lax.map(sel_block, (_to_blocks(q, SEL_QBLOCK), _to_blocks(idx, SEL_QBLOCK),
                                             q_pos.reshape(-1, SEL_QBLOCK))))
    kv_pad = jnp.pad(kv_win, ((0, 0), (WINDOW, 0), (0, 0), (0, 0), (0, 0)))
    span = WINDOW + WIN_QBLOCK

    def win_block(args):
        qb, start = args
        kb = lax.dynamic_slice_in_dim(kv_pad, start, span, axis=1)
        return _band_attend(qb, kb, start + jnp.arange(WIN_QBLOCK), start - WINDOW + jnp.arange(span))

    starts = jnp.arange(T // WIN_QBLOCK) * WIN_QBLOCK
    o_win = _from_blocks(lax.map(win_block, (_to_blocks(q, WIN_QBLOCK), starts)))
    return _combine(gates, o_cmp, o_sel, o_win), kv_win[:, -min(WINDOW, T):]

def _gather_paged_rows(pool, page_table, new_rows, pos):
    past = page_table.shape[1] * PAGE_SIZE
    b = page_table.shape[0]
    bidx = jnp.arange(b)[:, None, None, None]
    gidx = jnp.arange(KV_HEADS)[None, None, :, None]
    past_pos = jnp.minimum(pos, past - 1)
    phys = page_table[bidx, past_pos // PAGE_SIZE]
    from_pool = pool[phys, past_pos % PAGE_SIZE, gidx]
    new_pos = jnp.clip(pos - past, 0, new_rows.shape[1] - 1)
    from_new = new_rows[bidx, new_pos, gidx]
    return jnp.where((pos < past)[..., None, None], from_pool.astype(new_rows.dtype), from_new)

def _nsa_sample(pool_cmp, pool_sel, win_buf, page_table, q, kv_cmp, kv_sel, kv_win, gates):
    b, T = q.shape[:2]
    n_pages = page_table.shape[1]
    past = n_pages * PAGE_SIZE
    q_pos = past + jnp.arange(T)
    past_cmp = pool_cmp[page_table].reshape(b, past // CMP_BLOCK, CMP_BLOCK, KV_HEADS, 2, ATTN_HEAD_DIM).mean(axis=2)
    n_new = T // CMP_BLOCK
    new_cmp = kv_cmp[:, :n_new * CMP_BLOCK].reshape(b, n_new, CMP_BLOCK, KV_HEADS, 2, ATTN_HEAD_DIM).mean(axis=2)
    cmp_kv = jnp.concatenate([past_cmp.astype(kv_cmp.dtype), new_cmp], axis=1)
    o_cmp, imp = _cmp_attend(q, cmp_kv, q_pos)
    n_sel = -(-(past + T) // SEL_BLOCK)
    idx = _select_blocks(imp, q_pos, n_sel)
    pos = _block_positions(idx)
    o_sel = _sel_attend(q, _gather_paged_rows(pool_sel, page_table, kv_sel, pos), pos, q_pos)
    w_eff = win_buf.shape[1]
    keys = jnp.concatenate([win_buf.astype(kv_win.dtype), kv_win], axis=1)
    o_win = _band_attend(q, keys, q_pos, past - w_eff + jnp.arange(w_eff + T))
    return _combine(gates, o_cmp, o_sel, o_win), keys[:, -w_eff:]

def _peer(h, peer_wq, peer_sub_keys, peer_u, peer_v):
    n = h.shape[0]
    q = (h @ peer_wq).reshape(n, PEER_HEADS, 2, PEER_HALF)
    s = jnp.einsum('nhcd,hckd->nhck', q, peer_sub_keys).astype(jnp.float32)
    top_s, top_i = lax.top_k(s, PEER_TOPK)
    cand_s = (top_s[:, :, 0, :, None] + top_s[:, :, 1, None, :]).reshape(n, PEER_HEADS, -1)
    cand_i = (top_i[:, :, 0, :, None] * PEER_KEYS + top_i[:, :, 1, None, :]).reshape(n, PEER_HEADS, -1)
    best_s, best_pos = lax.top_k(cand_s, PEER_TOPK)
    experts = jnp.take_along_axis(cand_i, best_pos, axis=-1)
    g = jax.nn.softmax(best_s, axis=-1)
    act = jax.nn.gelu(jnp.einsum('nd,nhkd->nhk', h, peer_u[experts]).astype(jnp.float32))
    return jnp.einsum('nhk,nhkd->nd', (g * act).astype(peer_v.dtype), peer_v[experts])

def _peer_tokens(h, peer_wq, peer_sub_keys, peer_u, peer_v):
    shape = h.shape
    hf = h.reshape(-1, D_MODEL)
    n = hf.shape[0]
    if n % PEER_TOKEN_CHUNK == 0 and n > PEER_TOKEN_CHUNK:
        out = lax.map(lambda c: _peer(c, peer_wq, peer_sub_keys, peer_u, peer_v),
                      hf.reshape(-1, PEER_TOKEN_CHUNK, D_MODEL)).reshape(n, D_MODEL)
    else:
        out = _peer(hf, peer_wq, peer_sub_keys, peer_u, peer_v)
    return out.reshape(shape)

def _block(x, conv_prev, ssm_prev, nsa_core, norm_mix_w, w_in, conv_w, conv_b, dt_bias, a_log, d_skip, ssm_norm_w,
           w_ssm_branch, w_attn_branch, w_out, norm_ffn_w, peer_wq, peer_sub_keys, peer_u, peer_v):
    b, T, _ = x.shape
    h = _rmsnorm(x, norm_mix_w)
    z, xbc, dt_raw, q, kv_c, kv_s, kv_w, nsa_g, br_g = _split_proj(h @ w_in)
    y_ssm, conv_new, ssm_new = _mamba_branch(z, xbc, dt_raw, conv_prev, ssm_prev, conv_w, conv_b, dt_bias, a_log,
                                             d_skip, ssm_norm_w)
    q = q.reshape(b, T, KV_HEADS, HEADS_PER_KV, ATTN_HEAD_DIM)
    kv_c = kv_c.reshape(b, T, KV_HEADS, 2, ATTN_HEAD_DIM)
    kv_s = kv_s.reshape(b, T, KV_HEADS, 2, ATTN_HEAD_DIM)
    kv_w = kv_w.reshape(b, T, KV_HEADS, 2, ATTN_HEAD_DIM)
    gates = jax.nn.sigmoid(nsa_g.astype(jnp.float32)).reshape(b, T, KV_HEADS, HEADS_PER_KV, 3)
    o_attn, win_new = nsa_core(q, kv_c, kv_s, kv_w, gates)
    y_attn = o_attn.reshape(b, T, ATTN_WIDTH) @ w_attn_branch
    g = jax.nn.sigmoid(br_g.astype(jnp.float32))
    merged = (g[..., :D_MODEL] * (y_ssm @ w_ssm_branch).astype(jnp.float32)
              + g[..., D_MODEL:] * y_attn.astype(jnp.float32)).astype(x.dtype)
    x = x + merged @ w_out
    x = x + _peer_tokens(_rmsnorm(x, norm_ffn_w), peer_wq, peer_sub_keys, peer_u, peer_v)
    return x, kv_c, kv_s, win_new, conv_new, ssm_new

def setup_inputs(seed: int = 0) -> dict:
    key = jax.random.key(seed)
    ks = jax.random.split(key, 24)
    f32 = jnp.float32
    n_pages = PAST_LEN // PAGE_SIZE
    n_pool = (DEC_BATCH * n_pages * 5) // 4
    w_eff = min(WINDOW, PAST_LEN)

    def nrm(k, shape, scale):
        return jax.random.normal(k, shape, f32) * scale

    dt0 = jnp.exp(jax.random.uniform(ks[10], (DEPTH, SSM_HEADS), f32) * (math.log(0.1) - math.log(0.001)) + math.log(0.001))
    return {
        'x_prompt': nrm(ks[0], (BATCH, SEQ, D_MODEL), 1.0),
        'x_sample': nrm(ks[1], (DEC_BATCH, DEC_SEQ, D_MODEL), 1.0),
        'cache_cmp_kv': nrm(ks[2], (DEPTH, n_pool, PAGE_SIZE, KV_HEADS, 2, ATTN_HEAD_DIM), 1.0),
        'cache_sel_kv': nrm(ks[3], (DEPTH, n_pool, PAGE_SIZE, KV_HEADS, 2, ATTN_HEAD_DIM), 1.0),
        'cache_win_kv': nrm(ks[4], (DEPTH, DEC_BATCH, w_eff, KV_HEADS, 2, ATTN_HEAD_DIM), 1.0),
        'state_ssm': nrm(ks[5], (DEPTH, DEC_BATCH, SSM_HEADS, SSM_HEAD_DIM, SSM_STATE), 0.3),
        'state_conv': nrm(ks[6], (DEPTH, DEC_BATCH, CONV_WIDTH - 1, CONV_DIM), 1.0),
        'page_table': jax.random.permutation(ks[7], n_pool)[:DEC_BATCH * n_pages].reshape(DEC_BATCH, n_pages).astype(jnp.int32),
        'norm_mix_w': 1.0 + nrm(ks[8], (DEPTH, D_MODEL), 0.02),
        'w_in': nrm(ks[9], (DEPTH, D_MODEL, PROJ_DIM), D_MODEL ** -0.5),
        'conv_w': nrm(ks[11], (DEPTH, CONV_WIDTH, CONV_DIM), CONV_WIDTH ** -0.5),
        'conv_b': nrm(ks[12], (DEPTH, CONV_DIM), 0.02),
        'dt_bias': dt0 + jnp.log(-jnp.expm1(-dt0)),
        'a_log': jnp.log(jax.random.uniform(ks[13], (DEPTH, SSM_HEADS), f32, 1.0, 16.0)),
        'd_skip': 1.0 + nrm(ks[14], (DEPTH, SSM_HEADS), 0.02),
        'ssm_norm_w': 1.0 + nrm(ks[15], (DEPTH, D_INNER), 0.02),
        'w_ssm_branch': nrm(ks[16], (DEPTH, D_INNER, D_MODEL), D_INNER ** -0.5),
        'w_attn_branch': nrm(ks[17], (DEPTH, ATTN_WIDTH, D_MODEL), ATTN_WIDTH ** -0.5),
        'w_out': nrm(ks[18], (DEPTH, D_MODEL, D_MODEL), D_MODEL ** -0.5),
        'norm_ffn_w': 1.0 + nrm(ks[19], (DEPTH, D_MODEL), 0.02),
        'peer_wq': nrm(ks[20], (DEPTH, D_MODEL, PEER_HEADS * PEER_QDIM), D_MODEL ** -0.5),
        'peer_sub_keys': nrm(ks[21], (DEPTH, PEER_HEADS, 2, PEER_KEYS, PEER_HALF), PEER_HALF ** -0.5),
        'peer_u': nrm(ks[22], (DEPTH, N_EXPERTS, D_MODEL), D_MODEL ** -0.5),
        'peer_v': nrm(ks[23], (DEPTH, N_EXPERTS, D_MODEL), PEER_HEADS ** -0.5),
        'final_norm_w': 1.0 + nrm(jax.random.fold_in(key, 99), (D_MODEL,), 0.02),
    }

def reference(x_prompt, x_sample, cache_cmp_kv, cache_sel_kv, cache_win_kv, state_ssm, state_conv, page_table,
              norm_mix_w, w_in, conv_w, conv_b, dt_bias, a_log, d_skip, ssm_norm_w, w_ssm_branch, w_attn_branch,
              w_out, norm_ffn_w, peer_wq, peer_sub_keys, peer_u, peer_v, final_norm_w):
    xp, xs = x_prompt, x_sample
    cmp_p, cmp_s, sel_p, sel_s, win_p, win_s = [], [], [], [], [], []
    ssm_p, ssm_s, conv_p, conv_s = [], [], [], []
    for layer in range(DEPTH):
        lw = [a[layer] for a in (norm_mix_w, w_in, conv_w, conv_b, dt_bias, a_log, d_skip, ssm_norm_w, w_ssm_branch,
                                 w_attn_branch, w_out, norm_ffn_w, peer_wq, peer_sub_keys, peer_u, peer_v)]
        bp = xp.shape[0]
        conv0 = jnp.zeros((bp, CONV_WIDTH - 1, CONV_DIM), xp.dtype)
        ssm0 = jnp.zeros((bp, SSM_HEADS, SSM_HEAD_DIM, SSM_STATE), xp.dtype)
        xp, kc, ks, kw, cv, ss = _block(xp, conv0, ssm0, _nsa_prompt, *lw)
        cmp_p.append(kc); sel_p.append(ks); win_p.append(kw); conv_p.append(cv); ssm_p.append(ss)
        core = functools.partial(_nsa_sample, cache_cmp_kv[layer], cache_sel_kv[layer], cache_win_kv[layer], page_table)
        xs, kc, ks, kw, cv, ss = _block(xs, state_conv[layer], state_ssm[layer], core, *lw)
        cmp_s.append(kc); sel_s.append(ks); win_s.append(kw); conv_s.append(cv); ssm_s.append(ss)
    y_prompt = _rmsnorm(xp, final_norm_w)
    y_sample = _rmsnorm(xs, final_norm_w)
    return (y_prompt, y_sample, jnp.stack(cmp_p), jnp.stack(cmp_s), jnp.stack(sel_p), jnp.stack(sel_s),
            jnp.stack(win_p), jnp.stack(win_s), jnp.stack(ssm_p), jnp.stack(ssm_s), jnp.stack(conv_p), jnp.stack(conv_s))


_drawn_inputs = setup_inputs


def setup_inputs(seed=0):
    import zlib

    import numpy as np

    out = dict(_drawn_inputs(seed))
    spreads = {}
    factors = {'d_skip': 13.629,
     'ssm_norm_w': 2.985,
     'final_norm_w': 8.139,
     'cache_cmp_kv': 5.153,
     'cache_sel_kv': 4.931,
     'norm_ffn_w': 3.978}
    for name, (base, spread) in spreads.items():
        noise = np.random.default_rng([zlib.crc32(name.encode()), seed]).standard_normal(out[name].shape)
        drawn = base * np.exp(spread * noise) if base else spread * noise
        out[name] = __import__('jax').numpy.asarray(drawn.astype(out[name].dtype))
    for name, factor in factors.items():
        out[name] = (out[name] * factor).astype(out[name].dtype)
    return out
```

```python
from contextlib import ExitStack

import concourse.bass as bass
from concourse import mybir

F32 = mybir.dt.float32
BF16 = mybir.dt.bfloat16
U32 = mybir.dt.uint32
I32 = mybir.dt.int32
ALU = mybir.AluOpType
ACT = mybir.ActivationFunctionType
AX = mybir.AxisListType

P = 128
D = 1024
SEQ = 512
NB = 8
DS = 8
NS = NB * DS
T = SEQ + NS
TILES = 5
KD = D // P
D_INNER = 2048
HEADS = 32
HP = 64
GROUPS = 4
STATE = 128
CONV_W = 4
CONV_DIM = D_INNER + 2 * GROUPS * STATE
CT_TILES = CONV_DIM // P
AH = 16
HD = 64
KVH = 2
HPK = AH // KVH
PAST = 2048
PAGE = 128
NPAGES = PAST // PAGE
WINDOW = 512
CMP = 64
NCMP_P = SEQ // CMP
NCMP_S = PAST // CMP
NSEL = NCMP_S + 1
TOPK = 16
SCALE = HD ** -0.5
PH = 8
PKEYS = 128
EPS = 1e-6
NEG = -1e30

COL_Z = 0
COL_XBC = D_INNER
COL_DT = COL_XBC + CONV_DIM
COL_Q = COL_DT + HEADS
COL_KV = COL_Q + AH * HD
KVW = 2 * KVH * HD
COL_NG = COL_KV + 3 * KVW
COL_BG = COL_NG + 3 * AH
PROJ = COL_BG + 2 * D


def rows(t):
    return P if t < TILES - 1 else NS


def yT(k, t):
    return k.xnat[:, t, 0:16 * rows(t)].rearrange("p (f n) -> p f n", f=16)


def w_view(w, c0, n):
    return w[:, c0:c0 + n].rearrange("(k p) n -> p k n", p=P)


class Shared:
    pass


class Link:

    def __init__(self, eng, sem):
        self.eng, self.sem, self.n = eng, sem, 0

    def __call__(self, ins):
        self.n += 1
        ins.then_inc(self.sem, 1)
        self.eng.wait_ge(self.sem, self.n)


def stage_norm(nc, k):
    with ExitStack() as ctx:
        sb = lambda n, s, d=F32: ctx.enter_context(nc.sbuf_tensor(n, s, d))
        sem = lambda n: ctx.enter_context(nc.semaphore(n))
        x = sb("n_x", [P, TILES, D])
        junk = sb("n_junk", [P, D])
        vec_a = sb("n_vec_a", [32, P])
        vec_b = sb("n_vec_b", [120, P])
        ss = sb("n_ss", [P, TILES])
        mean = sb("n_mean", [P, TILES])
        root = sb("n_root", [P, TILES])
        rstd = sb("n_rstd", [P, TILES])
        x_in = [sem(f"n_x_in{t}") for t in range(TILES)]
        vec_in, const_set, consts_done = sem("n_vec_in"), sem("n_const_set"), sem("n_consts_done")
        squared, mean_done, rooted = sem("n_squared"), sem("n_mean_done"), sem("n_rooted")
        scaled, turned, vec_turned, evacuated, dve_own = (
            sem("n_scaled"), sem("n_turned"), sem("n_vec_turned"), sem("n_evacuated"), sem("n_dve_own"))
        block = ctx.enter_context(nc.Block())

        @block.sync
        def _(sp):
            for t in range(TILES):
                src = k.x_prompt[0, P * t:P * t + P, :] if t < 4 else k.x_sample.rearrange("b s d -> (b s) d")
                sp.dma_start(x[0:rows(t), t, :], src).then_inc(x_in[t], 16)
            for dst, src in (
                (vec_a[0:8, :], k.norm_mix_w[0].rearrange("(a p) -> a p", p=P)),
                (vec_a[8:16, :], k.norm_ffn_w[0].rearrange("(a p) -> a p", p=P)),
                (vec_a[16:32, :], k.ssm_norm_w[0].rearrange("(a p) -> a p", p=P)),
                (vec_b[0:24, :], k.conv_b[0].rearrange("(a p) -> a p", p=P)),
                (vec_b[24:120, :], k.conv_w[0].rearrange("w (a p) -> (w a) p", p=P)),
                (k.dt_bias_row[:], k.dt_bias.partition_broadcast(P)[:, 0, :]),
                (k.a_row[:], k.a_log.partition_broadcast(P)[:, 0, :]),
                (k.dskip_row[:], k.d_skip.partition_broadcast(P)[:, 0, :]),
            ):
                sp.dma_start(dst, src).then_inc(vec_in, 16)

        @block.gpsimd
        def _(pool):
            own = Link(pool, const_set)
            g = nc.gpsimd
            own(g.memset(k.ident[:], 0.0))
            own(g.affine_select(out=k.ident[:], in_=k.ident[:], compare_op=ALU.not_equal, fill=1.0, base=0,
                                pattern=[[-1, P]], channel_multiplier=1))
            own(g.tensor_copy(k.identb[:], k.ident[:]))
            own(g.memset(k.ones[:], 1.0))
            own(g.affine_select(out=k.cum[:], in_=k.ones[:], compare_op=ALU.is_ge, fill=0.0, base=0,
                                pattern=[[1, P]], channel_multiplier=-1))
            own(g.memset(k.later[:], 0.0))
            own(g.affine_select(out=k.later[:], in_=k.later[:], compare_op=ALU.is_ge, fill=NEG, base=0,
                                pattern=[[1, P]], channel_multiplier=-1))
            own(g.memset(k.causal[:], 0.0))
            own(g.affine_select(out=k.causal[:], in_=k.causal[:], compare_op=ALU.is_ge, fill=NEG, base=0,
                                pattern=[[-1, P]], channel_multiplier=1))
            same = k.same[:].rearrange("p (b t) -> p b t", b=NB)
            own(g.memset(k.same[:], 1.0))
            own(g.affine_select(out=same, in_=same, compare_op=ALU.is_ge, fill=0.0, base=0,
                                pattern=[[-DS, NB], [0, DS]], channel_multiplier=1))
            own(g.affine_select(out=same, in_=same, compare_op=ALU.is_ge, fill=0.0, base=DS - 1,
                                pattern=[[DS, NB], [0, DS]], channel_multiplier=-1))
            own(g.tensor_tensor(k.cum_s[:], k.same[:], k.cum[0:NS, 0:NS], ALU.mult))
            g.tensor_scalar(k.later_s[:], k.cum_s[:], -NEG, NEG, ALU.mult, ALU.add).then_inc(consts_done, 1)

        @block.scalar
        def _(act):
            for t in range(TILES):
                r = rows(t)
                act.wait_ge(x_in[t], 16)
                if t:
                    act.wait_ge(squared, t)
                nc.scalar.activation(junk[0:r, :], x[0:r, t, :], ACT.Square,
                                     accum_out=ss[0:r, t:t + 1]).then_inc(squared, 1)
            for t in range(TILES):
                r = rows(t)
                act.wait_ge(mean_done, t + 1)
                nc.scalar.activation(root[0:r, t:t + 1], mean[0:r, t:t + 1], ACT.Sqrt).then_inc(rooted, 1)
            act.wait_ge(vec_in, 16 * 8)
            nc.scalar.activation(k.a_row[:], k.a_row[:], ACT.Exp).then_inc(rooted, 1)

        @block.vector
        def _(dve):
            v = nc.vector
            own = Link(dve, dve_own)
            for t in range(TILES):
                r = rows(t)
                dve.wait_ge(squared, t + 1)
                v.tensor_scalar(mean[0:r, t:t + 1], ss[0:r, t:t + 1], 1.0 / D, EPS, ALU.mult,
                                ALU.add).then_inc(mean_done, 1)
            for t in range(TILES):
                r = rows(t)
                dve.wait_ge(rooted, t + 1)
                own(v.reciprocal(rstd[0:r, t:t + 1], root[0:r, t:t + 1]))
                v.tensor_scalar(x[0:r, t, :], x[0:r, t, :], rstd[0:r, t:t + 1], None, ALU.mult).then_inc(scaled, 1)
            dve.wait_ge(vec_turned, 1)
            own(v.tensor_copy(k.vcol[:, 0:32], k.ps[:, 6, 0:32]))
            own(v.tensor_copy(k.vcol[:, 32:152], k.ps[:, 7, 0:120]))
            dve.wait_ge(rooted, TILES + 1)
            own(v.tensor_scalar(k.a_row[:], k.a_row[:], -1.0, None, ALU.mult))
            for t in range(TILES):
                r = rows(t)
                dve.wait_ge(turned, t + 1)
                for f in range(KD):
                    b, o = 2 * (t % 2) + f // 4, (f % 4) * P
                    last = v.tensor_scalar(k.hT[:, f, P * t:P * t + r], k.ps[:, b, o:o + r],
                                           k.norm_mix_col[:, f:f + 1], None, ALU.mult)
                last.then_inc(evacuated, 1)

        @block.tensor
        def _(pe):
            pe.wait_ge(consts_done, 1)
            pe.wait_ge(vec_in, 16 * 8)
            nc.tensor.transpose(k.ps[:, 6, 0:32], vec_a[:], k.ident[0:32, 0:32])
            nc.tensor.transpose(k.ps[:, 7, 0:120], vec_b[:], k.ident[0:120, 0:120]).then_inc(vec_turned, 1)
            for t in range(TILES):
                r = rows(t)
                pe.wait_ge(scaled, t + 1)
                if t >= 2:
                    pe.wait_ge(evacuated, t - 1)
                for f in range(KD):
                    b, o = 2 * (t % 2) + f // 4, (f % 4) * P
                    last = nc.tensor.transpose(k.ps[:, b, o:o + r], x[0:r, t, f * P:f * P + P],
                                               k.ident[0:r, 0:r])
                last.then_inc(turned, 1)


def stage_conv(nc, k):
    with ExitStack() as ctx:
        sb = lambda n, s, d=F32: ctx.enter_context(nc.sbuf_tensor(n, s, d))
        sem = lambda n: ctx.enter_context(nc.semaphore(n))
        WB = 256
        NW = 3
        wbuf = sb("c_w", [P, NW, KD, WB])
        cin_p = sb("c_in_p", [P, 2, CONV_W - 1 + SEQ])
        cin_s = sb("c_in_s", [P, 2, NB, CONV_W - 1 + DS])
        acc = sb("c_acc", [P, 2, T])
        out = sb("c_out", [P, 2, T])
        state = sb("c_state", [NB * 3, CONV_DIM])
        tail = sb("c_tail", [P, 2, 27])
        tails = sb("c_tails", [27, CONV_DIM])
        w_in = [sem(f"c_w_in{i}") for i in range(NW)]
        state_in, projected, filled, convolved, activated = (
            sem("c_state_in"), sem("c_projected"), sem("c_filled"), sem("c_convolved"), sem("c_activated"))
        turned, dve_own, tailed, tail_turned, padded, written = (
            sem("c_turned"), sem("c_dve_own"), sem("c_tailed"), sem("c_tail_turned"), sem("c_padded"),
            sem("c_written"))
        block = ctx.enter_context(nc.Block())
        per = WB // P
        N = CT_TILES
        X_TILES = D_INNER // P
        B_TILES = X_TILES + GROUPS

        def bank(f):
            return 2 * (f % 2)

        @block.sync
        def _(sp):
            sp.dma_start(state[:], k.state_conv[0].rearrange("b w c -> (b w) c")).then_inc(state_in, 16)
            for i in range(N // per):
                if i >= NW:
                    sp.wait_ge(projected, per * (i - NW + 1))
                sp.dma_start(wbuf[:, i % NW], w_view(k.w_in, COL_XBC + WB * i, WB)).then_inc(w_in[i % NW], 16)
            sp.wait_ge(tail_turned, N)
            sp.dma_start(k.new_conv_prompt[0, 0], tails[0:3, :]).then_inc(written, 16)
            sp.dma_start(k.new_conv_sample[0].rearrange("b w c -> (b w) c"), tails[3:27, :]).then_inc(written, 16)
            sp.wait_ge(written, 32)

        @block.gpsimd
        def _(pool):
            nc.gpsimd.memset(k.dt[:], 0.0)
            nc.gpsimd.memset(cin_p[:, :, 0:3], 0.0).then_inc(padded, 1)

        @block.tensor
        def _(pe):
            def project(f):
                pe.wait_ge(w_in[(f // per) % NW], 16 * (f // per // NW + 1))
                if f == 0:
                    pe.wait_ge(state_in, 16)
                if f >= 2:
                    pe.wait_ge(filled, f - 1)
                b = bank(f)
                c = (f % per) * P
                for kk in range(KD):
                    nc.tensor.matmul(k.ps[:, b, :], wbuf[:, (f // per) % NW, kk, c:c + P], k.hT[:, kk, 0:SEQ],
                                     start=(kk == 0), stop=(kk == KD - 1))
                for kk in range(KD):
                    nc.tensor.matmul(k.ps[:, b + 1, 0:NS], wbuf[:, (f // per) % NW, kk, c:c + P],
                                     k.hT[:, kk, SEQ:T], start=(kk == 0), stop=(kk == KD - 1))
                nc.tensor.transpose(k.ps[:, b + 1, NS:NS + 24], state[:, f * P:f * P + P],
                                    k.ident[0:24, 0:24]).then_inc(projected, 1)

            def turn(f):
                if f >= 2:
                    pe.wait_ge(tail_turned, f - 1)
                pe.wait_ge(tailed, f + 1)
                b = 4 + bank(f)
                if f < B_TILES:
                    pe.wait_ge(activated, f + 1)
                    for t in range(TILES):
                        r = rows(t)
                        src = out[:, f % 2, P * t:P * t + r] if f < X_TILES else k.BT[:, f - X_TILES, P * t:P * t + r]
                        dst = k.ps[:, b, P * t:P * t + P] if t < 4 else k.ps[0:r, b + 1, 0:P]
                        nc.tensor.transpose(dst, src, k.ident[:])
                nc.tensor.transpose(k.ps[0:27, b + 1, P:2 * P], tail[:, f % 2, :], k.ident[:]).then_inc(turned, 1)

            for f in range(N + 1):
                if f < N:
                    project(f)
                if f:
                    turn(f - 1)

        @block.scalar
        def _(act):
            a = nc.scalar
            for f in range(N):
                act.wait_ge(projected, f + 1)
                if f == 0:
                    act.wait_ge(padded, 1)
                if f >= 2:
                    act.wait_ge(convolved, f - 1)
                    act.wait_ge(tailed, f - 1)
                b = bank(f)
                a.copy(cin_p[:, f % 2, 3:3 + SEQ], k.ps[:, b, :])
                a.copy(cin_s[:, f % 2, :, 3:3 + DS], k.ps[:, b + 1, 0:NS].rearrange("p (b t) -> p b t", b=NB))
                a.copy(cin_s[:, f % 2, :, 0:3],
                       k.ps[:, b + 1, NS:NS + 24].rearrange("p (b t) -> p b t", b=NB)).then_inc(filled, 1)
                act.wait_ge(convolved, f + 1)
                if f < X_TILES:
                    if f >= 2:
                        act.wait_ge(turned, f - 1)
                    dst = out[:, f % 2, :]
                elif f < B_TILES:
                    dst = k.BT[:, f - X_TILES, :]
                else:
                    dst = k.CT[:, f - B_TILES, :]
                a.activation(dst, acc[:, f % 2, :], ACT.Silu, bias=k.conv_b_col[:, f:f + 1]).then_inc(activated, 1)

        @block.vector
        def _(dve):
            v = nc.vector
            own = Link(dve, dve_own)

            def convolve(f):
                dve.wait_ge(filled, f + 1)
                if f >= 2:
                    dve.wait_ge(activated, f - 1)
                    dve.wait_ge(turned, f - 1)
                ap = acc[:, f % 2, 0:SEQ]
                as_ = acc[:, f % 2, SEQ:T].rearrange("p (b t) -> p b t", b=NB)
                for w in range(CONV_W):
                    wc = k.conv_w_col[:, w * CT_TILES + f:w * CT_TILES + f + 1]
                    ip, is_ = cin_p[:, f % 2, w:w + SEQ], cin_s[:, f % 2, :, w:w + DS]
                    if w == 0:
                        v.tensor_scalar(ap, ip, wc, None, ALU.mult)
                        own(v.tensor_scalar(as_, is_, wc, None, ALU.mult))
                    else:
                        v.scalar_tensor_tensor(out=ap, in0=ip, scalar=wc, in1=ap, op0=ALU.mult, op1=ALU.add)
                        last = v.scalar_tensor_tensor(out=as_, in0=is_, scalar=wc, in1=as_, op0=ALU.mult, op1=ALU.add)
                        if w < CONV_W - 1:
                            own(last)
                last.then_inc(convolved, 1)
                v.tensor_copy(tail[:, f % 2, 0:3], cin_p[:, f % 2, SEQ:SEQ + 3])
                v.tensor_copy(tail[:, f % 2, 3:27].rearrange("p (b t) -> p b t", b=NB),
                              cin_s[:, f % 2, :, DS:DS + 3]).then_inc(tailed, 1)

            def gather(f):
                dve.wait_ge(turned, f + 1)
                b = 4 + bank(f)
                if f < B_TILES:
                    dst = k.xnat if f < X_TILES else k.Bnat
                    c = (f if f < X_TILES else f - X_TILES) * P
                    v.tensor_copy(dst[:, 0:4, c:c + P], k.ps[:, b, :].rearrange("p (t n) -> p t n", t=4))
                    v.tensor_copy(dst[0:NS, 4, c:c + P], k.ps[0:NS, b + 1, 0:P])
                v.tensor_copy(tails[:, f * P:f * P + P], k.ps[0:27, b + 1, P:2 * P]).then_inc(tail_turned, 1)

            for f in range(N + 1):
                if f < N:
                    convolve(f)
                if f:
                    gather(f - 1)


def natural_projection(nc, k, name, blocks):
    with ExitStack() as ctx:
        sem = lambda n: ctx.enter_context(nc.semaphore(f"{name}_{n}"))
        NW, NBANK = 2, 4
        wbuf = ctx.enter_context(nc.sbuf_tensor(f"{name}_w", [P, NW, KD, 512], F32))
        w_in = [sem(f"w_in{i}") for i in range(NW)]
        projected, stored = sem("projected"), sem("stored")
        block = ctx.enter_context(nc.Block())

        @block.sync
        def _(sp):
            for i, (col, width, _, _) in enumerate(blocks):
                if i >= NW:
                    sp.wait_ge(projected, TILES * (i - NW + 1))
                sp.dma_start(wbuf[:, i % NW, :, 0:width], w_view(k.w_in, col, width)).then_inc(w_in[i % NW], 16)

        @block.tensor
        def _(pe):
            for i, (_, width, _, _) in enumerate(blocks):
                pe.wait_ge(w_in[i % NW], 16 * (i // NW + 1))
                for t in range(TILES):
                    n = TILES * i + t
                    if n >= NBANK:
                        pe.wait_ge(stored, n - NBANK + 1)
                    r = rows(t)
                    for kk in range(KD):
                        last = nc.tensor.matmul(k.ps[0:r, n % NBANK, 0:width], k.hT[:, kk, P * t:P * t + r],
                                                wbuf[:, i % NW, kk, 0:width], start=(kk == 0), stop=(kk == KD - 1))
                    last.then_inc(projected, 1)

        @block.scalar
        def _(act):
            for i, (_, width, dst, func) in enumerate(blocks):
                for t in range(TILES):
                    n = TILES * i + t
                    act.wait_ge(projected, n + 1)
                    nc.scalar.activation(dst(t), k.ps[0:rows(t), n % NBANK, 0:width], func).then_inc(stored, 1)


def stage_decays(nc, k):
    with ExitStack() as ctx:
        sb = lambda n, s, d=F32: ctx.enter_context(nc.sbuf_tensor(n, s, d))
        sem = lambda n: ctx.enter_context(nc.semaphore(n))
        shape = [P, TILES, HEADS]
        absx, u, lnw, zero, den = (sb(f"d_{n}", shape) for n in ("absx", "u", "lnw", "zero", "den"))
        abs_done, exp_done, plus_one, ln_done, step_done, summed, negated, exps, own_s = (
            sem(f"d_{n}") for n in ("abs", "exp", "plus_one", "ln", "step", "summed", "negated", "exps", "own"))
        block = ctx.enter_context(nc.Block())

        def each(row):
            return row[:].rearrange("p (a h) -> p a h", a=1).broadcast_to(shape)

        @block.vector
        def _(dve):
            v = nc.vector
            own = Link(dve, own_s)
            own(v.tensor_tensor(k.dt[:], k.dt[:], each(k.dt_bias_row), ALU.add))
            v.scalar_tensor_tensor(out=absx[:], in0=k.dt[:], scalar=-1.0, in1=k.dt[:], op0=ALU.mult,
                                   op1=ALU.max).then_inc(abs_done, 1)
            own(v.tensor_scalar(k.dt[:], k.dt[:], 0.0, None, ALU.max))
            dve.wait_ge(exp_done, 1)
            v.tensor_scalar(den[:], u[:], 1.0, None, ALU.add).then_inc(plus_one, 1)
            dve.wait_ge(ln_done, 1)
            own(v.tensor_scalar(den[:], den[:], -1.0, None, ALU.add))
            own(v.tensor_scalar(zero[:], den[:], 0.0, None, ALU.is_equal))
            own(v.tensor_tensor(den[:], den[:], zero[:], ALU.add))
            own(v.tensor_tensor(lnw[:], lnw[:], zero[:], ALU.add))
            own(v.reciprocal(den[:], den[:]))
            own(v.tensor_tensor(lnw[:], lnw[:], den[:], ALU.mult))
            own(v.tensor_tensor(lnw[:], lnw[:], u[:], ALU.mult))
            own(v.tensor_tensor(k.dt[:], k.dt[:], lnw[:], ALU.add))
            v.tensor_tensor(k.da[:], k.dt[:], each(k.a_row), ALU.mult).then_inc(step_done, 1)
            dve.wait_ge(summed, 1)
            for lo, hi, r in ((0, 4, P), (4, 5, NS)):
                a = k.ps[0:r, 0, lo * HEADS:hi * HEADS].rearrange("p (c h) -> p c h", h=HEADS)
                t = k.ps[0:r, 1, lo * HEADS:hi * HEADS].rearrange("p (c h) -> p c h", h=HEADS)
                own(v.tensor_scalar(k.nacum[0:r, lo:hi, :], a, -1.0, None, ALU.mult))
                v.tensor_tensor(k.to_end[0:r, lo:hi, :], t, k.nacum[0:r, lo:hi, :], ALU.add).then_inc(negated, 1)

        @block.tensor
        def _(pe):
            pe.wait_ge(step_done, 1)
            mm = nc.tensor.matmul
            for c in range(TILES):
                r = rows(c)
                cum, tot = (k.cum, k.ones) if c < 4 else (k.cum_s, k.same)
                mm(k.ps[0:r, 0, c * HEADS:c * HEADS + HEADS], cum[:], k.da[0:r, c, :], start=True, stop=True)
                mm(k.ps[0:r, 1, c * HEADS:c * HEADS + HEADS], tot[:], k.da[0:r, c, :], start=True, stop=True)
            for hh in range(HEADS):
                f, p0 = hh // 2, HP * (hh % 2)
                last = mm(k.ps[p0:p0 + HP, 2, f * NB:f * NB + NB], k.da[0:NS, 4, hh:hh + 1].broadcast_to([NS, HP]),
                          k.same[:, 0:NS:DS], start=True, stop=True)
            last.then_inc(summed, 1)

        @block.scalar
        def _(act):
            a = nc.scalar
            act.wait_ge(abs_done, 1)
            a.activation(u[:], absx[:], ACT.Exp, scale=-1.0).then_inc(exp_done, 1)
            act.wait_ge(plus_one, 1)
            a.activation(lnw[:], den[:], ACT.Ln).then_inc(ln_done, 1)
            act.wait_ge(summed, 1)
            act.wait_ge(negated, 2)
            for lo, hi, r in ((0, 4, P), (4, 5, NS)):
                acum = k.ps[0:r, 0, lo * HEADS:hi * HEADS].rearrange("p (c h) -> p c h", h=HEADS)
                a.activation(k.eacum[0:r, lo:hi, :], acum, ACT.Exp)
                a.activation(k.to_end[0:r, lo:hi, :], k.to_end[0:r, lo:hi, :], ACT.Exp)
            a.activation(k.cdec[:, 0:4, :], k.ps[:, 1, 0:4 * HEADS].rearrange("p (c h) -> p c h", h=HEADS), ACT.Exp)
            a.activation(k.tail_dec[:], k.ps[:, 2, 0:16 * NB].rearrange("p (f b) -> p f b", b=NB), ACT.Exp)


def by_head(col, r, n=8, width=HP):
    return col.rearrange("p (h a) -> p h a", a=1).broadcast_to([r, n, width])


def stage_sample_state(nc, k):
    with ExitStack() as ctx:
        sb = lambda n, s, d=F32: ctx.enter_context(nc.sbuf_tensor(n, s, d))
        sem = lambda n: ctx.enter_context(nc.semaphore("ss_" + n))
        NH0 = 3
        xde = sb("ss_xde", [NS, D_INNER])
        bsel = sb("ss_bsel", [NS, 2, GROUPS * STATE])
        h0 = sb("ss_h0", [P, NH0, 16, STATE])
        h0t = sb("ss_h0t", [P, 2, 4, P])
        h0_in = [sem(f"h0_in{i}") for i in range(NH0)]
        h0_out = [sem(f"h0_out{i}") for i in range(NH0)]
        xdt_done, xde_done, selected, turned, copied, read_out, contributed, updated = (
            sem(n) for n in ("xdt_done", "xde_done", "selected", "turned", "copied", "read_out", "contributed",
                             "updated"))
        block = ctx.enter_context(nc.Block())
        QUADS = 4 * NB

        def view(dram, b):
            return dram[0, b].rearrange("h p n -> (h p) n").rearrange("(f q) n -> q f n", q=P)

        @block.sync
        def _(sp):
            for b in range(NB):
                if b >= NH0:
                    sp.wait_ge(h0_out[b % NH0], 16 * (b // NH0))
                sp.dma_start(h0[:, b % NH0], view(k.state_ssm, b)).then_inc(h0_in[b % NH0], 16)
                if b >= 1:
                    sp.wait_ge(updated, 4 * b)
                    sp.dma_start(view(k.new_ssm_sample, b - 1), h0[:, (b - 1) % NH0]).then_inc(h0_out[(b - 1) % NH0], 16)
            sp.wait_ge(updated, 4 * NB)
            sp.dma_start(view(k.new_ssm_sample, NB - 1), h0[:, (NB - 1) % NH0]).then_inc(h0_out[(NB - 1) % NH0], 16)
            for i in range(NH0):
                sp.wait_ge(h0_out[i], 16 * len(range(i, NB, NH0)))

        @block.gpsimd
        def _(pool):
            g = nc.gpsimd
            x3 = k.xnat[0:NS, 4, :].rearrange("p (h q) -> p h q", q=HP)
            o3 = xde[:].rearrange("p (h q) -> p h q", q=HP)
            g.tensor_tensor(o3, x3, by_head(k.dt[0:NS, 4, :], NS, HEADS), ALU.mult).then_inc(xdt_done, 1)
            pool.wait_ge(xdt_done, 1)
            g.tensor_tensor(o3, o3, by_head(k.to_end[0:NS, 4, :], NS, HEADS), ALU.mult).then_inc(xde_done, 1)
            for b in range(NB):
                if b >= 2:
                    pool.wait_ge(contributed, 4 * (b - 1))
                g.tensor_scalar(bsel[:, b % 2, :], k.Bnat[0:NS, 4, :], k.same[:, DS * b:DS * b + 1], 1.0,
                                ALU.mult, ALU.mult).then_inc(selected, 1)

        @block.tensor
        def _(pe):
            mm = nc.tensor.matmul

            def turn(q):
                b, j = q // 4, q % 4
                if j == 0:
                    pe.wait_ge(h0_in[b % NH0], 16 * (b // NH0 + 1))
                if q >= 2:
                    pe.wait_ge(copied, q - 1)
                for i in range(4):
                    last = nc.tensor.transpose(k.ps[:, q % 2, i * P:i * P + P], h0[:, b % NH0, 4 * j + i, :], k.ident[:])
                last.then_inc(turned, 1)

            def use(q):
                b, j = q // 4, q % 4
                if q == 0:
                    pe.wait_ge(xde_done, 1)
                if j == 0:
                    pe.wait_ge(selected, b + 1)
                if q >= 2:
                    pe.wait_ge(updated, q - 1)
                for i in range(4):
                    f = 4 * j + i
                    last = mm(k.ps[:, 2 + q % 2, i * P:i * P + P], xde[:, f * P:f * P + P],
                              bsel[:, b % 2, j * STATE:j * STATE + STATE], start=True, stop=True)
                last.then_inc(contributed, 1)
                pe.wait_ge(copied, q + 1)
                for i in range(4):
                    f = 4 * j + i
                    c = f * NS + b * DS
                    last = mm(k.ps[:, 4 + c // 512, c % 512:c % 512 + DS], h0t[:, q % 2, i, :],
                              k.CT[:, j, SEQ + DS * b:SEQ + DS * b + DS], start=True, stop=True)
                last.then_inc(read_out, 1)

            for q in range(QUADS + 1):
                if q < QUADS:
                    turn(q)
                if q:
                    use(q - 1)

        @block.scalar
        def _(act):
            for q in range(QUADS):
                act.wait_ge(turned, q + 1)
                if q >= 2:
                    act.wait_ge(read_out, q - 1)
                nc.scalar.copy(h0t[:, q % 2], k.ps[:, q % 2, :].rearrange("p (i n) -> p i n", i=4)).then_inc(copied, 1)
            act.wait_ge(read_out, QUADS)
            for i in range(2):
                last = nc.scalar.copy(k.yt[:, 8 * i:8 * i + 8, :], k.ps[:, 4 + i, :].rearrange("p (f n) -> p f n", f=8))
            last.then_inc(copied, 1)

        @block.vector
        def _(dve):
            for q in range(QUADS):
                b, j = q // 4, q % 4
                dve.wait_ge(contributed, q + 1)
                dve.wait_ge(turned, q + 1)
                for i in range(4):
                    f = 4 * j + i
                    hh = h0[:, b % NH0, f, :]
                    last = nc.vector.scalar_tensor_tensor(out=hh, in0=hh, scalar=k.tail_dec[:, f, b:b + 1],
                                                          in1=k.ps[:, 2 + q % 2, i * P:i * P + P], op0=ALU.mult,
                                                          op1=ALU.add)
                last.then_inc(updated, 1)


def stage_ssd(nc, k):
    with ExitStack() as ctx:
        sb = lambda n, s, d=F32: ctx.enter_context(nc.sbuf_tensor(n, s, d))
        sem = lambda n: ctx.enter_context(nc.semaphore("s_" + n))
        xdt, xde, dx, y = (sb("s_" + n, [P, 2, 512]) for n in ("xdt", "xde", "dx", "y"))
        MT = sb("s_MT", [P, 4, 4, P])
        h = sb("s_h", [P, D_INNER])
        hout = sb("s_hout", [P, 16, STATE])
        junk = sb("s_junk", [P, 512])
        (scored, decayed, exped, weighted, diag, offs, states, xdt_done, xde_done, dx_done, y_done, updated, own_s,
         h_turned, h_copied, h_stored, squared) = (
            sem(n) for n in ("scored", "decayed", "exped", "weighted", "diag", "offs", "states", "xdt_done",
                             "xde_done", "dx_done", "y_done", "updated", "own", "h_turned", "h_copied", "h_stored",
                             "squared"))
        block = ctx.enter_context(nc.Block())
        U = TILES * GROUPS
        HG = HEADS // GROUPS

        @block.gpsimd
        def _(pool):
            g = nc.gpsimd
            for u in range(U):
                c, gr = u // GROUPS, u % GROUPS
                r = rows(c)
                x3 = k.xnat[0:r, c, gr * 512:gr * 512 + 512].rearrange("p (h q) -> p h q", q=HP)
                hs = slice(gr * HG, gr * HG + HG)
                v3 = lambda a: a[0:r, u % 2, :].rearrange("p (h q) -> p h q", q=HP)
                if u >= 2:
                    pool.wait_ge(diag, u - 1)
                    pool.wait_ge(states, min(u - 1, 16))
                    pool.wait_ge(y_done, u - 1)
                g.tensor_tensor(v3(xdt), x3, by_head(k.dt[0:r, c, hs], r), ALU.mult).then_inc(xdt_done, 1)
                g.tensor_tensor(v3(dx), x3, by_head(k.dskip_row[0:r, hs], r), ALU.mult).then_inc(dx_done, 1)
                if c < 4:
                    pool.wait_ge(xdt_done, u + 1)
                    g.tensor_tensor(v3(xde), v3(xdt), by_head(k.to_end[0:r, c, hs], r), ALU.mult).then_inc(xde_done, 1)

        @block.tensor
        def _(pe):
            mm = nc.tensor.matmul

            def scores(u):
                c, gr = u // GROUPS, u % GROUPS
                r = rows(c)
                tok = slice(P * c, P * c + r)
                if u >= 2:
                    pe.wait_ge(weighted, 2 * (u - 1))
                mm(k.ps[0:r, 7 * (u % 2), 0:r], k.BT[:, gr, tok], k.CT[:, gr, tok], start=True,
                   stop=True).then_inc(scored, 1)
                later, cum = (k.later, k.cum) if c < 4 else (k.later_s, k.cum_s)
                for i in range(2):
                    q = 2 * u + i
                    if q >= 2:
                        pe.wait_ge(exped, q - 1)
                    bank = k.ps[0:r, 1 + q % 2, 0:4 * r].rearrange("p (h l) -> p h l", h=4)
                    mm(bank, k.identb[0:r, 0:r], later[0:r, 0:r].rearrange("p (a l) -> p a l", a=1).broadcast_to([r, 4, r]),
                       start=True, stop=False, skip_group_check=True)
                    for j in range(4):
                        hh = gr * HG + 4 * i + j
                        last = mm(bank[:, j, :], k.da[0:r, c, hh:hh + 1].broadcast_to([r, r]), cum[0:r, 0:r],
                                  start=False, stop=(j == 3), skip_group_check=True)
                    last.then_inc(decayed, 1)

            def within(u):
                c = u // GROUPS
                r = rows(c)
                pe.wait_ge(weighted, 2 * u + 2)
                pe.wait_ge(xdt_done, u + 1)
                if u:
                    pe.wait_ge(y_done, u)
                for j in range(HG):
                    last = mm(k.ps[0:r, 3, j * HP:j * HP + HP], MT[0:r, (2 * u + j // 4) % 4, j % 4, 0:r],
                              xdt[0:r, u % 2, j * HP:j * HP + HP], start=True, stop=True)
                last.then_inc(diag, 1)

            def from_state(u):
                c, gr = u // GROUPS, u % GROUPS
                cols = slice(gr * 512, gr * 512 + 512)
                if 0 < c < 4:
                    pe.wait_ge(updated, u - GROUPS + 1)
                    mm(k.ps[:, 4, :], k.CT[:, gr, P * c:P * c + P], h[:, cols], start=True, stop=True).then_inc(offs, 1)
                if c == 4:
                    for i in range(4):
                        last = nc.tensor.transpose(k.ps[0:NS, 4, i * P:i * P + P], k.yt[:, 4 * gr + i, :], k.ident[:])
                    last.then_inc(offs, 1)
                if c < 4:
                    pe.wait_ge(xde_done, u + 1)
                    if u:
                        pe.wait_ge(updated, u)
                    mm(k.ps[:, 5, :], k.Bnat[:, c, gr * STATE:gr * STATE + STATE], xde[:, u % 2, :], start=True,
                       stop=True).then_inc(states, 1)

            for u in range(U + 1):
                if u < U:
                    scores(u)
                if u:
                    within(u - 1)
                    from_state(u - 1)
            pe.wait_ge(updated, 16)
            for q in range(4):
                if q >= 2:
                    pe.wait_ge(h_copied, q - 1)
                for i in range(4):
                    f = 4 * q + i
                    last = nc.tensor.transpose(k.ps[:, 5 + q % 2, i * P:i * P + P], h[:, f * P:f * P + P], k.ident[:])
                last.then_inc(h_turned, 1)

        def sum_squares(act, a, u):
            c, gr = u // GROUPS, u % GROUPS
            r = rows(c)
            act.wait_ge(y_done, u + 1)
            if u:
                act.wait_ge(squared, u)
            a.activation(junk[0:r, :], k.znat[0:r, c, gr * 512:gr * 512 + 512], ACT.Square,
                         accum_out=k.ysq[0:r, c, gr:gr + 1]).then_inc(squared, 1)

        @block.scalar
        def _(act):
            a = nc.scalar
            for u in range(U):
                c, gr = u // GROUPS, u % GROUPS
                r = rows(c)
                for i in range(2):
                    q = 2 * u + i
                    act.wait_ge(decayed, q + 1)
                    if q >= 4:
                        act.wait_ge(diag, (q - 4) // 2 + 1)
                    for j in range(4):
                        hh = gr * HG + 4 * i + j
                        last = a.activation(MT[0:r, q % 4, j, 0:r], k.ps[0:r, 1 + q % 2, j * r:j * r + r], ACT.Exp,
                                            bias=k.nacum[0:r, c, hh:hh + 1])
                    last.then_inc(exped, 1)
                if u:
                    sum_squares(act, a, u - 1)
            sum_squares(act, a, U - 1)
            for q in range(4):
                act.wait_ge(h_turned, q + 1)
                a.copy(hout[:, 4 * q:4 * q + 4, :], k.ps[:, 5 + q % 2, :].rearrange("p (i n) -> p i n", i=4)).then_inc(h_copied, 1)

        @block.vector
        def _(dve):
            v = nc.vector
            own = Link(dve, own_s)

            def weigh(u):
                r = rows(u // GROUPS)
                dve.wait_ge(scored, u + 1)
                s = k.ps[0:r, 7 * (u % 2), 0:r].rearrange("p (a l) -> p a l", a=1).broadcast_to([r, 4, r])
                for i in range(2):
                    q = 2 * u + i
                    dve.wait_ge(exped, q + 1)
                    m = MT[0:r, q % 4, :, 0:r]
                    v.tensor_tensor(m, m, s, ALU.mult).then_inc(weighted, 1)

            def finish(u):
                c, gr = u // GROUPS, u % GROUPS
                r = rows(c)
                hs = slice(gr * HG, gr * HG + HG)
                yy = y[0:r, u % 2, :]
                dve.wait_ge(diag, u + 1)
                dve.wait_ge(dx_done, u + 1)
                own(v.tensor_tensor(yy, k.ps[0:r, 3, :], dx[0:r, u % 2, :], ALU.add))
                if c > 0:
                    dve.wait_ge(offs, u - GROUPS + 1)
                    d3 = dx[0:r, u % 2, :]
                    own(v.tensor_tensor(d3.rearrange("p (h q) -> p h q", q=HP),
                                        k.ps[0:r, 4, :].rearrange("p (h q) -> p h q", q=HP),
                                        by_head(k.eacum[0:r, c, hs], r), ALU.mult))
                    own(v.tensor_tensor(yy, yy, d3, ALU.add))
                z = k.znat[0:r, c, gr * 512:gr * 512 + 512]
                v.tensor_tensor(z, z, yy, ALU.mult).then_inc(y_done, 1)
                if c < 4:
                    dve.wait_ge(states, u + 1)
                    hh = h[:, gr * 512:gr * 512 + 512]
                    if c == 0:
                        v.tensor_copy(hh, k.ps[:, 5, :]).then_inc(updated, 1)
                    else:
                        dve.wait_ge(offs, u - GROUPS + 1)
                        h3 = hh.rearrange("p (h q) -> p h q", q=HP)
                        own(v.tensor_tensor(h3, h3, by_head(k.cdec[:, c, hs], P), ALU.mult))
                        v.tensor_tensor(hh, hh, k.ps[:, 5, :], ALU.add).then_inc(updated, 1)

            for u in range(U + 1):
                if u < U:
                    weigh(u)
                if u:
                    finish(u - 1)

        @block.sync
        def _(sp):
            sp.wait_ge(h_copied, 4)
            sp.dma_start(k.new_ssm_prompt[0, 0].rearrange("h p n -> (h p) n").rearrange("(f q) n -> q f n", q=P),
                         hout[:]).then_inc(h_stored, 16)
            sp.wait_ge(h_stored, 16)


def stage_gate(nc, k):
    with ExitStack() as ctx:
        sb = lambda n, s, d=F32: ctx.enter_context(nc.sbuf_tensor(n, s, d))
        sem = lambda n: ctx.enter_context(nc.semaphore("g_" + n))
        ms = sb("g_ms", [P, TILES])
        rstd = sb("g_rstd", [P, TILES])
        mean_done, rooted, scaled, turned, stored, own_s = (
            sem(n) for n in ("mean", "rooted", "scaled", "turned", "stored", "own"))
        block = ctx.enter_context(nc.Block())

        def store(eng, n, done):
            t, q = n // 4, n % 4
            r = rows(t)
            for i in range(4):
                f = 4 * q + i
                src = k.ps[:, n % 4, i * P:i * P + r]
                col = k.ssm_norm_col[:, f:f + 1]
                if eng is nc.scalar:
                    last = eng.activation(yT(k, t)[:, f, :], src, ACT.Copy, scale=col)
                else:
                    last = eng.tensor_scalar(yT(k, t)[:, f, :], src, col, None, ALU.mult)
            last.then_inc(done, 1)

        @block.vector
        def _(dve):
            v = nc.vector
            own = Link(dve, own_s)
            for c, r in ((slice(0, 4), P), (slice(4, 5), NS)):
                own(v.tensor_reduce(ms[0:r, c], k.ysq[0:r, c, :], AX.X, ALU.add))
                v.tensor_scalar(ms[0:r, c], ms[0:r, c], 1.0 / D_INNER, EPS, ALU.mult, ALU.add).then_inc(mean_done, 1)
            dve.wait_ge(rooted, 2)
            own(v.reciprocal(rstd[:, 0:4], rstd[:, 0:4]))
            own(v.reciprocal(rstd[0:NS, 4:5], rstd[0:NS, 4:5]))
            for t in range(TILES):
                r = rows(t)
                v.tensor_scalar(k.znat[0:r, t, :], k.znat[0:r, t, :], rstd[0:r, t:t + 1], None,
                                ALU.mult).then_inc(scaled, 1)
                for q in range(4):
                    n = 4 * t + q
                    if q % 2 == 0:
                        dve.wait_ge(turned, n + 1)
                        store(v, n, stored)

        stored_act = ctx.enter_context(nc.semaphore("g_stored_act"))

        @block.scalar
        def _(act):
            act.wait_ge(mean_done, 2)
            nc.scalar.activation(rstd[:, 0:4], ms[:, 0:4], ACT.Sqrt).then_inc(rooted, 1)
            nc.scalar.activation(rstd[0:NS, 4:5], ms[0:NS, 4:5], ACT.Sqrt).then_inc(rooted, 1)
            for n in range(1, 4 * TILES, 2):
                act.wait_ge(turned, n + 1)
                store(nc.scalar, n, stored_act)

        @block.tensor
        def _(pe):
            for n in range(4 * TILES):
                t, q = n // 4, n % 4
                r = rows(t)
                pe.wait_ge(scaled, t + 1)
                if n >= 4:
                    pe.wait_ge(stored if n % 2 == 0 else stored_act, (n - 4) // 2 + 1)
                for i in range(4):
                    f = 4 * q + i
                    last = nc.tensor.transpose(k.ps[:, n % 4, i * P:i * P + r], k.znat[0:r, t, f * P:f * P + P],
                                               k.ident[0:r, 0:r])
                last.then_inc(turned, 1)


def stage_branch(nc, k, name, gate_col, w, depth, load_w, src_p, src_s, accumulate):
    with ExitStack() as ctx:
        sb = lambda n, s, d=F32: ctx.enter_context(nc.sbuf_tensor(f"{name}_{n}", s, d))
        sem = lambda n: ctx.enter_context(nc.semaphore(f"{name}_{n}"))
        NW, WB = 2, 256
        wg = sb("wg", [P, NW, KD, WB])
        wp = sb("wp", [P, NW, depth, WB])
        sig = sb("sig", [P, 2, T])
        prod = sb("prod", [P, 2, T])
        w_in = [sem(f"w_in{i}") for i in range(NW)]
        gated, projected, sigmoids, merged, own_s = (
            sem(n) for n in ("gated", "projected", "sigmoids", "merged", "own"))
        block = ctx.enter_context(nc.Block())
        per = WB // P
        n_loads = 1 + len(load_w(wp[:, 0], w, 0, WB))

        @block.sync
        def _(sp):
            for i in range(KD // per):
                if i >= NW:
                    sp.wait_ge(projected, per * (i - NW + 1))
                s = i % NW
                sp.dma_start(wg[:, s], w_view(k.w_in, gate_col + WB * i, WB)).then_inc(w_in[s], 16)
                for dst, src in load_w(wp[:, s], w, WB * i, WB):
                    sp.dma_start(dst, src).then_inc(w_in[s], 16)

        @block.tensor
        def _(pe):
            mm = nc.tensor.matmul
            for m in range(KD):
                s, c, b = (m // per) % NW, (m % per) * P, 3 * (m % 2)
                pe.wait_ge(w_in[s], 16 * n_loads * (m // per // NW + 1))
                if m >= 2:
                    pe.wait_ge(merged, m - 1)
                for f in range(KD):
                    mm(k.ps[:, b, :], wg[:, s, f, c:c + P], k.hT[:, f, 0:SEQ], start=(f == 0), stop=(f == KD - 1))
                for f in range(KD):
                    last = mm(k.ps[:, b + 2, 0:NS], wg[:, s, f, c:c + P], k.hT[:, f, SEQ:T], start=(f == 0),
                              stop=(f == KD - 1))
                for f in range(depth):
                    mm(k.ps[:, b + 1, :], wp[:, s, f, c:c + P], src_p(f), start=(f == 0), stop=(f == depth - 1))
                for f in range(depth):
                    last = mm(k.ps[:, b + 2, NS:2 * NS], wp[:, s, f, c:c + P], src_s(f), start=(f == 0),
                              stop=(f == depth - 1))
                last.then_inc(projected, 1)

        @block.scalar
        def _(act):
            for m in range(KD):
                b = 3 * (m % 2)
                act.wait_ge(projected, m + 1)
                if m >= 2:
                    act.wait_ge(merged, m - 1)
                nc.scalar.activation(sig[:, m % 2, 0:SEQ], k.ps[:, b, :], ACT.Sigmoid)
                nc.scalar.activation(sig[:, m % 2, SEQ:T], k.ps[:, b + 2, 0:NS], ACT.Sigmoid).then_inc(sigmoids, 1)

        @block.vector
        def _(dve):
            v = nc.vector
            own = Link(dve, own_s)
            for m in range(KD):
                b = 3 * (m % 2)
                dve.wait_ge(sigmoids, m + 1)
                dst = prod[:, m % 2, :] if accumulate else k.mT[:, m, :]
                v.tensor_tensor(dst[:, 0:SEQ], sig[:, m % 2, 0:SEQ], k.ps[:, b + 1, :], ALU.mult)
                last = v.tensor_tensor(dst[:, SEQ:T], sig[:, m % 2, SEQ:T], k.ps[:, b + 2, NS:2 * NS], ALU.mult)
                if accumulate:
                    own(last)
                    last = v.tensor_tensor(k.mT[:, m, :], k.mT[:, m, :], dst, ALU.add)
                last.then_inc(merged, 1)


def load_rows(dst, w, c0, n):
    return [(dst, w_view(w, c0, n))]


def load_head_rows(dst, w, c0, n):
    return [(dst[HD * g:HD * g + HD], w[:, c0:c0 + n].rearrange("(g j d) n -> g d j n", g=KVH, d=HD)[g])
            for g in range(KVH)]


def stage_qk(nc, k):
    with ExitStack() as ctx:
        sem = lambda n: ctx.enter_context(nc.semaphore("q_" + n))
        NW = 4
        wbuf = ctx.enter_context(nc.sbuf_tensor("q_w", [P, NW, KD, KVH, HD], F32))
        w_in = [sem(f"w_in{i}") for i in range(NW)]
        projected, stored = sem("projected"), sem("stored")
        block = ctx.enter_context(nc.Block())

        def q_cols(j):
            return lambda g: COL_Q + (g * HPK + j) * HD

        def k_cols(branch):
            return lambda g: COL_KV + branch * KVW + g * 2 * HD
        jobs = [(q_cols(j), k.qT[:, j, :], SCALE) for j in range(HPK)]
        jobs += [(k_cols(1), k.ksT[:], 1.0), (k_cols(2), k.kwT[:], 1.0)]

        @block.sync
        def _(sp):
            for i, (cols, _, _) in enumerate(jobs):
                if i >= NW:
                    sp.wait_ge(projected, i - NW + 1)
                for g in range(KVH):
                    sp.dma_start(wbuf[:, i % NW, :, g, :], w_view(k.w_in, cols(g), HD)).then_inc(w_in[i % NW], 16)

        @block.tensor
        def _(pe):
            for i in range(len(jobs)):
                s, b = i % NW, 2 * (i % 4)
                pe.wait_ge(w_in[s], 32 * (i // NW + 1))
                if i >= 4:
                    pe.wait_ge(stored, i - 3)
                for bank, cols in ((k.ps[:, b, :], slice(0, SEQ)), (k.ps[:, b + 1, 0:NS], slice(SEQ, T))):
                    for f in range(KD):
                        last = nc.tensor.matmul(bank, wbuf[:, s, f].rearrange("p g d -> p (g d)"), k.hT[:, f, cols],
                                                start=(f == 0), stop=(f == KD - 1))
                last.then_inc(projected, 1)

        @block.scalar
        def _(act):
            for i, (_, dst, scale) in enumerate(jobs):
                b = 2 * (i % 4)
                act.wait_ge(projected, i + 1)
                nc.scalar.activation(dst[:, 0:SEQ], k.ps[:, b, :], ACT.Copy, scale=scale)
                nc.scalar.activation(dst[:, SEQ:T], k.ps[:, b + 1, 0:NS], ACT.Copy, scale=scale).then_inc(stored, 1)


def v_of(kv, branch, g):
    c = branch * KVW + g * 2 * HD + HD
    return kv[..., c:c + HD]


def stage_cmp_prompt(nc, k):
    with ExitStack() as ctx:
        sb = lambda n, s, d=F32: ctx.enter_context(nc.sbuf_tensor("cp_" + n, s, d))
        sem = lambda n: ctx.enter_context(nc.semaphore("cp_" + n))
        N = NCMP_P
        ind = sb("ind", [P, 4, AH, N])
        seen = sb("seen", [P, 4, N])
        unseen = sb("unseen", [P, 4, N])
        own_head = sb("own_head", [P, HPK, KVH])
        kcT = sb("kcT", [P, N])
        vrep = sb("vrep", [P, P])
        vblk = sb("vblk", [P, HPK, KVH, HD])
        s = sb("s", [P, 4, AH, N])
        m = sb("m", [P, 4, AH])
        den = sb("den", [P, 4, AH])
        pT = sb("pT", [P, 4, P])
        consts, means, mean_copied, scored, weighed, turned, turned_copied, out_done, stored, own_s, pool_s, exped, shifted = (
            sem(n) for n in ("consts", "means", "mean_copied", "scored", "weighed", "turned", "turned_copied",
                             "out_done", "stored", "own", "pool", "exped", "shifted"))
        written = sem("written")
        block = ctx.enter_context(nc.Block())

        @block.sync
        def _(sp):
            for br, (p_out, s_out) in enumerate(((k.new_cmp_kv_prompt, k.new_cmp_kv_sample),
                                                 (k.new_sel_kv_prompt, k.new_sel_kv_sample),
                                                 (k.new_win_kv_prompt, None))):
                cols = slice(br * KVW, br * KVW + KVW)
                sp.dma_start(p_out[0, 0].rearrange("(t p) g c d -> p t (g c d)", p=P), k.kv[:, 0:4, cols]).then_inc(written, 16)
                if s_out is not None:
                    sp.dma_start(s_out[0].rearrange("b t g c d -> (b t) (g c d)"), k.kv[0:NS, 4, cols]).then_inc(written, 16)
            win = k.new_win_kv_sample[0].rearrange("b t g c d -> b t (g c d)")
            old = k.cache_win_kv[0].rearrange("b t g c d -> b t (g c d)")
            for b in range(NB):
                sp.dma_start(win[b, WINDOW - DS:WINDOW], k.kv[DS * b:DS * b + DS, 4, 2 * KVW:3 * KVW]).then_inc(written, 16)
            sp.dma_start(win[:, 0:WINDOW - DS], old[:, DS:WINDOW]).then_inc(written, 16)
            sp.dma_start(k.gates_dram, k.gates[0:NS, 4, :]).then_inc(written, 16)
            sp.wait_ge(written, 16 * (5 + NB + 2))

        @block.gpsimd
        def _(pool):
            g = nc.gpsimd
            own = Link(pool, pool_s)
            own(g.memset(ind[:], 1.0 / CMP))
            pat = [[P, 4], [0, AH], [-CMP, N]]
            own(g.affine_select(out=ind[:], in_=ind[:], compare_op=ALU.is_ge, fill=0.0, base=0, pattern=pat,
                                channel_multiplier=1))
            own(g.affine_select(out=ind[:], in_=ind[:], compare_op=ALU.is_ge, fill=0.0, base=CMP - 1,
                                pattern=[[-P, 4], [0, AH], [CMP, N]], channel_multiplier=-1))
            own(g.memset(seen[:], 1.0))
            own(g.affine_select(out=seen[:], in_=seen[:], compare_op=ALU.is_ge, fill=0.0, base=-(CMP - 1),
                                pattern=[[P, 4], [-CMP, N]], channel_multiplier=1))
            own(g.tensor_scalar(unseen[:], seen[:], -NEG, NEG, ALU.mult, ALU.add))
            own(g.memset(own_head[:], 1.0))
            own(g.affine_select(out=own_head[:], in_=own_head[:], compare_op=ALU.is_ge, fill=0.0, base=0,
                                pattern=[[-N, HPK], [-N * HPK, KVH]], channel_multiplier=1))
            g.affine_select(out=own_head[:], in_=own_head[:], compare_op=ALU.is_ge, fill=0.0, base=N - 1,
                            pattern=[[N, HPK], [N * HPK, KVH]], channel_multiplier=-1).then_inc(consts, 1)

        @block.tensor
        def _(pe):
            mm = nc.tensor.matmul
            pe.wait_ge(consts, 1)
            for g in range(KVH):
                for t in range(4):
                    mm(k.ps[HD * g:HD * g + HD, g, 0:N], k.kv[:, t, 2 * HD * g:2 * HD * g + HD], ind[:, t, 0, :],
                       start=(t == 0), stop=(t == 3))
            for t in range(4):
                last = mm(k.ps[:, 2, 0:P], ind[:, t].rearrange("p h n -> p (h n)"),
                          k.kv[:, t, 0:KVW].rearrange("p (g c d) -> p g c d", g=KVH, c=2)[:, :, 1, :],
                          start=(t == 0), stop=(t == 3))
            last.then_inc(means, 1)
            pe.wait_ge(mean_copied, 1)
            for t in range(4):
                if t >= 2:
                    pe.wait_ge(shifted, t - 1)
                for j in range(HPK):
                    for g in range(KVH):
                        hh = g * HPK + j
                        last = mm(k.ps[:, 3 + 2 * (t % 2) + g, hh * N:hh * N + N], k.qT[HD * g:HD * g + HD, j, P * t:P * t + P],
                                  kcT[HD * g:HD * g + HD, :], start=True, stop=True)
                last.then_inc(scored, 1)
            for t in range(4):
                pe.wait_ge(weighed, t + 1)
                if t >= 1:
                    pe.wait_ge(turned_copied, t)
                nc.tensor.transpose(k.ps[:, 0, 0:P], s[:, t].rearrange("p h n -> p (h n)"), k.ident[:]).then_inc(turned, 1)
                pe.wait_ge(turned_copied, t + 1)
                if t >= 1:
                    pe.wait_ge(stored, t)
                for i in range(2):
                    last = mm(k.ps[:, 1 + i, :], pT[:, t, :], vblk[:].rearrange("p j g d -> p (j g d)")[:, 512 * i:512 * i + 512],
                              start=True, stop=True)
                last.then_inc(out_done, 1)

        @block.scalar
        def _(act):
            for t in range(4):
                act.wait_ge(shifted, t + 1)
                nc.scalar.activation(s[:, t], s[:, t], ACT.Exp).then_inc(exped, 1)

        @block.vector
        def _(dve):
            v = nc.vector
            own = Link(dve, own_s)
            dve.wait_ge(means, 1)
            v.tensor_copy(kcT[0:HD, :], k.ps[0:HD, 0, 0:N])
            v.tensor_copy(kcT[HD:P, :], k.ps[HD:P, 1, 0:N])
            own(v.tensor_copy(vrep[:], k.ps[:, 2, 0:P]))
            for j in range(HPK):
                last = v.tensor_tensor(vblk[:, j], vrep[:].rearrange("p (g d) -> p g d", g=KVH),
                                       own_head[:, j, :].rearrange("p (g a) -> p g a", a=1).broadcast_to([P, KVH, HD]),
                                       ALU.mult)
            last.then_inc(mean_copied, 1)
            three = [P, AH, N]
            wide = lambda a: a.rearrange("p (h a) -> p h a", a=1).broadcast_to(three)
            over = lambda a: a.rearrange("p (a n) -> p a n", a=1).broadcast_to([P, HPK, N])
            for t in range(4):
                dve.wait_ge(scored, t + 1)
                for g in range(KVH):
                    own(v.tensor_tensor(s[:, t, HPK * g:HPK * g + HPK, :],
                                        k.ps[:, 3 + 2 * (t % 2) + g, g * HPK * N:(g + 1) * HPK * N].rearrange("p (h n) -> p h n", n=N),
                                        over(unseen[:, t, :]), ALU.add))
                own(v.tensor_reduce(m[:, t, :], s[:, t], AX.X, ALU.max))
                v.tensor_tensor(s[:, t], s[:, t], wide(m[:, t, :]), ALU.subtract).then_inc(shifted, 1)
            for t in range(4):
                dve.wait_ge(exped, t + 1)
                for g in range(KVH):
                    half = s[:, t, HPK * g:HPK * g + HPK, :]
                    own(v.tensor_tensor(half, half, over(seen[:, t, :]), ALU.mult))
                own(v.tensor_reduce(den[:, t, :], s[:, t], AX.X, ALU.add))
                own(v.tensor_scalar(den[:, t, :], den[:, t, :], 1e-30, None, ALU.max))
                own(v.reciprocal(den[:, t, :], den[:, t, :]))
                own(v.tensor_tensor(den[:, t, :], den[:, t, :], k.gates[:, t, 0:3 * AH:3], ALU.mult))
                v.tensor_tensor(s[:, t], s[:, t], wide(den[:, t, :]), ALU.mult).then_inc(weighed, 1)
            for t in range(4):
                dve.wait_ge(turned, t + 1)
                v.tensor_copy(pT[:, t, :], k.ps[:, 0, 0:P]).then_inc(turned_copied, 1)
                dve.wait_ge(out_done, t + 1)
                for i in range(2):
                    last = v.tensor_copy(k.onat[:, t, 512 * i:512 * i + 512], k.ps[:, 1 + i, :])
                last.then_inc(stored, 1)


def stage_attn_prompt(nc, k):
    with ExitStack() as ctx:
        sb = lambda n, s, d=F32: ctx.enter_context(nc.sbuf_tensor("ap_" + n, s, d))
        sem = lambda n: ctx.enter_context(nc.semaphore("ap_" + n))
        NPB = 3
        pbuf = sb("p", [P, NPB, SEQ])
        pT = sb("pT", [P, 2, SEQ])
        nmax = sb("nmax", [P, 4 * 2 * AH])
        ssum = sb("ssum", [P, 4 * 2 * AH])
        wgt = sb("wgt", [P, 4, HPK])
        o = sb("o", [P, 2, 512])
        scored, maxed, exped, turned, copied, valued, weighted, added, oturned, ostored, own_s = (
            sem(n) for n in ("scored", "maxed", "exped", "turned", "copied", "valued", "weighted", "added", "oturned",
                             "ostored", "own"))
        block = ctx.enter_context(nc.Block())
        units = [(t, br, g, j) for t in range(4) for br in (1, 2) for g in range(KVH) for j in range(HPK)]
        U = len(units)
        GR = U // HPK

        @block.tensor
        def _(pe):
            mm = nc.tensor.matmul

            def score(u):
                t, br, g, j = units[u]
                kT = k.ksT if br == 1 else k.kwT
                part = slice(HD * g, HD * g + HD)
                if u >= 3:
                    pe.wait_ge(exped, u - 2)
                n = P * (t + 1)
                mm(k.ps[:, u % 3, 0:n], k.qT[part, j, P * t:P * t + P], kT[part, 0:n], start=True, stop=False,
                   skip_group_check=True)
                mm(k.ps[:, u % 3, n - P:n], k.identb[:], k.causal[:], start=False, stop=True,
                   skip_group_check=True).then_inc(scored, 1)

            def turn(u):
                t = units[u][0]
                pe.wait_ge(exped, u + 1)
                if u >= 2:
                    pe.wait_ge(copied, u - 1)
                for kt in range(t + 1):
                    last = nc.tensor.transpose(k.ps[:, 3 + u % 2, kt * P:kt * P + P], pbuf[:, u % NPB, kt * P:kt * P + P],
                                               k.ident[:])
                last.then_inc(turned, 1)

            def value(u):
                t, br, g, j = units[u]
                pe.wait_ge(copied, u + 1)
                gr = u // HPK
                if j == 0 and gr >= 2:
                    pe.wait_ge(weighted, gr - 1)
                for kt in range(t + 1):
                    last = mm(k.ps[:, 5 + gr % 2, j * HD:j * HD + HD], pT[:, u % 2, kt * P:kt * P + P],
                              v_of(k.kv[:, kt, :], br, g), start=(kt == 0), stop=(kt == t))
                last.then_inc(valued, 1)

            def turn_out(n):
                t, i = n // 2, n % 2
                pe.wait_ge(added, 4 * t + 4)
                if n >= 1:
                    pe.wait_ge(ostored, n)
                for j in range(4):
                    last = nc.tensor.transpose(k.ps[:, 7, j * P:j * P + P],
                                               k.onat[:, t, (4 * i + j) * P:(4 * i + j) * P + P], k.ident[:])
                last.then_inc(oturned, 1)

            for i in range(U + 2):
                if i < U:
                    score(i)
                if 1 <= i <= U:
                    turn(i - 1)
                if i >= 2:
                    value(i - 2)
                if i % 32 in (14, 18) and i >= 32:
                    turn_out(2 * (i // 32 - 1) + (i % 32 == 18))
            turn_out(6)
            turn_out(7)

        @block.vector
        def _(dve):
            v = nc.vector
            own = Link(dve, own_s)

            def top(u):
                n = P * (units[u][0] + 1)
                dve.wait_ge(scored, u + 1)
                v.tensor_reduce(nmax[:, u:u + 1], k.ps[:, u % 3, 0:n], AX.X, ALU.max, negate=True).then_inc(maxed, 1)

            def copy(u):
                n = P * (units[u][0] + 1)
                dve.wait_ge(turned, u + 1)
                if u >= 2:
                    dve.wait_ge(valued, u - 1)
                v.tensor_copy(pT[:, u % 2, 0:n], k.ps[:, 3 + u % 2, 0:n]).then_inc(copied, 1)

            def weigh(gr):
                t, br, g, _ = units[gr * HPK]
                w = wgt[:, gr % 4, :]
                own(v.reciprocal(w, ssum[:, gr * HPK:gr * HPK + HPK]))
                own(v.tensor_tensor(w, w, k.gates[:, t, 3 * HPK * g + br:3 * HPK * (g + 1):3], ALU.mult))
                dve.wait_ge(valued, HPK * (gr + 1))
                oo = o[:, gr % 2, :].rearrange("p (j d) -> p j d", d=HD)
                v.tensor_tensor(oo, k.ps[:, 5 + gr % 2, :].rearrange("p (j d) -> p j d", d=HD), by_head(w, P),
                                ALU.mult).then_inc(weighted, 1)
                dve.wait_ge(weighted, gr + 1)
                dst = k.onat[:, t, :].rearrange("p (j g d) -> p j g d", g=KVH, d=HD)[:, :, g, :]
                if gr:
                    dve.wait_ge(added, gr)
                v.tensor_tensor(dst, dst, oo, ALU.add).then_inc(added, 1)

            for i in range(U + 4):
                if i < U:
                    top(i)
                if 1 <= i <= U:
                    copy(i - 1)
                if i >= 4 and (i - 4) % HPK == HPK - 1:
                    weigh((i - 4) // HPK)

        @block.scalar
        def _(act):
            def store(n):
                t, i = n // 2, n % 2
                act.wait_ge(oturned, n + 1)
                nc.scalar.copy(k.oT[:, 4 * i:4 * i + 4, P * t:P * t + P],
                               k.ps[:, 7, :].rearrange("p (j n) -> p j n", j=4)).then_inc(ostored, 1)

            for u in range(U):
                n = P * (units[u][0] + 1)
                act.wait_ge(maxed, u + 1)
                if u >= NPB:
                    act.wait_ge(turned, u - NPB + 1)
                nc.scalar.activation(pbuf[:, u % NPB, 0:n], k.ps[:, u % 3, 0:n], ACT.Exp, bias=nmax[:, u:u + 1],
                                     accum_out=ssum[:, u:u + 1]).then_inc(exped, 1)
                if u % 32 in (13, 17) and u >= 32:
                    store(2 * (u // 32 - 1) + (u % 32 == 17))
            store(6)
            store(7)


def hold(eng, sem, value, passed):
    eng.wait_ge(sem, value)
    eng.sem_inc(passed, 1)


def page_loop(nc, sp, k, cache, pages, page_in, free, page_row):
    rows_of = cache[0].rearrange("n p g c d -> n p (g c d)")
    n_pool = rows_of.shape[0]
    with sp.Fori(0, NB // 2) as pair:
        for half in range(2):
            if free is not None:
                free(pair, half)
            for pg in range(NPAGES):
                at = (pair * 2 + half) * NPAGES + pg
                page = sp.value_load(page_row[0:1, bass.ds(at, 1)], min_val=0, max_val=n_pool - 1)
                sp.dma_start(pages[:, half, pg, :], rows_of[bass.ds(page, 1)].rearrange("a p c -> p (a c)")).then_inc(
                    page_in[half], 16)


def stage_cmp_sample(nc, k):
    with ExitStack() as ctx:
        sb = lambda n, s, d=F32: ctx.enter_context(nc.sbuf_tensor("cs_" + n, s, d))
        sem = lambda n: ctx.enter_context(nc.semaphore("cs_" + n))
        N = NCMP_S
        AHEAD = 2
        pages = k.pages
        ind = sb("ind", [P, NPAGES, N])
        kmean, vmean = sb("kmean", [N, NB, P]), sb("vmean", [N, NB, P])
        kcT = sb("kcT", [P, NB, N])
        s = sb("s", [P, NB, N])
        m = sb("m", [P, NB])
        den = sb("den", [P, NB])
        pick = sb("pick", [P, NB, NSEL])
        force = sb("force", [P, NSEL])
        top = sb("top", [P, NB, 8])
        pT = sb("pT", [N, NB, P])
        group = sb("group", [P, 16, 8])
        passed = sem("passed")
        page_in = [sem("page_in0"), sem("page_in1")]
        table_in, gate_in, consts, pool_s, own_s, meant, mean_copied, turned, turned_copied, scored, exped, shifted = (
            sem(n) for n in ("table_in", "gate_in", "consts", "pool", "own", "meant", "mean_copied", "turned",
                             "turned_copied", "scored", "exped", "shifted"))
        weighed, imported, p_turned, p_copied, valued, qb_done = (
            sem(n) for n in ("weighed", "imported", "p_turned", "p_copied", "valued", "qb_done"))
        block = ctx.enter_context(nc.Block())

        @block.sync
        def _(sp):
            sp.sem_inc(meant, AHEAD)
            sp.dma_start(k.page_row[:], k.page_table.rearrange("b n -> (b n)").rearrange("(a n) -> a n", a=1)).then_inc(table_in, 16)
            gates = k.gates_dram.rearrange("(b t) (h c) -> t h b c", t=DS, c=3)
            for g in range(KVH):
                for t in range(DS):
                    r0 = (g * DS + t) * HPK
                    sp.dma_start(k.grow[r0:r0 + HPK], gates[t, g * HPK:(g + 1) * HPK]).then_inc(gate_in, 16)
            sp.wait_ge(table_in, 16)

            def free(pair, half):
                hold(sp, meant, pair * 2 + half - 1 + AHEAD, passed)
            page_loop(nc, sp, k, k.cache_cmp_kv, pages, page_in, free, k.page_row)

        @block.gpsimd
        def _(pool):
            g = nc.gpsimd
            own = Link(pool, pool_s)
            own(g.memset(ind[:], 1.0 / CMP))
            own(g.affine_select(out=ind[:], in_=ind[:], compare_op=ALU.is_ge, fill=0.0, base=0,
                                pattern=[[P, NPAGES], [-CMP, N]], channel_multiplier=1))
            own(g.affine_select(out=ind[:], in_=ind[:], compare_op=ALU.is_ge, fill=0.0, base=CMP - 1,
                                pattern=[[-P, NPAGES], [CMP, N]], channel_multiplier=-1))
            own(g.memset(group[:], 1.0))
            own(g.affine_select(out=group[:], in_=group[:], compare_op=ALU.is_ge, fill=0.0, base=0,
                                pattern=[[-8, 16], [0, 8]], channel_multiplier=1))
            own(g.affine_select(out=group[:], in_=group[:], compare_op=ALU.is_ge, fill=0.0, base=7,
                                pattern=[[8, 16], [0, 8]], channel_multiplier=-1))
            own(g.memset(force[:], 0.0))
            own(g.memset(force[:, 0:1], 1000.0))
            own(g.memset(force[:, NSEL - 2:NSEL], 1000.0))
            own(g.memset(k.step_mask[:], 0.0))
            own(g.memset(k.old_mask[:], 0.0))
            own(g.memset(k.new_mask[:], NEG))
            for lo in (0, HD):
                half = slice(lo, lo + HD)
                own(g.affine_select(out=k.step_mask[half], in_=k.step_mask[half], compare_op=ALU.is_ge, fill=NEG,
                                    base=0, pattern=[[-HPK, DS]], channel_multiplier=1))
                own(g.affine_select(out=k.old_mask[half], in_=k.old_mask[half], compare_op=ALU.is_ge, fill=NEG,
                                    base=HPK - 1, pattern=[[HPK, DS]], channel_multiplier=-1))
            for b in range(NB):
                own(g.tensor_copy(k.new_mask[:, b, DS * b:DS * b + DS], k.step_mask[:]))
            g.memset(k.qb[:], 0.0).then_inc(consts, 1)

        @block.tensor
        def _(pe):
            mm = nc.tensor.matmul
            pe.wait_ge(consts, 1)
            pe.wait_ge(qb_done, 1)
            for b in range(NB):
                pe.wait_ge(page_in[b % 2], 16 * NPAGES * (b // 2 + 1))
                if b >= 2:
                    pe.wait_ge(mean_copied, b - 1)
                for pg in range(NPAGES):
                    last = mm(k.ps[0:N, b % 2, 0:KVW], ind[:, pg, :], pages[:, b % 2, pg, :], start=(pg == 0),
                              stop=(pg == NPAGES - 1))
                last.then_inc(meant, 1)
                pe.wait_ge(mean_copied, b + 1)
                if b >= 2:
                    pe.wait_ge(turned_copied, b - 1)
                nc.tensor.transpose(k.ps[:, 2 + b % 2, 0:N], kmean[:, b], k.ident[0:N, 0:N]).then_inc(turned, 1)
                pe.wait_ge(turned_copied, b + 1)
                last = mm(k.ps[:, 4, b * N:b * N + N], k.qb[:, b], kcT[:, b, :], start=True, stop=True)
            last.then_inc(scored, 1)
            pe.wait_ge(weighed, 1)
            mm(k.ps[:, 5, 0:NB * N], group[:].rearrange("p a c -> p (a c)"), s[:].rearrange("p b n -> p (b n)"),
               start=True, stop=True).then_inc(imported, 1)
            pe.wait_ge(weighed, 2)
            for b in range(NB):
                last = nc.tensor.transpose(k.ps[0:N, 6 + b // 4, (b % 4) * P:(b % 4) * P + P], s[:, b, :], k.ident[:])
            last.then_inc(p_turned, 1)
            pe.wait_ge(p_copied, 1)
            for b in range(NB):
                last = mm(k.ps[:, b // 4, (b % 4) * P:(b % 4) * P + P], pT[:, b, :],
                          vmean[:, b], start=True, stop=True)
            last.then_inc(valued, 1)

        @block.scalar
        def _(act):
            act.wait_ge(shifted, 1)
            nc.scalar.activation(s[:], s[:], ACT.Exp).then_inc(exped, 1)

        @block.vector
        def _(dve):
            v = nc.vector
            own = Link(dve, own_s)
            dve.wait_ge(consts, 1)
            for g in range(KVH):
                part = slice(HD * g, HD * g + HD)
                for b in range(NB):
                    last = v.tensor_copy(k.qb[part, b].rearrange("p (g t j) -> p g t j", g=KVH, t=DS)[:, g],
                                         k.qT[part, :, SEQ + DS * b:SEQ + DS * b + DS].rearrange("p j t -> p t j"))
            last.then_inc(qb_done, 1)
            for b in range(NB):
                dve.wait_ge(meant, AHEAD + b + 1)
                both = k.ps[0:N, b % 2, 0:KVW].rearrange("n (g c d) -> n g c d", g=KVH, c=2)
                v.tensor_copy(kmean[:, b].rearrange("n (g d) -> n g d", g=KVH), both[:, :, 0, :])
                v.tensor_copy(vmean[:, b].rearrange("n (g d) -> n g d", g=KVH), both[:, :, 1, :]).then_inc(mean_copied, 1)
                dve.wait_ge(turned, b + 1)
                v.tensor_copy(kcT[:, b, :], k.ps[:, 2 + b % 2, 0:N]).then_inc(turned_copied, 1)
            dve.wait_ge(scored, 1)
            sc = k.ps[:, 4, 0:NB * N].rearrange("p (b n) -> p b n", n=N)
            wide = lambda a: a.rearrange("p (b a) -> p b a", a=1).broadcast_to([P, NB, N])
            own(v.tensor_reduce(m[:], sc, AX.X, ALU.max))
            v.tensor_tensor(s[:], sc, wide(m[:]), ALU.subtract).then_inc(shifted, 1)
            dve.wait_ge(exped, 1)
            own(v.tensor_reduce(den[:], s[:], AX.X, ALU.add))
            own(v.reciprocal(den[:], den[:]))
            v.tensor_tensor(s[:], s[:], wide(den[:]), ALU.mult).then_inc(weighed, 1)
            dve.wait_ge(imported, 1)
            dve.wait_ge(gate_in, 16 * DS * KVH)
            v.tensor_tensor(s[:], s[:], wide(k.grow[:, :, 0]), ALU.mult).then_inc(weighed, 1)
            over = force[:, 0:N].rearrange("p (a n) -> p a n", a=1).broadcast_to([P, NB, N])
            last_force = force[:, N:NSEL].rearrange("p (a n) -> p a n", a=1).broadcast_to([P, NB, 1])
            v.tensor_copy(pick[:, :, N:NSEL], last_force)
            own(v.tensor_tensor(pick[:, :, 0:N], k.ps[:, 5, 0:NB * N].rearrange("p (b n) -> p b n", n=N), over, ALU.add))
            for _ in range(TOPK // 8):
                for b in range(NB):
                    last = v.max(top[:, b, :], pick[:, b, :])
                own(last)
                for b in range(NB):
                    last = v.match_replace(out=pick[:, b, :], in_to_replace=top[:, b, :], in_values=pick[:, b, :],
                                           imm_value=NEG)
                own(last)
            own(v.tensor_scalar(k.sel_bias[:], pick[:], 0.1 * NEG, NEG, ALU.is_gt, ALU.mult))
            dve.wait_ge(p_turned, 1)
            for i in range(2):
                last = v.tensor_copy(pT[:, 4 * i:4 * i + 4, :], k.ps[0:N, 6 + i, :].rearrange("n (b p) -> n b p", b=4))
            last.then_inc(p_copied, 1)
            dve.wait_ge(valued, 1)
            for i in range(2):
                last = v.tensor_copy(k.acc[:, 4 * i:4 * i + 4, :], k.ps[:, i, :].rearrange("p (b c) -> p b c", b=4))
            own(last)


def stage_attn_sample(nc, k):
    with ExitStack() as ctx:
        sb = lambda n, s, d=F32: ctx.enter_context(nc.sbuf_tensor("as_" + n, s, d))
        sem = lambda n: ctx.enter_context(nc.semaphore("as_" + n))
        WPAGES = WINDOW // PAGE
        AHEAD = 3
        pages = k.pages
        wpages = sb("wpages", [P, 2, WPAGES, KVW])
        kT = sb("kT", [P, 2, PAST])
        s = sb("s", [P, 2, PAST + NS])
        pT = sb("pT", [P, NPAGES + 1, P])
        nmax = sb("nmax", [P, 2 * NB])
        ssum = sb("ssum", [P, 2 * NB])
        wgt = sb("wgt", [P, 2 * NB])
        packed = k.onat[:].rearrange("p a b -> p (a b)").rearrange("p (u i c) -> p u i c", u=2, i=NPAGES)
        packed_done = sem("packed")
        passed = sem("passed")
        page_in = [sem("page_in0"), sem("page_in1")]
        wpage_in = [sem("wpage_in0"), sem("wpage_in1")]
        turned, k_copied, p_copied, scored, masked, maxed, exped, valued, added, own_s, acc_turned, stored, p_turned = (
            sem(n) for n in ("turned", "k_copied", "p_copied", "scored", "masked", "maxed", "exped", "valued", "added",
                             "own", "acc_turned", "stored", "p_turned"))
        block = ctx.enter_context(nc.Block())
        U = 2 * NB
        npg = lambda u: NPAGES if u % 2 == 0 else WPAGES

        def page(u, i):
            return pages[:, (u // 2) % 2, i, :] if u % 2 == 0 else wpages[:, (u // 2) % 2, i, :]

        turns, index = [], {}
        for step in range(U + 1):
            todo = [("k", step, i) for i in range(npg(step) // 4)] if step < U else []
            if step:
                todo += [("p", step - 1, i) for i in range(npg(step - 1) // 4 + 1)]
            for job in todo:
                index[job] = len(turns)
                turns.append(job)
        copies_before = lambda kind, n: sum(1 for j in turns[:n + 1] if j[0] == kind)

        @block.sync
        def _(sp):
            old = k.cache_win_kv[0].rearrange("b (i p) g c d -> b p i (g c d)", p=P)

            sp.sem_inc(valued, AHEAD)

            def free(pair, half):
                hold(sp, valued, (pair * 2 + half) * 2 - 2 + AHEAD, passed)
                sp.dma_start(wpages[:, half], old[bass.ds(pair * 2 + half, 1)].rearrange("a p i c -> p (a i) c")).then_inc(
                    wpage_in[half], 16)
            page_loop(nc, sp, k, k.cache_sel_kv, pages, page_in, free, k.page_row)

        @block.gpsimd
        def _(pool):
            for u in range(U):
                b = u // 2
                if u % 2 == 0:
                    pool.wait_ge(page_in[b % 2], 16 * NPAGES * (b // 2 + 1))
                else:
                    pool.wait_ge(wpage_in[b % 2], 16 * (b // 2 + 1))
                if u >= 2:
                    pool.wait_ge(turned, copies_before("k", index["k", u - 2, npg(u) // 4 - 1]))
                src = pages[:, b % 2] if u % 2 == 0 else wpages[:, b % 2]
                src = src.rearrange("p i (g c d) -> p i g c d", g=KVH, c=2)
                dst = packed[:, u % 2, 0:npg(u), :].rearrange("p i (g d) -> p i g d", g=KVH)
                for g in range(KVH):
                    last = nc.gpsimd.tensor_copy(dst[:, :, g, :], src[:, :, g, 0, :])
                last.then_inc(packed_done, 1)

        @block.tensor
        def _(pe):
            mm = nc.tensor.matmul

            def bank_free(n):
                if n >= 2:
                    kind = turns[n - 2][0]
                    pe.wait_ge(k_copied if kind == "k" else p_copied, copies_before(kind, n - 2))

            def keys(u):
                b = u // 2
                pe.wait_ge(packed_done, u + 1)
                for i in range(npg(u) // 4):
                    n = index["k", u, i]
                    bank_free(n)
                    for q in range(4):
                        last = nc.tensor.transpose(k.ps[:, n % 2, q * P:q * P + P], packed[:, u % 2, 4 * i + q, :],
                                                   k.ident[:])
                    last.then_inc(turned, 1)
                if u:
                    pe.wait_ge(masked, u)
                for i in range(npg(u) // 4):
                    pe.wait_ge(k_copied, copies_before("k", index["k", u, i]))
                    mm(k.ps[:, 2 + i, :], k.qb[:, b], kT[:, u % 2, 512 * i:512 * i + 512], start=True, stop=True)
                new = k.ksT if u % 2 == 0 else k.kwT
                mm(k.ps[:, 6, 0:NS], k.qb[:, b], new[:, SEQ:T], start=True, stop=True).then_inc(scored, 1)

            def values(u):
                pe.wait_ge(exped, u + 1)
                for i in range(npg(u) // 4 + 1):
                    n = index["p", u, i]
                    bank_free(n)
                    if i < npg(u) // 4:
                        for q in range(4):
                            c = (4 * i + q) * P
                            last = nc.tensor.transpose(k.ps[:, n % 2, q * P:q * P + P], s[:, u % 2, c:c + P], k.ident[:])
                    else:
                        c = npg(u) * P
                        last = nc.tensor.transpose(k.ps[0:NS, n % 2, 0:P], s[:, u % 2, c:c + NS], k.ident[:])
                    last.then_inc(p_turned, 1)
                if u:
                    pe.wait_ge(added, u)
                for i in range(npg(u)):
                    if i % 4 == 0:
                        pe.wait_ge(p_copied, copies_before("p", index["p", u, i // 4]))
                    mm(k.ps[:, 7, 0:P], pT[:, i, :], page(u, i).rearrange("p (g c d) -> p g c d", g=KVH, c=2)[:, :, 1, :],
                       start=(i == 0), stop=False)
                pe.wait_ge(p_copied, copies_before("p", index["p", u, npg(u) // 4]))
                cols = slice((1 + u % 2) * KVW, (2 + u % 2) * KVW)
                mm(k.ps[:, 7, 0:P], pT[0:NS, NPAGES, :],
                   k.kv[0:NS, 4, cols].rearrange("p (g c d) -> p g c d", g=KVH, c=2)[:, :, 1, :], start=False,
                   stop=True).then_inc(valued, 1)

            for step in range(U + 1):
                if step < U:
                    keys(step)
                if step:
                    values(step - 1)
            pe.wait_ge(added, U)
            for i in range(2):
                for q in range(4):
                    last = nc.tensor.transpose(k.ps[:, 2 + i, q * P:q * P + P], k.acc[:, 4 * i + q, :], k.ident[:])
                last.then_inc(acc_turned, 1)

        @block.scalar
        def _(act):
            nk = 0
            for u in range(U):
                for i in range(npg(u) // 4):
                    n = index["k", u, i]
                    nk += 1
                    act.wait_ge(turned, nk)
                    if u >= 2 and i == 0:
                        act.wait_ge(scored, u - 1)
                    nc.scalar.copy(kT[:, u % 2, 512 * i:512 * i + 512], k.ps[:, n % 2, :]).then_inc(k_copied, 1)
                w = npg(u) * P + NS
                act.wait_ge(maxed, u + 1)
                nc.scalar.activation(s[:, u % 2, 0:w], s[:, u % 2, 0:w], ACT.Exp, bias=nmax[:, u:u + 1],
                                     accum_out=ssum[:, u:u + 1]).then_inc(exped, 1)

        @block.vector
        def _(dve):
            v = nc.vector
            own = Link(dve, own_s)

            def mask(u):
                b, n = u // 2, npg(u) * P
                dve.wait_ge(scored, u + 1)
                if u >= 2:
                    dve.wait_ge(valued, AHEAD + u - 1)
                for i in range(npg(u) // 4):
                    dst, src = s[:, u % 2, 512 * i:512 * i + 512], k.ps[:, 2 + i, :]
                    if u % 2 == 0:
                        v.tensor_tensor(dst.rearrange("p (n c) -> p n c", c=CMP), src.rearrange("p (n c) -> p n c", c=CMP),
                                        by_head(k.sel_bias[:, b, 8 * i:8 * i + 8], P, 8, CMP), ALU.add)
                    else:
                        v.tensor_tensor(dst[:, 0:DS], src[:, 0:DS], k.old_mask[:], ALU.add)
                        v.tensor_copy(dst[:, DS:], src[:, DS:])
                new = s[:, u % 2, n:n + NS]
                if u % 2 == 0:
                    last = v.scalar_tensor_tensor(out=new, in0=k.ps[:, 6, 0:NS], scalar=k.sel_bias[:, b, N_PAST:NSEL],
                                                  in1=k.new_mask[:, b, :], op0=ALU.add, op1=ALU.add)
                else:
                    last = v.tensor_tensor(new, k.ps[:, 6, 0:NS], k.new_mask[:, b, :], ALU.add)
                last.then_inc(masked, 1)
                dve.wait_ge(masked, u + 1)
                v.tensor_reduce(nmax[:, u:u + 1], s[:, u % 2, 0:n + NS], AX.X, ALU.max, negate=True).then_inc(maxed, 1)

            N_PAST = NCMP_S
            np_ = [0]

            def finish(u):
                b = u // 2
                for i in range(npg(u) // 4 + 1):
                    n = index["p", u, i]
                    np_[0] += 1
                    dve.wait_ge(p_turned, np_[0])
                    if u and i == 0:
                        dve.wait_ge(valued, AHEAD + u)
                    if i < npg(u) // 4:
                        v.tensor_copy(pT[:, 4 * i:4 * i + 4, :],
                                      k.ps[:, n % 2, :].rearrange("p (q c) -> p q c", q=4)).then_inc(p_copied, 1)
                    else:
                        v.tensor_copy(pT[0:NS, NPAGES, :], k.ps[0:NS, n % 2, 0:P]).then_inc(p_copied, 1)
                own(v.reciprocal(wgt[:, u:u + 1], ssum[:, u:u + 1]))
                own(v.tensor_tensor(wgt[:, u:u + 1], wgt[:, u:u + 1], k.grow[:, b, 1 + u % 2:2 + u % 2], ALU.mult))
                dve.wait_ge(valued, AHEAD + u + 1)
                if u:
                    dve.wait_ge(added, u)
                v.scalar_tensor_tensor(out=k.acc[:, b, :], in0=k.ps[:, 7, 0:P], scalar=wgt[:, u:u + 1],
                                       in1=k.acc[:, b, :], op0=ALU.mult, op1=ALU.add).then_inc(added, 1)

            for step in range(U + 1):
                if step < U:
                    mask(step)
                if step:
                    finish(step - 1)
            for i in range(2):
                dve.wait_ge(acc_turned, i + 1)
                for q in range(4):
                    b = 4 * i + q
                    for g in range(KVH):
                        part = slice(HD * g, HD * g + HD)
                        c = q * P + g * NS
                        v.tensor_copy(k.oT[part, :, SEQ + DS * b:SEQ + DS * b + DS].rearrange("p j t -> p t j"),
                                      k.ps[part, 2 + i, c:c + NS].rearrange("p (t j) -> p t j", t=DS))
            v.tensor_copy(wgt[:, 0:1], ssum[:, 0:1]).then_inc(stored, 1)
            dve.wait_ge(stored, 1)


def stage_out(nc, k):
    with ExitStack() as ctx:
        sb = lambda n, s, d=F32: ctx.enter_context(nc.sbuf_tensor("o_" + n, s, d))
        sem = lambda n: ctx.enter_context(nc.semaphore("o_" + n))
        w = sb("w", [P, 2, KD, 512])
        x = sb("x", [P, TILES, D])
        h = sb("h", [P, TILES, D])
        rest = sb("rest", [P, TILES, D])
        part = sb("part", [P, 3, TILES, D], BF16)
        junk = sb("junk", [P, D])
        row = sb("row", [P, D])
        ss, mean, root, rstd = (sb(n, [P, TILES]) for n in ("ss", "mean", "root", "rstd"))
        w_in = [sem("w_in0"), sem("w_in1")]
        x_in = [sem(f"x_in{t}") for t in range(TILES)]
        row_in, projected, added, squared, averaged, rooted, normed, turned, copied, parted, own_s, pool_s, written = (
            sem(n) for n in ("row_in", "projected", "added", "squared", "averaged", "rooted", "normed", "turned",
                             "copied", "parted", "own", "pool", "written"))
        block = ctx.enter_context(nc.Block())

        @block.sync
        def _(sp):
            for i in range(2):
                sp.dma_start(w[:, i], w_view(k.w_out, 512 * i, 512)).then_inc(w_in[i], 16)
            for t in range(TILES):
                src = k.x_prompt[0, P * t:P * t + P, :] if t < 4 else k.x_sample.rearrange("b s d -> (b s) d")
                sp.dma_start(x[0:rows(t), t, :], src).then_inc(x_in[t], 16)
            sp.dma_start(row[:], k.norm_ffn_w.partition_broadcast(P)[:, 0, :]).then_inc(row_in, 16)
            for t in range(TILES):
                r = rows(t)
                sp.wait_ge(added, t + 1)
                sp.dma_start(k.x1_dram[P * t:P * t + r], x[0:r, t]).then_inc(written, 16)
            for t in range(TILES):
                r = rows(t)
                sp.wait_ge(parted, t + 1)
                sp.dma_start(k.parts_dram[:, P * t:P * t + r].rearrange("c p d -> p c d"), part[0:r, :, t]).then_inc(written, 16)
            sp.wait_ge(written, 32 * TILES)

        @block.tensor
        def _(pe):
            def project(t):
                r = rows(t)
                if t >= 2:
                    pe.wait_ge(added, t - 1)
                for i in range(2):
                    if t == 0:
                        pe.wait_ge(w_in[i], 16)
                    for f in range(KD):
                        last = nc.tensor.matmul(k.ps[0:r, 2 * (t % 2) + i, :], k.mT[:, f, P * t:P * t + r], w[:, i, f, :],
                                                start=(f == 0), stop=(f == KD - 1))
                last.then_inc(projected, 1)

            def turn(t):
                r = rows(t)
                pe.wait_ge(normed, t + 1)
                if t >= 2:
                    pe.wait_ge(copied, t - 1)
                for f in range(KD):
                    b, o = 4 + 2 * (t % 2) + f // 4, (f % 4) * P
                    last = nc.tensor.transpose(k.ps[:, b, o:o + r], h[0:r, t, f * P:f * P + P], k.ident[0:r, 0:r])
                last.then_inc(turned, 1)

            for t in range(TILES + 1):
                if t < TILES:
                    project(t)
                if t:
                    turn(t - 1)

        @block.scalar
        def _(act):
            def copy(t):
                r = rows(t)
                act.wait_ge(turned, t + 1)
                for i in range(2):
                    src = k.ps[:, 4 + 2 * (t % 2) + i, :].rearrange("p (f n) -> p f n", f=4)[:, :, 0:r]
                    last = nc.scalar.copy(k.hT[:, 4 * i:4 * i + 4, P * t:P * t + r], src)
                last.then_inc(copied, 1)

            for t in range(TILES):
                r = rows(t)
                act.wait_ge(added, t + 1)
                if t:
                    act.wait_ge(squared, t)
                nc.scalar.activation(junk[0:r], x[0:r, t], ACT.Square, accum_out=ss[0:r, t:t + 1]).then_inc(squared, 1)
                act.wait_ge(averaged, t + 1)
                nc.scalar.activation(root[0:r, t:t + 1], mean[0:r, t:t + 1], ACT.Sqrt).then_inc(rooted, 1)
                if t:
                    copy(t - 1)
            copy(TILES - 1)

        @block.vector
        def _(dve):
            v = nc.vector
            own = Link(dve, own_s)
            dve.wait_ge(row_in, 16)
            for t in range(TILES):
                r = rows(t)
                dve.wait_ge(projected, t + 1)
                dve.wait_ge(x_in[t], 16)
                for i in range(2):
                    xx = x[0:r, t, 512 * i:512 * i + 512]
                    last = v.tensor_tensor(xx, xx, k.ps[0:r, 2 * (t % 2) + i, :], ALU.add)
                last.then_inc(added, 1)
                dve.wait_ge(squared, t + 1)
                v.tensor_scalar(mean[0:r, t:t + 1], ss[0:r, t:t + 1], 1.0 / D, EPS, ALU.mult, ALU.add).then_inc(averaged, 1)
                dve.wait_ge(rooted, t + 1)
                own(v.reciprocal(rstd[0:r, t:t + 1], root[0:r, t:t + 1]))
                v.scalar_tensor_tensor(out=h[0:r, t], in0=x[0:r, t], scalar=rstd[0:r, t:t + 1], in1=row[0:r],
                                       op0=ALU.mult, op1=ALU.mult).then_inc(normed, 1)

        @block.gpsimd
        def _(pool):
            g = nc.gpsimd
            own = Link(pool, pool_s)
            for t in range(TILES):
                r = rows(t)
                pool.wait_ge(normed, t + 1)
                own(g.tensor_copy(part[0:r, 0, t], h[0:r, t]))
                own(g.tensor_tensor(rest[0:r, t], h[0:r, t], part[0:r, 0, t], ALU.subtract))
                own(g.tensor_copy(part[0:r, 1, t], rest[0:r, t]))
                own(g.tensor_tensor(rest[0:r, t], rest[0:r, t], part[0:r, 1, t], ALU.subtract))
                g.tensor_copy(part[0:r, 2, t], rest[0:r, t]).then_inc(parted, 1)


def stage_route(nc, k):
    with ExitStack() as ctx:
        sb = lambda n, s, d=F32: ctx.enter_context(nc.sbuf_tensor("r_" + n, s, d))
        sem = lambda n: ctx.enter_context(nc.semaphore("r_" + n))
        NW, HC, K = 4, 2 * PH, TOPK
        wbuf = sb("w", [P, NW, KD, P])
        sk = sb("sk", [P, HC, P])
        skT = sb("skT", [P, HC, P])
        qT = sb("qT", [P, 2, T])
        s = sb("s", [P, 2, TILES, P])
        top = sb("top", [P, PH, 2, TILES, K])
        at = sb("at", [P, PH, 2, TILES, K], U32)
        atf = sb("atf", [P, 2, TILES, K])
        cand = sb("cand", [P, TILES, K * K])
        best = sb("best", [P, TILES, PH, K])
        pos = sb("pos", [P, TILES, K], U32)
        half = sb("half", [P, 2, TILES, K], U32)
        halff = sb("halff", [P, 2, TILES, K])
        iota = sb("iota", [P, K], I32)
        iotaf = sb("iotaf", [P, K])
        hit = sb("hit", [P, 2, K, K])
        pick = sb("pick", [P, 2, TILES, K])
        expert = sb("expert", [P, TILES, PH, K])
        den = sb("den", [P, TILES, PH])
        w_in = [sem(f"w_in{i}") for i in range(NW)]
        (sk_in, sk_turned, sk_copied, projected, q_copied, scored, s_copied, ranked, own_s, pool_s, iota_done, shifted,
         exped, routed, routed_turned) = (
            sem(n) for n in ("sk_in", "sk_turned", "sk_copied", "projected", "q_copied", "scored", "s_copied", "ranked",
                             "own", "pool", "iota", "shifted", "exped", "routed", "routed_turned"))
        block = ctx.enter_context(nc.Block())

        @block.sync
        def _(sp):
            sp.dma_start(sk[:], k.peer_sub_keys[0].rearrange("h c k d -> k (h c) d")).then_inc(sk_in, 16)
            for i in range(HC):
                if i >= NW:
                    sp.wait_ge(projected, i - NW + 1)
                sp.dma_start(wbuf[:, i % NW], w_view(k.peer_wq, P * i, P)).then_inc(w_in[i % NW], 16)

        @block.gpsimd
        def _(pool):
            own = Link(pool, pool_s)
            own(nc.gpsimd.iota(iota[:], pattern=[[1, K]], base=0, channel_multiplier=0))
            own(nc.gpsimd.tensor_copy(iotaf[:], iota[:]))
            nc.gpsimd.memset(s[NS:P, :, TILES - 1, :], 0.0).then_inc(iota_done, 1)

        @block.tensor
        def _(pe):
            mm = nc.tensor.matmul
            pe.wait_ge(sk_in, 16)
            for q in range(HC // 4):
                for i in range(4):
                    last = nc.tensor.transpose(k.ps[:, 4 + q, i * P:i * P + P], sk[:, 4 * q + i, :], k.ident[:])
                last.then_inc(sk_turned, 1)
            pe.wait_ge(sk_copied, 4)

            def query(i):
                pe.wait_ge(w_in[i % NW], 16 * (i // NW + 1))
                if i >= 2:
                    pe.wait_ge(q_copied, i - 1)
                for bank, cols in ((k.ps[:, 2 * (i % 2), :], slice(0, SEQ)), (k.ps[:, 2 * (i % 2) + 1, 0:NS], slice(SEQ, T))):
                    for f in range(KD):
                        last = mm(bank, wbuf[:, i % NW, f, :], k.hT[:, f, cols], start=(f == 0), stop=(f == KD - 1))
                last.then_inc(projected, 1)

            def score(i):
                pe.wait_ge(q_copied, i + 1)
                if i >= 2:
                    pe.wait_ge(s_copied, i - 1)
                for t in range(TILES):
                    r = rows(t)
                    b, c = 4 + 2 * (i % 2) + t // 4, (t % 4) * P
                    last = mm(k.ps[0:r, b, c:c + P], qT[:, i % 2, P * t:P * t + r], skT[:, i, :], start=True, stop=True)
                last.then_inc(scored, 1)

            for i in range(HC + 1):
                if i < HC:
                    query(i)
                if i:
                    score(i - 1)
            pe.wait_ge(routed, 1)
            for n, src in enumerate((expert, best)):
                for t in range(TILES):
                    r = rows(t)
                    b, c = 2 * n + t // 4, (t % 4) * P
                    last = nc.tensor.transpose(k.ps[:, b, c:c + r], src[0:r, t].rearrange("p h k -> p (h k)"),
                                               k.ident[0:r, 0:r])
            last.then_inc(routed_turned, 1)

        @block.scalar
        def _(act):
            a = nc.scalar
            for q in range(4):
                act.wait_ge(sk_turned, q + 1)
                a.copy(skT[:, 4 * q:4 * q + 4, :], k.ps[:, 4 + q, :].rearrange("p (i n) -> p i n", i=4)).then_inc(sk_copied, 1)

            def copy_s(i):
                act.wait_ge(scored, i + 1)
                if i >= 2:
                    act.wait_ge(ranked, i - 1)
                else:
                    act.wait_ge(iota_done, 1)
                b = 4 + 2 * (i % 2)
                a.copy(s[:, i % 2, 0:4, :], k.ps[:, b, :].rearrange("p (t n) -> p t n", t=4))
                a.copy(s[0:NS, i % 2, 4, :], k.ps[0:NS, b + 1, 0:P]).then_inc(s_copied, 1)

            for i in range(HC + 1):
                if i < HC:
                    act.wait_ge(projected, i + 1)
                    if i >= 2:
                        act.wait_ge(scored, i - 1)
                    a.copy(qT[:, i % 2, 0:SEQ], k.ps[:, 2 * (i % 2), :])
                    a.copy(qT[:, i % 2, SEQ:T], k.ps[:, 2 * (i % 2) + 1, 0:NS]).then_inc(q_copied, 1)
                if i:
                    copy_s(i - 1)
            act.wait_ge(shifted, 1)
            a.activation(best[:], best[:], ACT.Exp).then_inc(exped, 1)

        @block.vector
        def _(dve):
            v = nc.vector
            own = Link(dve, own_s)
            dve.wait_ge(iota_done, 1)

            def top16(values, tops, ats):
                n = len(values)
                for e in range(2):
                    part = slice(8 * e, 8 * e + 8)
                    for j in range(n):
                        last = v.max(tops[j][:, part], values[j])
                    own(last)
                    for j in range(n):
                        last = v.max_index(ats[j][:, part], tops[j][:, part], values[j])
                    if e == 0:
                        own(last)
                        for j in range(n):
                            last = v.match_replace(out=values[j], in_to_replace=tops[j][:, part], in_values=values[j],
                                                   imm_value=NEG)
                        own(last)
                return last

            for h in range(PH):
                for c in range(2):
                    i = 2 * h + c
                    dve.wait_ge(s_copied, i + 1)
                    top16([s[:, i % 2, t, :] for t in range(TILES)], [top[:, h, c, t, :] for t in range(TILES)],
                          [at[:, h, c, t, :] for t in range(TILES)]).then_inc(ranked, 1)
                    dve.wait_ge(ranked, i + 1)
                for t in range(TILES):
                    first = top[:, h, 0, t, :].rearrange("p (i a) -> p i a", a=1).broadcast_to([P, K, K])
                    second = top[:, h, 1, t, :].rearrange("p (a j) -> p a j", a=1).broadcast_to([P, K, K])
                    last = v.tensor_tensor(cand[:, t, :].rearrange("p (i j) -> p i j", i=K), first, second, ALU.add)
                own(last)
                own(top16([cand[:, t, :] for t in range(TILES)], [best[:, t, h, :] for t in range(TILES)],
                          [pos[:, t, :] for t in range(TILES)]))
                v.tensor_copy(atf[:], at[:, h])
                v.tensor_scalar(half[:, 0], pos[:], 4, None, ALU.logical_shift_right)
                own(v.tensor_scalar(half[:, 1], pos[:], K - 1, None, ALU.bitwise_and))
                own(v.tensor_copy(halff[:], half[:]))
                for t in range(TILES):
                    for c in range(2):
                        one = halff[:, c, t, :].rearrange("p (i a) -> p i a", a=1).broadcast_to([P, K, K])
                        io = iotaf[:].rearrange("p (a j) -> p a j", a=1).broadcast_to([P, K, K])
                        last = v.tensor_tensor(hit[:, c], one, io, ALU.is_equal)
                    own(last)
                    for c in range(2):
                        where = atf[:, c, t, :].rearrange("p (a j) -> p a j", a=1).broadcast_to([P, K, K])
                        last = v.tensor_tensor(hit[:, c], hit[:, c], where, ALU.mult)
                    own(last)
                    own(v.tensor_reduce(pick[:, :, t, :], hit[:], AX.X, ALU.add))
                own(v.scalar_tensor_tensor(out=expert[:, :, h, :], in0=pick[:, 0], scalar=float(PKEYS), in1=pick[:, 1],
                                           op0=ALU.mult, op1=ALU.add))
            top1 = best[:, :, :, 0:1]
            own(v.tensor_copy(den[:], top1.rearrange("p t h a -> p t (h a)")))
            flat = best[:].rearrange("p t h k -> p (t h) k")
            wide = den[:].rearrange("p t h -> p (t h)").rearrange("p (h a) -> p h a", a=1).broadcast_to([P, TILES * PH, K])
            v.tensor_tensor(flat, flat, wide, ALU.subtract).then_inc(shifted, 1)
            dve.wait_ge(exped, 1)
            own(v.tensor_reduce(den[:].rearrange("p t h -> p (t h)"), flat, AX.X, ALU.add))
            own(v.reciprocal(den[:], den[:]))
            v.tensor_tensor(flat, flat, wide, ALU.mult).then_inc(routed, 1)
            dve.wait_ge(routed_turned, 1)
            for n, dst in enumerate((k.experts, k.routew)):
                v.tensor_copy(dst[:, 0:SEQ], k.ps[:, 2 * n, :])
                last = v.tensor_copy(dst[:, SEQ:T], k.ps[:, 2 * n + 1, 0:NS])
            own(last)


def stage_experts(nc, k):
    with ExitStack() as ctx:
        sb = lambda n, s, d=F32: ctx.enter_context(nc.sbuf_tensor("e_" + n, s, d))
        sem = lambda n: ctx.enter_context(nc.semaphore("e_" + n))
        G, NU, NV, B = 32, 8, 16, 8
        BODY = 2 * G
        BATCHES = BODY // B
        ubuf, vbuf = sb("u", [P, NU, D]), sb("v", [P, NV, D])
        hp = sb("hp", [3 * G, 2, D], BF16)
        sel = sb("sel", [3 * G, G, P], BF16)
        x1 = sb("x1", [G, 2, D])
        y = sb("y", [G, 2, D])
        junk = sb("junk", [G, D])
        row = sb("row", [G, D])
        idx = sb("idx", [P, 2, G], U32)
        rw = sb("rw", [P, 2, G])
        dot = sb("dot", [P, BODY])
        act_ = sb("act", [P, BODY])
        wz = sb("wz", [P, 2, G * G])
        ss, mean, root, rstd = (sb(n, [G, 2]) for n in ("ss", "mean", "root", "rstd"))
        u_in = [sem(f"u_in{i}") for i in range(NU)]
        v_in = [sem(f"v_in{i}") for i in range(NV)]
        hp_in, x1_in, y_out = ([sem(f"{n}{i}") for i in range(2)] for n in ("hp_in", "x1_in", "y_out"))
        consts, row_in, staged, spread, dotted, gelud, weighed, summed, drained, squared, averaged, rooted, own_s, y_done, pool_s = (
            sem(n) for n in ("consts", "row_in", "staged", "spread", "dotted", "gelud", "weighed", "summed", "drained",
                             "squared", "averaged", "rooted", "own", "y_done", "pool"))
        passed_sp, passed_pool = sem("passed_sp"), sem("passed_pool")
        DOT0, SPREAD0, SUM0, DRAIN0 = NU, BODY, BATCHES, 2
        block = ctx.enter_context(nc.Block())
        u_rows, v_rows = k.peer_u, k.peer_v

        def in_turn(eng, body):
            with eng.Fori(0, SEQ // BODY) as it:
                body(it, False)
            body(SEQ // BODY, True)

        @block.sync
        def _(sp):
            sp.sem_inc(dotted, DOT0)
            sp.sem_inc(spread, SPREAD0)
            sp.sem_inc(summed, SUM0)
            sp.sem_inc(drained, DRAIN0)
            for half in range(2):
                sp.sem_inc(y_out[half], 16)
            sp.dma_start(row[:], k.final_norm_w.rearrange("(a d) -> a d", a=1).partition_broadcast(G)[:, 0, :]).then_inc(row_in, 16)
            parts = k.parts_dram

            def store(it, half, sample):
                hold(sp, y_done, it * 2 + half + 1, passed_sp)
                if sample:
                    dst = k.y_sample.rearrange("b t d -> (b t) d")[G * half:G * half + G]
                else:
                    dst = k.y_prompt[0][bass.ds(it * BODY + half * G, G)]
                sp.dma_start(dst, y[:, half, :]).then_inc(y_out[half], 16)

            def body(it, sample):
                for half in range(2):
                    hold(sp, spread, (it * 2 + half) * G - G + SPREAD0, passed_sp)
                    for c in range(3):
                        sp.dma_start(hp[G * c:G * c + G, half, :], parts[c][bass.ds(it * BODY + half * G, G)]).then_inc(
                            hp_in[half], 16)
                    hold(sp, drained, it * 2 + half - 1 + DRAIN0, passed_sp)
                    sp.dma_start(x1[:, half, :], k.x1_dram[bass.ds(it * BODY + half * G, G)]).then_inc(x1_in[half], 16)
                for half in range(2):
                    store(it, half, sample)
            in_turn(sp, body)
            for half in range(2):
                sp.wait_ge(y_out[half], 16 * (T // BODY + 1))

        @block.gpsimd
        def _(pool):
            g = nc.gpsimd
            own = Link(pool, pool_s)
            own(g.memset(wz[:], 0.0))
            own(g.memset(sel[:], 1.0))
            for c in range(3):
                part = sel[G * c:G * c + G]
                own(g.affine_select(out=part, in_=part, compare_op=ALU.is_equal, fill=0.0, base=0,
                                    pattern=[[-1, G], [0, P]], channel_multiplier=1))
            g.memset(dot[:], 0.0).then_inc(consts, 1)

            def body(it, sample):
                for t in range(BODY):
                    half, col = t // G, t % G
                    off = bass.IndirectOffsetOnAxis(ap=idx[:, half, col:col + 1], axis=0)
                    hold(pool, dotted, it * BODY + t + 1 - NU + DOT0, passed_pool)
                    if col == 0:
                        hold(pool, staged, it * 2 + half + 1, passed_pool)
                    g.indirect_dma_start(out=ubuf[:, t % NU, :], out_offset=None, in_=u_rows, in_offset=off).then_inc(
                        u_in[t % NU], 16)
                    if t % B == 0:
                        hold(pool, summed, it * BATCHES + t // B - 1 + SUM0, passed_pool)
                    g.indirect_dma_start(out=vbuf[:, t % NV, :], out_offset=None, in_=v_rows, in_offset=off).then_inc(
                        v_in[t % NV], 16)
            in_turn(pool, body)

        @block.tensor
        def _(pe):
            mm = nc.tensor.matmul
            pe.wait_ge(consts, 1)

            def spread_h(it, t):
                half, col = t // G, t % G
                if col == 0:
                    pe.wait_ge(hp_in[half], it * 48 + 48)
                pe.wait_ge(dotted, it * BODY + t - 1 + DOT0)
                for i in range(2):
                    last = mm(k.ps[:, 2 * (t % 2) + i, :], sel[:, col, :], hp[:, half, 512 * i:512 * i + 512], start=True,
                              stop=True)
                last.then_inc(spread, 1)

            def sum_v(it, t):
                half, col = t // G, t % G
                if t % B == 0:
                    pe.wait_ge(weighed, it * BATCHES + t // B + 1)
                if col == 0:
                    pe.wait_ge(drained, it * 2 + half - 1 + DRAIN0)
                pe.wait_ge(v_in[t % NV], 16 * (BODY // NV) * it + 16 * (t // NV + 1))
                for i in range(2):
                    last = mm(k.ps[0:G, 4 + 2 * half + i, :], wz[:, half, col * G:col * G + G],
                              vbuf[:, t % NV, 512 * i:512 * i + 512], start=(col == 0), stop=(col == G - 1),
                              skip_group_check=True)
                if t % B == B - 1:
                    last.then_inc(summed, 1)

            def body(it, sample):
                for t in range(BODY + B + 1):
                    if t < BODY:
                        spread_h(it, t)
                    if t >= B + 1:
                        sum_v(it, t - B - 1)
            in_turn(pe, body)

        @block.vector
        def _(dve):
            v = nc.vector
            dve.wait_ge(consts, 1)
            dve.wait_ge(row_in, 16)

            def weigh(it, q):
                half, col = (q * B) // G, (q * B) % G
                dve.wait_ge(gelud, it * BATCHES + q + 1)
                dve.wait_ge(summed, it * BATCHES + q + 1 - BATCHES + SUM0)
                diag = wz[:, half, (G + 1) * col:(G + 1) * (col + B - 1) + 1:G + 1]
                v.tensor_tensor(diag, act_[:, q * B:q * B + B], rw[:, half, col:col + B], ALU.mult).then_inc(weighed, 1)

            def add(it, half):
                dve.wait_ge(summed, it * BATCHES + (half + 1) * (G // B) + SUM0)
                dve.wait_ge(x1_in[half], it * 16 + 16)
                for i in range(2):
                    c = slice(512 * i, 512 * i + 512)
                    last = v.tensor_tensor(x1[:, half, c], x1[:, half, c], k.ps[0:G, 4 + 2 * half + i, :], ALU.add)
                last.then_inc(own_s, 1)

            def mean_of(it, half):
                dve.wait_ge(squared, it * 2 + half + 1)
                v.tensor_scalar(mean[:, half:half + 1], ss[:, half:half + 1], 1.0 / D, EPS, ALU.mult, ALU.add).then_inc(averaged, 1)

            def norm(it, half):
                dve.wait_ge(rooted, it * 2 + half + 1)
                v.reciprocal(rstd[:, half:half + 1], root[:, half:half + 1]).then_inc(own_r, 1)
                dve.wait_ge(y_out[half], it * 16 + 16)
                dve.wait_ge(own_r, it * 2 + half + 1)
                v.scalar_tensor_tensor(out=y[:, half, :], in0=x1[:, half, :], scalar=rstd[:, half:half + 1], in1=row[:],
                                       op0=ALU.mult, op1=ALU.mult).then_inc(y_done, 1)
                dve.wait_ge(y_done, it * 2 + half + 1)
                v.tensor_copy(mean[:, half:half + 1], rstd[:, half:half + 1]).then_inc(drained, 1)

            def body(it, sample):
                for t in range(BODY):
                    dve.wait_ge(u_in[t % NU], 16 * (BODY // NU) * it + 16 * (t // NU + 1))
                    dve.wait_ge(spread, it * BODY + t + 1 + SPREAD0)
                    uu = ubuf[:, t % NU, :]
                    v.tensor_tensor_reduce(uu, uu, k.ps[:, 2 * (t % 2):2 * (t % 2) + 2, :].rearrange("p a b -> p (a b)"),
                                           1.0, 0.0, ALU.mult, ALU.add, dot[:, t:t + 1]).then_inc(dotted, 1)
                    if t % B == 1 and t > B:
                        weigh(it, t // B - 1)
                    if t == G + 12:
                        add(it, 0)
                    if t == G + 14:
                        mean_of(it, 0)
                    if t == G + 16:
                        norm(it, 0)
                weigh(it, BATCHES - 1)
                add(it, 1)
                mean_of(it, 1)
                norm(it, 1)
            own_r = ctx.enter_context(nc.semaphore("e_own_r"))
            in_turn(dve, body)

        @block.scalar
        def _(act):
            a = nc.scalar

            def stage(it, half):
                act.wait_ge(summed, it * BATCHES + half * (G // B) - G // B + SUM0)
                a.copy(idx[:, half, :], k.experts[:, bass.ds(it * BODY + half * G, G)])
                a.copy(rw[:, half, :], k.routew[:, bass.ds(it * BODY + half * G, G)]).then_inc(staged, 1)

            def square(it, half):
                act.wait_ge(own_s, it * 2 + half + 1)
                a.activation(junk[:], x1[:, half, :], ACT.Square, accum_out=ss[:, half:half + 1]).then_inc(squared, 1)
                act.wait_ge(averaged, it * 2 + half + 1)
                a.activation(root[:, half:half + 1], mean[:, half:half + 1], ACT.Sqrt).then_inc(rooted, 1)

            def body(it, sample):
                stage(it, 0)
                for q in range(BATCHES):
                    act.wait_ge(dotted, it * BODY + B * (q + 1) + DOT0)
                    a.activation(act_[:, B * q:B * q + B], dot[:, B * q:B * q + B], ACT.Gelu_apprx_tanh).then_inc(gelud, 1)
                    if q == 1:
                        stage(it, 1)
                    if q == 4:
                        square(it, 0)
                square(it, 1)
            in_turn(act, body)


def build(nc, k):
    with ExitStack() as ctx:
        allocate(nc, k, ctx)
        stage_norm(nc, k)
        with ExitStack() as ssm:
            allocate_ssm(nc, k, ssm)
            stage_conv(nc, k)
            natural_projection(nc, k, "z", z_blocks(k))
            stage_decays(nc, k)
            stage_sample_state(nc, k)
            stage_ssd(nc, k)
            stage_gate(nc, k)
            stage_branch(nc, k, "bs", COL_BG, k.w_ssm_branch, 16, load_rows,
                         lambda f: k.xnat[:, 0:4, P * f:P * f + P], lambda f: yT(k, 4)[:, f, :], False)
        with ExitStack() as attn:
            allocate_attn(nc, k, attn)
            natural_projection(nc, k, "kv", kv_blocks(k))
            stage_qk(nc, k)
            stage_cmp_prompt(nc, k)
            stage_attn_prompt(nc, k)
            clear_semaphores(nc)
            stage_cmp_sample(nc, k)
            stage_attn_sample(nc, k)
            stage_branch(nc, k, "ba", COL_BG + D, k.w_attn_branch, HPK, load_head_rows,
                         lambda f: k.oT[:, f, 0:SEQ], lambda f: k.oT[:, f, SEQ:T], True)
        with ExitStack() as peer:
            allocate_peer(nc, k, peer)
            stage_out(nc, k)
            stage_route(nc, k)
            stage_experts(nc, k)


def clear_semaphores(nc):
    free = sorted(nc.free_semaphores)
    assert free == list(range(free[0], free[-1] + 1))
    with nc.Block() as block:
        @block.gpsimd
        def _(pool):
            pool.sem_clear(range(free[0], free[-1] + 1))


def allocate(nc, k, ctx):
    sb = lambda n, s, d=F32: ctx.enter_context(nc.sbuf_tensor(n, s, d))
    k.ps = ctx.enter_context(nc.psum_tensor("ps", [P, 8, 512], F32))
    k.ident, k.ones, k.cum = sb("ident", [P, P]), sb("ones", [P, P]), sb("cum", [P, P])
    k.identb, k.later, k.causal = sb("identb", [P, P], BF16), sb("later", [P, P], BF16), sb("causal", [P, P], BF16)
    k.same, k.cum_s, k.later_s = sb("same", [NS, NS]), sb("cum_s", [NS, NS]), sb("later_s", [NS, NS], BF16)
    k.dt_bias_row, k.a_row, k.dskip_row = (sb(n, [P, HEADS]) for n in ("dt_bias_row", "a_row", "dskip_row"))
    k.vcol = sb("vcol", [P, 152])
    k.norm_mix_col, k.norm_ffn_col, k.ssm_norm_col = k.vcol[:, 0:8], k.vcol[:, 8:16], k.vcol[:, 16:32]
    k.conv_b_col, k.conv_w_col = k.vcol[:, 32:56], k.vcol[:, 56:152]
    k.hT = sb("hT", [P, KD, T])
    k.mT = sb("mT", [P, KD, T])
    k.BT, k.CT = k.mT[:, 0:4, :], k.mT[:, 4:8, :]


def allocate_ssm(nc, k, ctx):
    sb = lambda n, s, d=F32: ctx.enter_context(nc.sbuf_tensor(n, s, d))
    k.xnat = sb("xnat", [P, TILES, D_INNER])
    k.znat = sb("znat", [P, TILES, D_INNER])
    k.Bnat = sb("Bnat", [P, TILES, GROUPS * STATE])
    k.dt, k.da, k.nacum, k.eacum, k.to_end, k.cdec = (
        sb(n, [P, TILES, HEADS]) for n in ("dt", "da", "nacum", "eacum", "to_end", "cdec"))
    k.tail_dec = sb("tail_dec", [P, 16, NB])
    k.yt = sb("yt", [P, 16, NS])
    k.ysq = sb("ysq", [P, TILES, GROUPS])


def allocate_attn(nc, k, ctx):
    sb = lambda n, s, d=F32: ctx.enter_context(nc.sbuf_tensor(n, s, d))
    k.qT = sb("qT", [P, HPK, T])
    k.ksT, k.kwT = sb("ksT", [P, T]), sb("kwT", [P, T])
    k.kv = sb("kv", [P, TILES, 3 * KVW])
    k.gates = sb("gates", [P, TILES, 3 * AH])
    k.oT = sb("oT", [P, HPK, T])
    k.onat = sb("onat", [P, 4, AH * HD])
    k.pages = sb("pages", [P, 2, NPAGES, KVW])
    k.page_row = sb("page_row", [1, NB * NPAGES], I32)
    k.grow = sb("grow", [P, NB, 3])
    k.qb = sb("qb", [P, NB, P])
    k.acc = sb("acc", [P, NB, P])
    k.sel_bias = sb("sel_bias", [P, NB, NSEL])
    k.step_mask, k.old_mask = sb("step_mask", [P, DS]), sb("old_mask", [P, DS])
    k.new_mask = sb("new_mask", [P, NB, NS])
    k.gates_dram = nc.dram_tensor("gates_scratch", (NS, 3 * AH), F32).ap()


def allocate_peer(nc, k, ctx):
    sb = lambda n, s, d=F32: ctx.enter_context(nc.sbuf_tensor(n, s, d))
    k.experts = sb("experts", [P, T], U32)
    k.routew = sb("routew", [P, T])
    k.x1_dram = nc.dram_tensor("x1_scratch", (T, D), F32).ap()
    k.parts_dram = nc.dram_tensor("h_parts_scratch", (3, T, D), BF16).ap()


def z_blocks(k):
    def z(i):
        return lambda t: k.znat[0:rows(t), t, 512 * i:512 * i + 512]
    return [(COL_Z + 512 * i, 512, z(i), ACT.Silu) for i in range(4)] + [
        (COL_DT, HEADS, lambda t: k.dt[0:rows(t), t, :], ACT.Copy)]


def kv_blocks(k):
    return [(COL_KV, 512, lambda t: k.kv[0:rows(t), t, 0:512], ACT.Copy),
            (COL_KV + 512, 256, lambda t: k.kv[0:rows(t), t, 512:768], ACT.Copy),
            (COL_NG, 3 * AH, lambda t: k.gates[0:rows(t), t, :], ACT.Sigmoid)]


INPUTS = ['x_prompt', 'x_sample', 'cache_cmp_kv', 'cache_sel_kv', 'cache_win_kv', 'state_ssm', 'state_conv',
          'page_table', 'norm_mix_w', 'w_in', 'conv_w', 'conv_b', 'dt_bias', 'a_log', 'd_skip', 'ssm_norm_w',
          'w_ssm_branch', 'w_attn_branch', 'w_out', 'norm_ffn_w', 'peer_wq', 'peer_sub_keys', 'peer_u', 'peer_v',
          'final_norm_w']
OUTPUTS = [('y_prompt', (1, SEQ, D)), ('y_sample', (NB, DS, D)),
           ('new_cmp_kv_prompt', (1, 1, SEQ, KVH, 2, HD)), ('new_cmp_kv_sample', (1, NB, DS, KVH, 2, HD)),
           ('new_sel_kv_prompt', (1, 1, SEQ, KVH, 2, HD)), ('new_sel_kv_sample', (1, NB, DS, KVH, 2, HD)),
           ('new_win_kv_prompt', (1, 1, WINDOW, KVH, 2, HD)), ('new_win_kv_sample', (1, NB, WINDOW, KVH, 2, HD)),
           ('new_ssm_prompt', (1, 1, HEADS, HP, STATE)), ('new_ssm_sample', (1, NB, HEADS, HP, STATE)),
           ('new_conv_prompt', (1, 1, CONV_W - 1, CONV_DIM)), ('new_conv_sample', (1, NB, CONV_W - 1, CONV_DIM))]
MATRICES = ('w_in', 'w_ssm_branch', 'w_attn_branch', 'w_out', 'peer_wq', 'peer_u', 'peer_v')


def name_tensors(k, aps):
    (k.x_prompt, k.x_sample, k.cache_cmp_kv, k.cache_sel_kv, k.cache_win_kv, k.state_ssm, k.state_conv,
     k.page_table, k.norm_mix_w, k.w_in, k.conv_w, k.conv_b, k.dt_bias, k.a_log, k.d_skip, k.ssm_norm_w,
     k.w_ssm_branch, k.w_attn_branch, k.w_out, k.norm_ffn_w, k.peer_wq, k.peer_sub_keys, k.peer_u, k.peer_v,
     k.final_norm_w) = (aps[name] for name in INPUTS)
    (k.y_prompt, k.y_sample, k.new_cmp_kv_prompt, k.new_cmp_kv_sample, k.new_sel_kv_prompt, k.new_sel_kv_sample,
     k.new_win_kv_prompt, k.new_win_kv_sample, k.new_ssm_prompt, k.new_ssm_sample, k.new_conv_prompt,
     k.new_conv_sample) = (aps[name] for name, _ in OUTPUTS)


def kernel(**inputs):
    import numpy as np
    import concourse.bacc as bacc
    from concourse.bass_utils import run_bass_kernel_spmd

    nc = bacc.Bacc("TRN2", target_bir_lowering=False, num_devices=1)
    arrays, aps = {}, {}
    for name in INPUTS:
        a = np.ascontiguousarray(inputs[name])
        arrays[f"in_{name}"] = a
        ap = nc.dram_tensor(f"in_{name}", a.shape, mybir.dt.from_np(a.dtype), kind="ExternalInput").ap()
        aps[name] = ap[0] if name in MATRICES else ap
    for name, shape in OUTPUTS:
        aps[name] = nc.dram_tensor(f"out_{name}", shape, F32, kind="ExternalOutput").ap()
    k = Shared()
    name_tensors(k, aps)
    build(nc, k)
    r = run_bass_kernel_spmd(nc, [arrays], core_ids=[0])
    return tuple(r.results[0][f"out_{name}"] for name, _ in OUTPUTS)
```

```python
from contextlib import ExitStack

import concourse.bass as bass
from concourse import mybir

F32 = mybir.dt.float32
BF16 = mybir.dt.bfloat16
U32 = mybir.dt.uint32
I32 = mybir.dt.int32
ALU = mybir.AluOpType
ACT = mybir.ActivationFunctionType
AX = mybir.AxisListType

P = 128
D = 1024
SEQ = 512
NB = 8
DS = 8
NS = NB * DS
T = SEQ + NS
TILES = 5
KD = D // P
D_INNER = 2048
HEADS = 32
HP = 64
GROUPS = 4
STATE = 128
CONV_W = 4
CONV_DIM = D_INNER + 2 * GROUPS * STATE
CT_TILES = CONV_DIM // P
AH = 16
HD = 64
KVH = 2
HPK = AH // KVH
PAST = 2048
PAGE = 128
NPAGES = PAST // PAGE
WINDOW = 512
CMP = 64
NCMP_P = SEQ // CMP
NCMP_S = PAST // CMP
NSEL = NCMP_S + 1
TOPK = 16
SCALE = HD ** -0.5
PH = 8
HG = 32
WRING = 32
PKEYS = 128
EPS = 1e-6
NEG = -1e30

COL_Z = 0
COL_XBC = D_INNER
COL_DT = COL_XBC + CONV_DIM
COL_Q = COL_DT + HEADS
COL_KV = COL_Q + AH * HD
KVW = 2 * KVH * HD
COL_NG = COL_KV + 3 * KVW
COL_BG = COL_NG + 3 * AH
PROJ = COL_BG + 2 * D


def rows(t):
    return P if t < TILES - 1 else NS


def yT(k, t):
    return k.xnat[:, t, 0:16 * rows(t)].rearrange("p (f n) -> p f n", f=16)


def w_view(w, c0, n):
    return w[:, c0:c0 + n].rearrange("(k p) n -> p k n", p=P)


class Shared:
    pass


class Link:

    def __init__(self, eng, sem):
        self.eng, self.sem, self.n = eng, sem, 0

    def __call__(self, ins):
        self.n += 1
        ins.then_inc(self.sem, 1)
        self.eng.wait_ge(self.sem, self.n)


def stage_norm(nc, k):
    with ExitStack() as ctx:
        sb = lambda n, s, d=F32: ctx.enter_context(nc.sbuf_tensor(n, s, d))
        sem = lambda n: ctx.enter_context(nc.semaphore(n))
        x = sb("n_x", [P, TILES, D])
        junk = sb("n_junk", [P, D])
        vec_a = sb("n_vec_a", [32, P])
        vec_b = sb("n_vec_b", [120, P])
        ss = sb("n_ss", [P, TILES])
        mean = sb("n_mean", [P, TILES])
        root = sb("n_root", [P, TILES])
        rstd = sb("n_rstd", [P, TILES])
        x_in = [sem(f"n_x_in{t}") for t in range(TILES)]
        vec_in, const_set, consts_done = sem("n_vec_in"), sem("n_const_set"), sem("n_consts_done")
        squared, mean_done, rooted = sem("n_squared"), sem("n_mean_done"), sem("n_rooted")
        scaled, turned, vec_turned, evacuated, dve_own = (
            sem("n_scaled"), sem("n_turned"), sem("n_vec_turned"), sem("n_evacuated"), sem("n_dve_own"))
        block = ctx.enter_context(nc.Block())

        @block.sync
        def _(sp):
            for t in range(TILES):
                src = k.x_prompt[0, P * t:P * t + P, :] if t < 4 else k.x_sample.rearrange("b s d -> (b s) d")
                sp.dma_start(x[0:rows(t), t, :], src).then_inc(x_in[t], 16)
            for dst, src in (
                (vec_a[0:8, :], k.norm_mix_w[0].rearrange("(a p) -> a p", p=P)),
                (vec_a[8:16, :], k.norm_ffn_w[0].rearrange("(a p) -> a p", p=P)),
                (vec_a[16:32, :], k.ssm_norm_w[0].rearrange("(a p) -> a p", p=P)),
                (vec_b[0:24, :], k.conv_b[0].rearrange("(a p) -> a p", p=P)),
                (vec_b[24:120, :], k.conv_w[0].rearrange("w (a p) -> (w a) p", p=P)),
                (k.dt_bias_row[:], k.dt_bias.partition_broadcast(P)[:, 0, :]),
                (k.a_row[:], k.a_log.partition_broadcast(P)[:, 0, :]),
                (k.dskip_row[:], k.d_skip.partition_broadcast(P)[:, 0, :]),
            ):
                sp.dma_start(dst, src).then_inc(vec_in, 16)

        @block.gpsimd
        def _(pool):
            own = Link(pool, const_set)
            g = nc.gpsimd
            own(g.memset(k.ident[:], 0.0))
            own(g.affine_select(out=k.ident[:], in_=k.ident[:], compare_op=ALU.not_equal, fill=1.0, base=0,
                                pattern=[[-1, P]], channel_multiplier=1))
            own(g.tensor_copy(k.identb[:], k.ident[:]))
            own(g.memset(k.ones[:], 1.0))
            own(g.affine_select(out=k.cum[:], in_=k.ones[:], compare_op=ALU.is_ge, fill=0.0, base=0,
                                pattern=[[1, P]], channel_multiplier=-1))
            own(g.memset(k.later[:], 0.0))
            own(g.affine_select(out=k.later[:], in_=k.later[:], compare_op=ALU.is_ge, fill=NEG, base=0,
                                pattern=[[1, P]], channel_multiplier=-1))
            own(g.memset(k.causal[:], 0.0))
            own(g.affine_select(out=k.causal[:], in_=k.causal[:], compare_op=ALU.is_ge, fill=NEG, base=0,
                                pattern=[[-1, P]], channel_multiplier=1))
            same = k.same[:].rearrange("p (b t) -> p b t", b=NB)
            own(g.memset(k.same[:], 1.0))
            own(g.affine_select(out=same, in_=same, compare_op=ALU.is_ge, fill=0.0, base=0,
                                pattern=[[-DS, NB], [0, DS]], channel_multiplier=1))
            own(g.affine_select(out=same, in_=same, compare_op=ALU.is_ge, fill=0.0, base=DS - 1,
                                pattern=[[DS, NB], [0, DS]], channel_multiplier=-1))
            own(g.tensor_tensor(k.cum_s[:], k.same[:], k.cum[0:NS, 0:NS], ALU.mult))
            g.tensor_scalar(k.later_s[:], k.cum_s[:], -NEG, NEG, ALU.mult, ALU.add).then_inc(consts_done, 1)

        @block.scalar
        def _(act):
            for t in range(TILES):
                r = rows(t)
                act.wait_ge(x_in[t], 16)
                if t:
                    act.wait_ge(squared, t)
                nc.scalar.activation(junk[0:r, :], x[0:r, t, :], ACT.Square,
                                     accum_out=ss[0:r, t:t + 1]).then_inc(squared, 1)
            for t in range(TILES):
                r = rows(t)
                act.wait_ge(mean_done, t + 1)
                nc.scalar.activation(root[0:r, t:t + 1], mean[0:r, t:t + 1], ACT.Sqrt).then_inc(rooted, 1)
            act.wait_ge(vec_in, 16 * 8)
            nc.scalar.activation(k.a_row[:], k.a_row[:], ACT.Exp).then_inc(rooted, 1)

        @block.vector
        def _(dve):
            v = nc.vector
            own = Link(dve, dve_own)
            for t in range(TILES):
                r = rows(t)
                dve.wait_ge(squared, t + 1)
                v.tensor_scalar(mean[0:r, t:t + 1], ss[0:r, t:t + 1], 1.0 / D, EPS, ALU.mult,
                                ALU.add).then_inc(mean_done, 1)
            for t in range(TILES):
                r = rows(t)
                dve.wait_ge(rooted, t + 1)
                own(v.reciprocal(rstd[0:r, t:t + 1], root[0:r, t:t + 1]))
                v.tensor_scalar(x[0:r, t, :], x[0:r, t, :], rstd[0:r, t:t + 1], None, ALU.mult).then_inc(scaled, 1)
            dve.wait_ge(vec_turned, 1)
            own(v.tensor_copy(k.vcol[:, 0:32], k.ps[:, 6, 0:32]))
            own(v.tensor_copy(k.vcol[:, 32:152], k.ps[:, 7, 0:120]))
            dve.wait_ge(rooted, TILES + 1)
            own(v.tensor_scalar(k.a_row[:], k.a_row[:], -1.0, None, ALU.mult))
            for t in range(TILES):
                r = rows(t)
                dve.wait_ge(turned, t + 1)
                for f in range(KD):
                    b, o = 2 * (t % 2) + f // 4, (f % 4) * P
                    last = v.tensor_scalar(k.hT[:, f, P * t:P * t + r], k.ps[:, b, o:o + r],
                                           k.norm_mix_col[:, f:f + 1], None, ALU.mult)
                last.then_inc(evacuated, 1)

        @block.tensor
        def _(pe):
            pe.wait_ge(consts_done, 1)
            pe.wait_ge(vec_in, 16 * 8)
            nc.tensor.transpose(k.ps[:, 6, 0:32], vec_a[:], k.ident[0:32, 0:32])
            nc.tensor.transpose(k.ps[:, 7, 0:120], vec_b[:], k.ident[0:120, 0:120]).then_inc(vec_turned, 1)
            for t in range(TILES):
                r = rows(t)
                pe.wait_ge(scaled, t + 1)
                if t >= 2:
                    pe.wait_ge(evacuated, t - 1)
                for f in range(KD):
                    b, o = 2 * (t % 2) + f // 4, (f % 4) * P
                    last = nc.tensor.transpose(k.ps[:, b, o:o + r], x[0:r, t, f * P:f * P + P],
                                               k.ident[0:r, 0:r])
                last.then_inc(turned, 1)


def stage_conv(nc, k):
    with ExitStack() as ctx:
        sb = lambda n, s, d=F32: ctx.enter_context(nc.sbuf_tensor(n, s, d))
        sem = lambda n: ctx.enter_context(nc.semaphore(n))
        WB = 256
        NW = 3
        wbuf = sb("c_w", [P, NW, KD, WB])
        cin_p = sb("c_in_p", [P, 2, CONV_W - 1 + SEQ])
        cin_s = sb("c_in_s", [P, 2, NB, CONV_W - 1 + DS])
        acc = sb("c_acc", [P, 2, T])
        out = sb("c_out", [P, 2, T])
        state = sb("c_state", [NB * 3, CONV_DIM])
        tail = sb("c_tail", [P, 2, 27])
        tails = sb("c_tails", [27, CONV_DIM])
        w_in = [sem(f"c_w_in{i}") for i in range(NW)]
        state_in, projected, filled, convolved, activated = (
            sem("c_state_in"), sem("c_projected"), sem("c_filled"), sem("c_convolved"), sem("c_activated"))
        turned, dve_own, tailed, tail_turned, padded, written = (
            sem("c_turned"), sem("c_dve_own"), sem("c_tailed"), sem("c_tail_turned"), sem("c_padded"),
            sem("c_written"))
        block = ctx.enter_context(nc.Block())
        per = WB // P
        N = CT_TILES
        X_TILES = D_INNER // P
        B_TILES = X_TILES + GROUPS

        def bank(f):
            return 2 * (f % 2)

        @block.sync
        def _(sp):
            for i in range(N // per):
                if i == 1:
                    sp.dma_start(state[:], k.state_conv[0].rearrange("b w c -> (b w) c")).then_inc(state_in, 16)
                if i >= NW:
                    sp.wait_ge(projected, per * (i - NW + 1))
                sp.dma_start(wbuf[:, i % NW], w_view(k.w_in, COL_XBC + WB * i, WB)).then_inc(w_in[i % NW], 16)
            sp.wait_ge(tail_turned, N)
            sp.dma_start(k.new_conv_prompt[0, 0], tails[0:3, :]).then_inc(written, 16)
            sp.dma_start(k.new_conv_sample[0].rearrange("b w c -> (b w) c"), tails[3:27, :]).then_inc(written, 16)
            sp.wait_ge(written, 32)

        @block.gpsimd
        def _(pool):
            nc.gpsimd.memset(k.dt[:], 0.0)
            nc.gpsimd.memset(cin_p[:, :, 0:3], 0.0).then_inc(padded, 1)

        @block.tensor
        def _(pe):
            def project(f):
                pe.wait_ge(w_in[(f // per) % NW], 16 * (f // per // NW + 1))
                if f >= 2:
                    pe.wait_ge(filled, f - 1)
                b = bank(f)
                c = (f % per) * P
                for kk in range(KD):
                    nc.tensor.matmul(k.ps[:, b, :], wbuf[:, (f // per) % NW, kk, c:c + P], k.hT[:, kk, 0:SEQ],
                                     start=(kk == 0), stop=(kk == KD - 1))
                for kk in range(KD):
                    nc.tensor.matmul(k.ps[:, b + 1, 0:NS], wbuf[:, (f // per) % NW, kk, c:c + P],
                                     k.hT[:, kk, SEQ:T], start=(kk == 0), stop=(kk == KD - 1))
                if f == 0:
                    pe.wait_ge(state_in, 16)
                nc.tensor.transpose(k.ps[:, b + 1, NS:NS + 24], state[:, f * P:f * P + P],
                                    k.ident[0:24, 0:24]).then_inc(projected, 1)

            def turn(f):
                if f >= 2:
                    pe.wait_ge(tail_turned, f - 1)
                pe.wait_ge(tailed, f + 1)
                b = 4 + bank(f)
                if f < B_TILES:
                    pe.wait_ge(activated, f + 1)
                    for t in range(TILES):
                        r = rows(t)
                        src = out[:, f % 2, P * t:P * t + r] if f < X_TILES else k.BT[:, f - X_TILES, P * t:P * t + r]
                        dst = k.ps[:, b, P * t:P * t + P] if t < 4 else k.ps[0:r, b + 1, 0:P]
                        nc.tensor.transpose(dst, src, k.ident[:])
                nc.tensor.transpose(k.ps[0:27, b + 1, P:2 * P], tail[:, f % 2, :], k.ident[:]).then_inc(turned, 1)

            for f in range(N + 1):
                if f < N:
                    project(f)
                if f:
                    turn(f - 1)

        @block.scalar
        def _(act):
            a = nc.scalar
            for f in range(N):
                act.wait_ge(projected, f + 1)
                if f == 0:
                    act.wait_ge(padded, 1)
                if f >= 2:
                    act.wait_ge(convolved, f - 1)
                    act.wait_ge(tailed, f - 1)
                b = bank(f)
                a.copy(cin_p[:, f % 2, 3:3 + SEQ], k.ps[:, b, :])
                a.copy(cin_s[:, f % 2, :, 3:3 + DS], k.ps[:, b + 1, 0:NS].rearrange("p (b t) -> p b t", b=NB))
                a.copy(cin_s[:, f % 2, :, 0:3],
                       k.ps[:, b + 1, NS:NS + 24].rearrange("p (b t) -> p b t", b=NB)).then_inc(filled, 1)
                act.wait_ge(convolved, f + 1)
                if f < X_TILES:
                    if f >= 2:
                        act.wait_ge(turned, f - 1)
                    dst = out[:, f % 2, :]
                elif f < B_TILES:
                    dst = k.BT[:, f - X_TILES, :]
                else:
                    dst = k.CT[:, f - B_TILES, :]
                a.activation(dst, acc[:, f % 2, :], ACT.Silu, bias=k.conv_b_col[:, f:f + 1]).then_inc(activated, 1)

        @block.vector
        def _(dve):
            v = nc.vector
            own = Link(dve, dve_own)

            def convolve(f):
                dve.wait_ge(filled, f + 1)
                if f >= 2:
                    dve.wait_ge(activated, f - 1)
                    dve.wait_ge(turned, f - 1)
                ap = acc[:, f % 2, 0:SEQ]
                as_ = acc[:, f % 2, SEQ:T].rearrange("p (b t) -> p b t", b=NB)
                for w in range(CONV_W):
                    wc = k.conv_w_col[:, w * CT_TILES + f:w * CT_TILES + f + 1]
                    ip, is_ = cin_p[:, f % 2, w:w + SEQ], cin_s[:, f % 2, :, w:w + DS]
                    if w == 0:
                        v.tensor_scalar(ap, ip, wc, None, ALU.mult)
                        own(v.tensor_scalar(as_, is_, wc, None, ALU.mult))
                    else:
                        v.scalar_tensor_tensor(out=ap, in0=ip, scalar=wc, in1=ap, op0=ALU.mult, op1=ALU.add)
                        last = v.scalar_tensor_tensor(out=as_, in0=is_, scalar=wc, in1=as_, op0=ALU.mult, op1=ALU.add)
                        if w < CONV_W - 1:
                            own(last)
                last.then_inc(convolved, 1)
                v.tensor_copy(tail[:, f % 2, 0:3], cin_p[:, f % 2, SEQ:SEQ + 3])
                v.tensor_copy(tail[:, f % 2, 3:27].rearrange("p (b t) -> p b t", b=NB),
                              cin_s[:, f % 2, :, DS:DS + 3]).then_inc(tailed, 1)

            def gather(f):
                dve.wait_ge(turned, f + 1)
                b = 4 + bank(f)
                if f < B_TILES:
                    dst = k.xnat if f < X_TILES else k.Bnat
                    c = (f if f < X_TILES else f - X_TILES) * P
                    v.tensor_copy(dst[:, 0:4, c:c + P], k.ps[:, b, :].rearrange("p (t n) -> p t n", t=4))
                    v.tensor_copy(dst[0:NS, 4, c:c + P], k.ps[0:NS, b + 1, 0:P])
                v.tensor_copy(tails[:, f * P:f * P + P], k.ps[0:27, b + 1, P:2 * P]).then_inc(tail_turned, 1)

            for f in range(N + 1):
                if f < N:
                    convolve(f)
                if f:
                    gather(f - 1)


PIECES = 4
PIECE = KD // PIECES


def load_pieces(sp, dst, src, arrived):
    for j in range(PIECES):
        part = slice(PIECE * j, PIECE * j + PIECE)
        sp.dma_start(dst[:, part], src[:, part]).then_inc(arrived[j], 16)


def natural_projection(nc, k, name, blocks):
    with ExitStack() as ctx:
        sem = lambda n: ctx.enter_context(nc.semaphore(f"{name}_{n}"))
        NW, NBANK = 2, 4
        wbuf = ctx.enter_context(nc.sbuf_tensor(f"{name}_w", [P, NW, KD, 512], F32))
        w_in = [sem(f"w_in{i}") for i in range(NW)]
        first_in = [sem(f"first_in{j}") for j in range(PIECES)]
        projected, stored = sem("projected"), sem("stored")
        block = ctx.enter_context(nc.Block())

        @block.sync
        def _(sp):
            for i, (col, width, _, _) in enumerate(blocks):
                if i >= NW:
                    sp.wait_ge(projected, TILES * (i - NW + 1))
                if i == 0:
                    load_pieces(sp, wbuf[:, 0, :, 0:width], w_view(k.w_in, col, width), first_in)
                    continue
                sp.dma_start(wbuf[:, i % NW, :, 0:width], w_view(k.w_in, col, width)).then_inc(w_in[i % NW], 16)

        @block.tensor
        def _(pe):
            for i, (_, width, _, _) in enumerate(blocks):
                if i:
                    pe.wait_ge(w_in[i % NW], 16 * ((i - 1) // NW + 1 if i % NW else i // NW))
                for t in range(TILES):
                    n = TILES * i + t
                    if n >= NBANK:
                        pe.wait_ge(stored, n - NBANK + 1)
                    r = rows(t)
                    for kk in range(KD):
                        if n == 0 and kk % PIECE == 0:
                            pe.wait_ge(first_in[kk // PIECE], 16)
                        last = nc.tensor.matmul(k.ps[0:r, n % NBANK, 0:width], k.hT[:, kk, P * t:P * t + r],
                                                wbuf[:, i % NW, kk, 0:width], start=(kk == 0), stop=(kk == KD - 1))
                    last.then_inc(projected, 1)

        @block.scalar
        def _(act):
            for i, (_, width, dst, func) in enumerate(blocks):
                for t in range(TILES):
                    n = TILES * i + t
                    act.wait_ge(projected, n + 1)
                    nc.scalar.activation(dst(t), k.ps[0:rows(t), n % NBANK, 0:width], func).then_inc(stored, 1)


def stage_decays(nc, k):
    with ExitStack() as ctx:
        sb = lambda n, s, d=F32: ctx.enter_context(nc.sbuf_tensor(n, s, d))
        sem = lambda n: ctx.enter_context(nc.semaphore(n))
        shape = [P, TILES, HEADS]
        absx, u, lnw, zero, den = (sb(f"d_{n}", shape) for n in ("absx", "u", "lnw", "zero", "den"))
        abs_done, exp_done, plus_one, ln_done, step_done, summed, negated, exps, own_s = (
            sem(f"d_{n}") for n in ("abs", "exp", "plus_one", "ln", "step", "summed", "negated", "exps", "own"))
        block = ctx.enter_context(nc.Block())

        def each(row):
            return row[:].rearrange("p (a h) -> p a h", a=1).broadcast_to(shape)

        @block.vector
        def _(dve):
            v = nc.vector
            own = Link(dve, own_s)
            own(v.tensor_tensor(k.dt[:], k.dt[:], each(k.dt_bias_row), ALU.add))
            v.scalar_tensor_tensor(out=absx[:], in0=k.dt[:], scalar=-1.0, in1=k.dt[:], op0=ALU.mult,
                                   op1=ALU.max).then_inc(abs_done, 1)
            own(v.tensor_scalar(k.dt[:], k.dt[:], 0.0, None, ALU.max))
            dve.wait_ge(exp_done, 1)
            v.tensor_scalar(den[:], u[:], 1.0, None, ALU.add).then_inc(plus_one, 1)
            dve.wait_ge(ln_done, 1)
            own(v.tensor_scalar(den[:], den[:], -1.0, None, ALU.add))
            own(v.tensor_scalar(zero[:], den[:], 0.0, None, ALU.is_equal))
            own(v.tensor_tensor(den[:], den[:], zero[:], ALU.add))
            own(v.tensor_tensor(lnw[:], lnw[:], zero[:], ALU.add))
            own(v.reciprocal(den[:], den[:]))
            own(v.tensor_tensor(lnw[:], lnw[:], den[:], ALU.mult))
            own(v.tensor_tensor(lnw[:], lnw[:], u[:], ALU.mult))
            own(v.tensor_tensor(k.dt[:], k.dt[:], lnw[:], ALU.add))
            v.tensor_tensor(k.da[:], k.dt[:], each(k.a_row), ALU.mult).then_inc(step_done, 1)
            dve.wait_ge(summed, 1)
            for lo, hi, r in ((0, 4, P), (4, 5, NS)):
                a = k.ps[0:r, 0, lo * HEADS:hi * HEADS].rearrange("p (c h) -> p c h", h=HEADS)
                t = k.ps[0:r, 1, lo * HEADS:hi * HEADS].rearrange("p (c h) -> p c h", h=HEADS)
                own(v.tensor_scalar(k.nacum[0:r, lo:hi, :], a, -1.0, None, ALU.mult))
                v.tensor_tensor(k.to_end[0:r, lo:hi, :], t, k.nacum[0:r, lo:hi, :], ALU.add).then_inc(negated, 1)

        @block.tensor
        def _(pe):
            pe.wait_ge(step_done, 1)
            mm = nc.tensor.matmul
            for c in range(TILES):
                r = rows(c)
                cum, tot = (k.cum, k.ones) if c < 4 else (k.cum_s, k.same)
                mm(k.ps[0:r, 0, c * HEADS:c * HEADS + HEADS], cum[:], k.da[0:r, c, :], start=True, stop=True)
                mm(k.ps[0:r, 1, c * HEADS:c * HEADS + HEADS], tot[:], k.da[0:r, c, :], start=True, stop=True)
            for hh in range(HEADS):
                f, p0 = hh // 2, HP * (hh % 2)
                last = mm(k.ps[p0:p0 + HP, 2, f * NB:f * NB + NB], k.da[0:NS, 4, hh:hh + 1].broadcast_to([NS, HP]),
                          k.same[:, 0:NS:DS], start=True, stop=True)
            last.then_inc(summed, 1)

        @block.scalar
        def _(act):
            a = nc.scalar
            act.wait_ge(abs_done, 1)
            a.activation(u[:], absx[:], ACT.Exp, scale=-1.0).then_inc(exp_done, 1)
            act.wait_ge(plus_one, 1)
            a.activation(lnw[:], den[:], ACT.Ln).then_inc(ln_done, 1)
            act.wait_ge(summed, 1)
            act.wait_ge(negated, 2)
            for lo, hi, r in ((0, 4, P), (4, 5, NS)):
                acum = k.ps[0:r, 0, lo * HEADS:hi * HEADS].rearrange("p (c h) -> p c h", h=HEADS)
                a.activation(k.eacum[0:r, lo:hi, :], acum, ACT.Exp)
                a.activation(k.to_end[0:r, lo:hi, :], k.to_end[0:r, lo:hi, :], ACT.Exp)
            a.activation(k.cdec[:, 0:4, :], k.ps[:, 1, 0:4 * HEADS].rearrange("p (c h) -> p c h", h=HEADS), ACT.Exp)
            a.activation(k.tail_dec[:], k.ps[:, 2, 0:16 * NB].rearrange("p (f b) -> p f b", b=NB), ACT.Exp)


def by_head(col, r, n=8, width=HP):
    return col.rearrange("p (h a) -> p h a", a=1).broadcast_to([r, n, width])


def stage_sample_state(nc, k):
    with ExitStack() as ctx:
        sb = lambda n, s, d=F32: ctx.enter_context(nc.sbuf_tensor(n, s, d))
        sem = lambda n: ctx.enter_context(nc.semaphore("ss_" + n))
        NH0 = 3
        xde = sb("ss_xde", [NS, D_INNER])
        bsel = sb("ss_bsel", [NS, 2, GROUPS * STATE])
        h0 = sb("ss_h0", [P, NH0, 16, STATE])
        h0t = sb("ss_h0t", [P, 2, 4, P])
        h0_in = [sem(f"h0_in{i}") for i in range(NH0)]
        h0_out = [sem(f"h0_out{i}") for i in range(NH0)]
        xdt_done, xde_done, selected, turned, copied, read_out, contributed, updated = (
            sem(n) for n in ("xdt_done", "xde_done", "selected", "turned", "copied", "read_out", "contributed",
                             "updated"))
        block = ctx.enter_context(nc.Block())
        QUADS = 4 * NB

        def view(dram, b):
            return dram[0, b].rearrange("h p n -> (h p) n").rearrange("(f q) n -> q f n", q=P)

        @block.sync
        def _(sp):
            for b in range(NB):
                if b >= NH0:
                    sp.wait_ge(h0_out[b % NH0], 16 * (b // NH0))
                sp.dma_start(h0[:, b % NH0], view(k.state_ssm, b)).then_inc(h0_in[b % NH0], 16)
                if b >= 1:
                    sp.wait_ge(updated, 4 * b)
                    sp.dma_start(view(k.new_ssm_sample, b - 1), h0[:, (b - 1) % NH0]).then_inc(h0_out[(b - 1) % NH0], 16)
            sp.wait_ge(updated, 4 * NB)
            sp.dma_start(view(k.new_ssm_sample, NB - 1), h0[:, (NB - 1) % NH0]).then_inc(h0_out[(NB - 1) % NH0], 16)
            for i in range(NH0):
                sp.wait_ge(h0_out[i], 16 * len(range(i, NB, NH0)))

        @block.gpsimd
        def _(pool):
            g = nc.gpsimd
            x3 = k.xnat[0:NS, 4, :].rearrange("p (h q) -> p h q", q=HP)
            o3 = xde[:].rearrange("p (h q) -> p h q", q=HP)
            g.tensor_tensor(o3, x3, by_head(k.dt[0:NS, 4, :], NS, HEADS), ALU.mult).then_inc(xdt_done, 1)
            pool.wait_ge(xdt_done, 1)
            g.tensor_tensor(o3, o3, by_head(k.to_end[0:NS, 4, :], NS, HEADS), ALU.mult).then_inc(xde_done, 1)
            for b in range(NB):
                if b >= 2:
                    pool.wait_ge(contributed, 4 * (b - 1))
                g.tensor_scalar(bsel[:, b % 2, :], k.Bnat[0:NS, 4, :], k.same[:, DS * b:DS * b + 1], 1.0,
                                ALU.mult, ALU.mult).then_inc(selected, 1)

        @block.tensor
        def _(pe):
            mm = nc.tensor.matmul

            def turn(q):
                b, j = q // 4, q % 4
                if j == 0:
                    pe.wait_ge(h0_in[b % NH0], 16 * (b // NH0 + 1))
                if q >= 2:
                    pe.wait_ge(copied, q - 1)
                for i in range(4):
                    last = nc.tensor.transpose(k.ps[:, q % 2, i * P:i * P + P], h0[:, b % NH0, 4 * j + i, :], k.ident[:])
                last.then_inc(turned, 1)

            def use(q):
                b, j = q // 4, q % 4
                if q == 0:
                    pe.wait_ge(xde_done, 1)
                if j == 0:
                    pe.wait_ge(selected, b + 1)
                if q >= 2:
                    pe.wait_ge(updated, q - 1)
                for i in range(4):
                    f = 4 * j + i
                    last = mm(k.ps[:, 2 + q % 2, i * P:i * P + P], xde[:, f * P:f * P + P],
                              bsel[:, b % 2, j * STATE:j * STATE + STATE], start=True, stop=True)
                last.then_inc(contributed, 1)
                pe.wait_ge(copied, q + 1)
                for i in range(4):
                    f = 4 * j + i
                    c = f * NS + b * DS
                    last = mm(k.ps[:, 4 + c // 512, c % 512:c % 512 + DS], h0t[:, q % 2, i, :],
                              k.CT[:, j, SEQ + DS * b:SEQ + DS * b + DS], start=True, stop=True)
                last.then_inc(read_out, 1)

            for q in range(QUADS + 1):
                if q < QUADS:
                    turn(q)
                if q:
                    use(q - 1)

        @block.scalar
        def _(act):
            for q in range(QUADS):
                act.wait_ge(turned, q + 1)
                if q >= 2:
                    act.wait_ge(read_out, q - 1)
                nc.scalar.copy(h0t[:, q % 2], k.ps[:, q % 2, :].rearrange("p (i n) -> p i n", i=4)).then_inc(copied, 1)
            act.wait_ge(read_out, QUADS)
            for i in range(2):
                last = nc.scalar.copy(k.yt[:, 8 * i:8 * i + 8, :], k.ps[:, 4 + i, :].rearrange("p (f n) -> p f n", f=8))
            last.then_inc(copied, 1)

        @block.vector
        def _(dve):
            for q in range(QUADS):
                b, j = q // 4, q % 4
                dve.wait_ge(contributed, q + 1)
                dve.wait_ge(turned, q + 1)
                for i in range(4):
                    f = 4 * j + i
                    hh = h0[:, b % NH0, f, :]
                    last = nc.vector.scalar_tensor_tensor(out=hh, in0=hh, scalar=k.tail_dec[:, f, b:b + 1],
                                                          in1=k.ps[:, 2 + q % 2, i * P:i * P + P], op0=ALU.mult,
                                                          op1=ALU.add)
                last.then_inc(updated, 1)


def stage_ssd(nc, k):
    with ExitStack() as ctx:
        sb = lambda n, s, d=F32: ctx.enter_context(nc.sbuf_tensor(n, s, d))
        sem = lambda n: ctx.enter_context(nc.semaphore("s_" + n))
        xdt, xde, dx, y = (sb("s_" + n, [P, 2, 512]) for n in ("xdt", "xde", "dx", "y"))
        MT = sb("s_MT", [P, 4, 4, P])
        h = sb("s_h", [P, D_INNER])
        hout = sb("s_hout", [P, 16, STATE])
        junk = sb("s_junk", [P, 512])
        (scored, decayed, exped, weighted, diag, offs, states, xdt_done, xde_done, dx_done, y_done, updated, own_s,
         h_turned, h_copied, h_stored, squared) = (
            sem(n) for n in ("scored", "decayed", "exped", "weighted", "diag", "offs", "states", "xdt_done",
                             "xde_done", "dx_done", "y_done", "updated", "own", "h_turned", "h_copied", "h_stored",
                             "squared"))
        block = ctx.enter_context(nc.Block())
        U = TILES * GROUPS
        HG = HEADS // GROUPS

        @block.gpsimd
        def _(pool):
            g = nc.gpsimd
            for u in range(U):
                c, gr = u // GROUPS, u % GROUPS
                r = rows(c)
                x3 = k.xnat[0:r, c, gr * 512:gr * 512 + 512].rearrange("p (h q) -> p h q", q=HP)
                hs = slice(gr * HG, gr * HG + HG)
                v3 = lambda a: a[0:r, u % 2, :].rearrange("p (h q) -> p h q", q=HP)
                if u >= 2:
                    pool.wait_ge(diag, u - 1)
                    pool.wait_ge(states, min(u - 1, 16))
                    pool.wait_ge(y_done, u - 1)
                g.tensor_tensor(v3(xdt), x3, by_head(k.dt[0:r, c, hs], r), ALU.mult).then_inc(xdt_done, 1)
                g.tensor_tensor(v3(dx), x3, by_head(k.dskip_row[0:r, hs], r), ALU.mult).then_inc(dx_done, 1)
                if c < 4:
                    pool.wait_ge(xdt_done, u + 1)
                    g.tensor_tensor(v3(xde), v3(xdt), by_head(k.to_end[0:r, c, hs], r), ALU.mult).then_inc(xde_done, 1)

        @block.tensor
        def _(pe):
            mm = nc.tensor.matmul

            def scores(u):
                c, gr = u // GROUPS, u % GROUPS
                r = rows(c)
                tok = slice(P * c, P * c + r)
                if u >= 2:
                    pe.wait_ge(weighted, 2 * (u - 1))
                mm(k.ps[0:r, 7 * (u % 2), 0:r], k.BT[:, gr, tok], k.CT[:, gr, tok], start=True,
                   stop=True).then_inc(scored, 1)
                later, cum = (k.later, k.cum) if c < 4 else (k.later_s, k.cum_s)
                for i in range(2):
                    q = 2 * u + i
                    if q >= 2:
                        pe.wait_ge(exped, q - 1)
                    bank = k.ps[0:r, 1 + q % 2, 0:4 * r].rearrange("p (h l) -> p h l", h=4)
                    mm(bank, k.identb[0:r, 0:r], later[0:r, 0:r].rearrange("p (a l) -> p a l", a=1).broadcast_to([r, 4, r]),
                       start=True, stop=False, skip_group_check=True)
                    for j in range(4):
                        hh = gr * HG + 4 * i + j
                        last = mm(bank[:, j, :], k.da[0:r, c, hh:hh + 1].broadcast_to([r, r]), cum[0:r, 0:r],
                                  start=False, stop=(j == 3), skip_group_check=True)
                    last.then_inc(decayed, 1)

            def within(u):
                c = u // GROUPS
                r = rows(c)
                pe.wait_ge(weighted, 2 * u + 2)
                pe.wait_ge(xdt_done, u + 1)
                if u:
                    pe.wait_ge(y_done, u)
                for j in range(HG):
                    last = mm(k.ps[0:r, 3, j * HP:j * HP + HP], MT[0:r, (2 * u + j // 4) % 4, j % 4, 0:r],
                              xdt[0:r, u % 2, j * HP:j * HP + HP], start=True, stop=True)
                last.then_inc(diag, 1)

            def from_state(u):
                c, gr = u // GROUPS, u % GROUPS
                cols = slice(gr * 512, gr * 512 + 512)
                if 0 < c < 4:
                    pe.wait_ge(updated, u - GROUPS + 1)
                    mm(k.ps[:, 4, :], k.CT[:, gr, P * c:P * c + P], h[:, cols], start=True, stop=True).then_inc(offs, 1)
                if c == 4:
                    for i in range(4):
                        last = nc.tensor.transpose(k.ps[0:NS, 4, i * P:i * P + P], k.yt[:, 4 * gr + i, :], k.ident[:])
                    last.then_inc(offs, 1)
                if c < 4:
                    pe.wait_ge(xde_done, u + 1)
                    if u:
                        pe.wait_ge(updated, u)
                    mm(k.ps[:, 5, :], k.Bnat[:, c, gr * STATE:gr * STATE + STATE], xde[:, u % 2, :], start=True,
                       stop=True).then_inc(states, 1)

            for u in range(U + 1):
                if u < U:
                    scores(u)
                if u:
                    within(u - 1)
                    from_state(u - 1)
            pe.wait_ge(updated, 16)
            for q in range(4):
                if q >= 2:
                    pe.wait_ge(h_copied, q - 1)
                for i in range(4):
                    f = 4 * q + i
                    last = nc.tensor.transpose(k.ps[:, 5 + q % 2, i * P:i * P + P], h[:, f * P:f * P + P], k.ident[:])
                last.then_inc(h_turned, 1)

        def sum_squares(act, a, u):
            c, gr = u // GROUPS, u % GROUPS
            r = rows(c)
            act.wait_ge(y_done, u + 1)
            if u:
                act.wait_ge(squared, u)
            a.activation(junk[0:r, :], k.znat[0:r, c, gr * 512:gr * 512 + 512], ACT.Square,
                         accum_out=k.ysq[0:r, c, gr:gr + 1]).then_inc(squared, 1)

        @block.scalar
        def _(act):
            a = nc.scalar
            for u in range(U):
                c, gr = u // GROUPS, u % GROUPS
                r = rows(c)
                for i in range(2):
                    q = 2 * u + i
                    act.wait_ge(decayed, q + 1)
                    if q >= 4:
                        act.wait_ge(diag, (q - 4) // 2 + 1)
                    for j in range(4):
                        hh = gr * HG + 4 * i + j
                        last = a.activation(MT[0:r, q % 4, j, 0:r], k.ps[0:r, 1 + q % 2, j * r:j * r + r], ACT.Exp,
                                            bias=k.nacum[0:r, c, hh:hh + 1])
                    last.then_inc(exped, 1)
                if u:
                    sum_squares(act, a, u - 1)
            sum_squares(act, a, U - 1)
            for q in range(4):
                act.wait_ge(h_turned, q + 1)
                a.copy(hout[:, 4 * q:4 * q + 4, :], k.ps[:, 5 + q % 2, :].rearrange("p (i n) -> p i n", i=4)).then_inc(h_copied, 1)

        @block.vector
        def _(dve):
            v = nc.vector
            own = Link(dve, own_s)

            def weigh(u):
                r = rows(u // GROUPS)
                dve.wait_ge(scored, u + 1)
                s = k.ps[0:r, 7 * (u % 2), 0:r].rearrange("p (a l) -> p a l", a=1).broadcast_to([r, 4, r])
                for i in range(2):
                    q = 2 * u + i
                    dve.wait_ge(exped, q + 1)
                    m = MT[0:r, q % 4, :, 0:r]
                    v.tensor_tensor(m, m, s, ALU.mult).then_inc(weighted, 1)

            def finish(u):
                c, gr = u // GROUPS, u % GROUPS
                r = rows(c)
                hs = slice(gr * HG, gr * HG + HG)
                yy = y[0:r, u % 2, :]
                dve.wait_ge(diag, u + 1)
                dve.wait_ge(dx_done, u + 1)
                own(v.tensor_tensor(yy, k.ps[0:r, 3, :], dx[0:r, u % 2, :], ALU.add))
                if c > 0:
                    dve.wait_ge(offs, u - GROUPS + 1)
                    d3 = dx[0:r, u % 2, :]
                    own(v.tensor_tensor(d3.rearrange("p (h q) -> p h q", q=HP),
                                        k.ps[0:r, 4, :].rearrange("p (h q) -> p h q", q=HP),
                                        by_head(k.eacum[0:r, c, hs], r), ALU.mult))
                    own(v.tensor_tensor(yy, yy, d3, ALU.add))
                z = k.znat[0:r, c, gr * 512:gr * 512 + 512]
                v.tensor_tensor(z, z, yy, ALU.mult).then_inc(y_done, 1)
                if c < 4:
                    dve.wait_ge(states, u + 1)
                    hh = h[:, gr * 512:gr * 512 + 512]
                    if c == 0:
                        v.tensor_copy(hh, k.ps[:, 5, :]).then_inc(updated, 1)
                    else:
                        dve.wait_ge(offs, u - GROUPS + 1)
                        h3 = hh.rearrange("p (h q) -> p h q", q=HP)
                        own(v.tensor_tensor(h3, h3, by_head(k.cdec[:, c, hs], P), ALU.mult))
                        v.tensor_tensor(hh, hh, k.ps[:, 5, :], ALU.add).then_inc(updated, 1)

            for u in range(U + 1):
                if u < U:
                    weigh(u)
                if u:
                    finish(u - 1)

        @block.sync
        def _(sp):
            sp.wait_ge(h_copied, 4)
            sp.dma_start(k.new_ssm_prompt[0, 0].rearrange("h p n -> (h p) n").rearrange("(f q) n -> q f n", q=P),
                         hout[:]).then_inc(h_stored, 16)
            sp.wait_ge(h_stored, 16)


def stage_gate(nc, k):
    with ExitStack() as ctx:
        sb = lambda n, s, d=F32: ctx.enter_context(nc.sbuf_tensor(n, s, d))
        sem = lambda n: ctx.enter_context(nc.semaphore("g_" + n))
        ms = sb("g_ms", [P, TILES])
        rstd = sb("g_rstd", [P, TILES])
        mean_done, rooted, scaled, turned, stored, own_s = (
            sem(n) for n in ("mean", "rooted", "scaled", "turned", "stored", "own"))
        block = ctx.enter_context(nc.Block())

        def store(eng, n, done):
            t, q = n // 4, n % 4
            r = rows(t)
            for i in range(4):
                f = 4 * q + i
                src = k.ps[:, n % 4, i * P:i * P + r]
                col = k.ssm_norm_col[:, f:f + 1]
                if eng is nc.scalar:
                    last = eng.activation(yT(k, t)[:, f, :], src, ACT.Copy, scale=col)
                else:
                    last = eng.tensor_scalar(yT(k, t)[:, f, :], src, col, None, ALU.mult)
            last.then_inc(done, 1)

        @block.vector
        def _(dve):
            v = nc.vector
            own = Link(dve, own_s)
            for c, r in ((slice(0, 4), P), (slice(4, 5), NS)):
                own(v.tensor_reduce(ms[0:r, c], k.ysq[0:r, c, :], AX.X, ALU.add))
                v.tensor_scalar(ms[0:r, c], ms[0:r, c], 1.0 / D_INNER, EPS, ALU.mult, ALU.add).then_inc(mean_done, 1)
            dve.wait_ge(rooted, 2)
            own(v.reciprocal(rstd[:, 0:4], rstd[:, 0:4]))
            own(v.reciprocal(rstd[0:NS, 4:5], rstd[0:NS, 4:5]))
            for t in range(TILES):
                r = rows(t)
                v.tensor_scalar(k.znat[0:r, t, :], k.znat[0:r, t, :], rstd[0:r, t:t + 1], None,
                                ALU.mult).then_inc(scaled, 1)
                for q in range(4):
                    n = 4 * t + q
                    if q % 2 == 0:
                        dve.wait_ge(turned, n + 1)
                        store(v, n, stored)

        stored_act = ctx.enter_context(nc.semaphore("g_stored_act"))

        @block.scalar
        def _(act):
            act.wait_ge(mean_done, 2)
            nc.scalar.activation(rstd[:, 0:4], ms[:, 0:4], ACT.Sqrt).then_inc(rooted, 1)
            nc.scalar.activation(rstd[0:NS, 4:5], ms[0:NS, 4:5], ACT.Sqrt).then_inc(rooted, 1)
            for n in range(1, 4 * TILES, 2):
                act.wait_ge(turned, n + 1)
                store(nc.scalar, n, stored_act)

        @block.tensor
        def _(pe):
            for n in range(4 * TILES):
                t, q = n // 4, n % 4
                r = rows(t)
                pe.wait_ge(scaled, t + 1)
                if n >= 4:
                    pe.wait_ge(stored if n % 2 == 0 else stored_act, (n - 4) // 2 + 1)
                for i in range(4):
                    f = 4 * q + i
                    last = nc.tensor.transpose(k.ps[:, n % 4, i * P:i * P + r], k.znat[0:r, t, f * P:f * P + P],
                                               k.ident[0:r, 0:r])
                last.then_inc(turned, 1)


def stage_branch(nc, k, name, gate_col, w, depth, load_w, src_p, src_s, accumulate):
    with ExitStack() as ctx:
        sb = lambda n, s, d=F32: ctx.enter_context(nc.sbuf_tensor(f"{name}_{n}", s, d))
        sem = lambda n: ctx.enter_context(nc.semaphore(f"{name}_{n}"))
        NW, WB = 2, 256
        wg = sb("wg", [P, NW, KD, WB])
        wp = sb("wp", [P, NW, depth, WB])
        sig = sb("sig", [P, 2, T])
        prod = sb("prod", [P, 2, T])
        wg_in, wp_in = ([sem(f"{n}_in{i}") for i in range(NW)] for n in ("wg", "wp"))
        projected, sigmoids, merged, own_s = (sem(n) for n in ("projected", "sigmoids", "merged", "own"))
        block = ctx.enter_context(nc.Block())
        per = WB // P
        n_loads = len(load_w(wp[:, 0], w, 0, WB))

        @block.sync
        def _(sp):
            for i in range(KD // per):
                if i >= NW:
                    sp.wait_ge(projected, per * (i - NW + 1))
                s = i % NW
                sp.dma_start(wg[:, s], w_view(k.w_in, gate_col + WB * i, WB)).then_inc(wg_in[s], 16)
                for dst, src in load_w(wp[:, s], w, WB * i, WB):
                    sp.dma_start(dst, src).then_inc(wp_in[s], 16)

        @block.tensor
        def _(pe):
            mm = nc.tensor.matmul
            for m in range(KD):
                s, c, b = (m // per) % NW, (m % per) * P, 3 * (m % 2)
                pe.wait_ge(wg_in[s], 16 * (m // per // NW + 1))
                if m >= 2:
                    pe.wait_ge(merged, m - 1)
                for f in range(KD):
                    mm(k.ps[:, b, :], wg[:, s, f, c:c + P], k.hT[:, f, 0:SEQ], start=(f == 0), stop=(f == KD - 1))
                for f in range(KD):
                    last = mm(k.ps[:, b + 2, 0:NS], wg[:, s, f, c:c + P], k.hT[:, f, SEQ:T], start=(f == 0),
                              stop=(f == KD - 1))
                pe.wait_ge(wp_in[s], 16 * n_loads * (m // per // NW + 1))
                for f in range(depth):
                    mm(k.ps[:, b + 1, :], wp[:, s, f, c:c + P], src_p(f), start=(f == 0), stop=(f == depth - 1))
                for f in range(depth):
                    last = mm(k.ps[:, b + 2, NS:2 * NS], wp[:, s, f, c:c + P], src_s(f), start=(f == 0),
                              stop=(f == depth - 1))
                last.then_inc(projected, 1)

        @block.scalar
        def _(act):
            for m in range(KD):
                b = 3 * (m % 2)
                act.wait_ge(projected, m + 1)
                if m >= 2:
                    act.wait_ge(merged, m - 1)
                nc.scalar.activation(sig[:, m % 2, 0:SEQ], k.ps[:, b, :], ACT.Sigmoid)
                nc.scalar.activation(sig[:, m % 2, SEQ:T], k.ps[:, b + 2, 0:NS], ACT.Sigmoid).then_inc(sigmoids, 1)

        @block.vector
        def _(dve):
            v = nc.vector
            own = Link(dve, own_s)
            for m in range(KD):
                b = 3 * (m % 2)
                dve.wait_ge(sigmoids, m + 1)
                dst = prod[:, m % 2, :] if accumulate else k.mT[:, m, :]
                v.tensor_tensor(dst[:, 0:SEQ], sig[:, m % 2, 0:SEQ], k.ps[:, b + 1, :], ALU.mult)
                last = v.tensor_tensor(dst[:, SEQ:T], sig[:, m % 2, SEQ:T], k.ps[:, b + 2, NS:2 * NS], ALU.mult)
                if accumulate:
                    own(last)
                    last = v.tensor_tensor(k.mT[:, m, :], k.mT[:, m, :], dst, ALU.add)
                last.then_inc(merged, 1)


def load_rows(dst, w, c0, n):
    return [(dst, w_view(w, c0, n))]


def load_head_rows(dst, w, c0, n):
    return [(dst[HD * g:HD * g + HD], w[:, c0:c0 + n].rearrange("(g j d) n -> g d j n", g=KVH, d=HD)[g])
            for g in range(KVH)]


def stage_qk(nc, k):
    with ExitStack() as ctx:
        sem = lambda n: ctx.enter_context(nc.semaphore("q_" + n))
        NW = 4
        wbuf = ctx.enter_context(nc.sbuf_tensor("q_w", [P, NW, KD, KVH, HD], F32))
        w_in = [sem(f"w_in{i}") for i in range(NW)]
        projected, stored = sem("projected"), sem("stored")
        block = ctx.enter_context(nc.Block())

        def q_cols(j):
            return lambda g: COL_Q + (g * HPK + j) * HD

        def k_cols(branch):
            return lambda g: COL_KV + branch * KVW + g * 2 * HD
        jobs = [(q_cols(j), k.qT[:, j, :], SCALE) for j in range(HPK)]
        jobs += [(k_cols(1), k.ksT[:], 1.0), (k_cols(2), k.kwT[:], 1.0)]

        @block.sync
        def _(sp):
            for i, (cols, _, _) in enumerate(jobs):
                if i >= NW:
                    sp.wait_ge(projected, i - NW + 1)
                for g in range(KVH):
                    sp.dma_start(wbuf[:, i % NW, :, g, :], w_view(k.w_in, cols(g), HD)).then_inc(w_in[i % NW], 16)

        @block.tensor
        def _(pe):
            for i in range(len(jobs)):
                s, b = i % NW, 2 * (i % 4)
                pe.wait_ge(w_in[s], 32 * (i // NW + 1))
                if i >= 4:
                    pe.wait_ge(stored, i - 3)
                for bank, cols in ((k.ps[:, b, :], slice(0, SEQ)), (k.ps[:, b + 1, 0:NS], slice(SEQ, T))):
                    for f in range(KD):
                        last = nc.tensor.matmul(bank, wbuf[:, s, f].rearrange("p g d -> p (g d)"), k.hT[:, f, cols],
                                                start=(f == 0), stop=(f == KD - 1))
                last.then_inc(projected, 1)

        @block.scalar
        def _(act):
            for i, (_, dst, scale) in enumerate(jobs):
                b = 2 * (i % 4)
                act.wait_ge(projected, i + 1)
                nc.scalar.activation(dst[:, 0:SEQ], k.ps[:, b, :], ACT.Copy, scale=scale)
                nc.scalar.activation(dst[:, SEQ:T], k.ps[:, b + 1, 0:NS], ACT.Copy, scale=scale).then_inc(stored, 1)


def v_of(kv, branch, g):
    c = branch * KVW + g * 2 * HD + HD
    return kv[..., c:c + HD]


def stage_cmp_prompt(nc, k):
    with ExitStack() as ctx:
        sb = lambda n, s, d=F32: ctx.enter_context(nc.sbuf_tensor("cp_" + n, s, d))
        sem = lambda n: ctx.enter_context(nc.semaphore("cp_" + n))
        N = NCMP_P
        ind = sb("ind", [P, 4, AH, N])
        seen = sb("seen", [P, 4, N])
        unseen = sb("unseen", [P, 4, N])
        own_head = sb("own_head", [P, HPK, KVH])
        kcT = sb("kcT", [P, N])
        vrep = sb("vrep", [P, P])
        vblk = sb("vblk", [P, HPK, KVH, HD])
        s = sb("s", [P, 4, AH, N])
        m = sb("m", [P, 4, AH])
        den = sb("den", [P, 4, AH])
        pT = sb("pT", [P, 4, P])
        consts, means, mean_copied, scored, weighed, turned, turned_copied, out_done, stored, own_s, pool_s, exped, shifted = (
            sem(n) for n in ("consts", "means", "mean_copied", "scored", "weighed", "turned", "turned_copied",
                             "out_done", "stored", "own", "pool", "exped", "shifted"))
        written = sem("written")
        block = ctx.enter_context(nc.Block())

        @block.sync
        def _(sp):
            for br, (p_out, s_out) in enumerate(((k.new_cmp_kv_prompt, k.new_cmp_kv_sample),
                                                 (k.new_sel_kv_prompt, k.new_sel_kv_sample),
                                                 (k.new_win_kv_prompt, None))):
                cols = slice(br * KVW, br * KVW + KVW)
                sp.dma_start(p_out[0, 0].rearrange("(t p) g c d -> p t (g c d)", p=P), k.kv[:, 0:4, cols]).then_inc(written, 16)
                if s_out is not None:
                    sp.dma_start(s_out[0].rearrange("b t g c d -> (b t) (g c d)"), k.kv[0:NS, 4, cols]).then_inc(written, 16)
            win = k.new_win_kv_sample[0].rearrange("b t g c d -> b t (g c d)")
            old = k.cache_win_kv[0].rearrange("b t g c d -> b t (g c d)")
            for b in range(NB):
                sp.dma_start(win[b, WINDOW - DS:WINDOW], k.kv[DS * b:DS * b + DS, 4, 2 * KVW:3 * KVW]).then_inc(written, 16)
            sp.dma_start(win[:, 0:WINDOW - DS], old[:, DS:WINDOW]).then_inc(written, 16)
            sp.dma_start(k.gates_dram, k.gates[0:NS, 4, :]).then_inc(written, 16)
            sp.wait_ge(written, 16 * (5 + NB + 2))

        @block.gpsimd
        def _(pool):
            g = nc.gpsimd
            own = Link(pool, pool_s)
            own(g.memset(ind[:], 1.0 / CMP))
            pat = [[P, 4], [0, AH], [-CMP, N]]
            own(g.affine_select(out=ind[:], in_=ind[:], compare_op=ALU.is_ge, fill=0.0, base=0, pattern=pat,
                                channel_multiplier=1))
            own(g.affine_select(out=ind[:], in_=ind[:], compare_op=ALU.is_ge, fill=0.0, base=CMP - 1,
                                pattern=[[-P, 4], [0, AH], [CMP, N]], channel_multiplier=-1))
            own(g.memset(seen[:], 1.0))
            own(g.affine_select(out=seen[:], in_=seen[:], compare_op=ALU.is_ge, fill=0.0, base=-(CMP - 1),
                                pattern=[[P, 4], [-CMP, N]], channel_multiplier=1))
            own(g.tensor_scalar(unseen[:], seen[:], -NEG, NEG, ALU.mult, ALU.add))
            own(g.memset(own_head[:], 1.0))
            own(g.affine_select(out=own_head[:], in_=own_head[:], compare_op=ALU.is_ge, fill=0.0, base=0,
                                pattern=[[-N, HPK], [-N * HPK, KVH]], channel_multiplier=1))
            g.affine_select(out=own_head[:], in_=own_head[:], compare_op=ALU.is_ge, fill=0.0, base=N - 1,
                            pattern=[[N, HPK], [N * HPK, KVH]], channel_multiplier=-1).then_inc(consts, 1)

        @block.tensor
        def _(pe):
            mm = nc.tensor.matmul
            pe.wait_ge(consts, 1)
            for g in range(KVH):
                for t in range(4):
                    mm(k.ps[HD * g:HD * g + HD, g, 0:N], k.kv[:, t, 2 * HD * g:2 * HD * g + HD], ind[:, t, 0, :],
                       start=(t == 0), stop=(t == 3))
            for t in range(4):
                last = mm(k.ps[:, 2, 0:P], ind[:, t].rearrange("p h n -> p (h n)"),
                          k.kv[:, t, 0:KVW].rearrange("p (g c d) -> p g c d", g=KVH, c=2)[:, :, 1, :],
                          start=(t == 0), stop=(t == 3))
            last.then_inc(means, 1)
            pe.wait_ge(mean_copied, 1)
            for t in range(4):
                if t >= 2:
                    pe.wait_ge(shifted, t - 1)
                for j in range(HPK):
                    for g in range(KVH):
                        hh = g * HPK + j
                        last = mm(k.ps[:, 3 + 2 * (t % 2) + g, hh * N:hh * N + N], k.qT[HD * g:HD * g + HD, j, P * t:P * t + P],
                                  kcT[HD * g:HD * g + HD, :], start=True, stop=True)
                last.then_inc(scored, 1)
            for t in range(4):
                pe.wait_ge(weighed, t + 1)
                if t >= 1:
                    pe.wait_ge(turned_copied, t)
                nc.tensor.transpose(k.ps[:, 0, 0:P], s[:, t].rearrange("p h n -> p (h n)"), k.ident[:]).then_inc(turned, 1)
                pe.wait_ge(turned_copied, t + 1)
                if t >= 1:
                    pe.wait_ge(stored, t)
                for i in range(2):
                    last = mm(k.ps[:, 1 + i, :], pT[:, t, :], vblk[:].rearrange("p j g d -> p (j g d)")[:, 512 * i:512 * i + 512],
                              start=True, stop=True)
                last.then_inc(out_done, 1)

        @block.scalar
        def _(act):
            for t in range(4):
                act.wait_ge(shifted, t + 1)
                nc.scalar.activation(s[:, t], s[:, t], ACT.Exp).then_inc(exped, 1)

        @block.vector
        def _(dve):
            v = nc.vector
            own = Link(dve, own_s)
            dve.wait_ge(means, 1)
            v.tensor_copy(kcT[0:HD, :], k.ps[0:HD, 0, 0:N])
            v.tensor_copy(kcT[HD:P, :], k.ps[HD:P, 1, 0:N])
            own(v.tensor_copy(vrep[:], k.ps[:, 2, 0:P]))
            for j in range(HPK):
                last = v.tensor_tensor(vblk[:, j], vrep[:].rearrange("p (g d) -> p g d", g=KVH),
                                       own_head[:, j, :].rearrange("p (g a) -> p g a", a=1).broadcast_to([P, KVH, HD]),
                                       ALU.mult)
            last.then_inc(mean_copied, 1)
            three = [P, AH, N]
            wide = lambda a: a.rearrange("p (h a) -> p h a", a=1).broadcast_to(three)
            over = lambda a: a.rearrange("p (a n) -> p a n", a=1).broadcast_to([P, HPK, N])
            for t in range(4):
                dve.wait_ge(scored, t + 1)
                for g in range(KVH):
                    own(v.tensor_tensor(s[:, t, HPK * g:HPK * g + HPK, :],
                                        k.ps[:, 3 + 2 * (t % 2) + g, g * HPK * N:(g + 1) * HPK * N].rearrange("p (h n) -> p h n", n=N),
                                        over(unseen[:, t, :]), ALU.add))
                own(v.tensor_reduce(m[:, t, :], s[:, t], AX.X, ALU.max))
                v.tensor_tensor(s[:, t], s[:, t], wide(m[:, t, :]), ALU.subtract).then_inc(shifted, 1)
            for t in range(4):
                dve.wait_ge(exped, t + 1)
                for g in range(KVH):
                    half = s[:, t, HPK * g:HPK * g + HPK, :]
                    own(v.tensor_tensor(half, half, over(seen[:, t, :]), ALU.mult))
                own(v.tensor_reduce(den[:, t, :], s[:, t], AX.X, ALU.add))
                own(v.tensor_scalar(den[:, t, :], den[:, t, :], 1e-30, None, ALU.max))
                own(v.reciprocal(den[:, t, :], den[:, t, :]))
                own(v.tensor_tensor(den[:, t, :], den[:, t, :], k.gates[:, t, 0:3 * AH:3], ALU.mult))
                v.tensor_tensor(s[:, t], s[:, t], wide(den[:, t, :]), ALU.mult).then_inc(weighed, 1)
            for t in range(4):
                dve.wait_ge(turned, t + 1)
                v.tensor_copy(pT[:, t, :], k.ps[:, 0, 0:P]).then_inc(turned_copied, 1)
                dve.wait_ge(out_done, t + 1)
                for i in range(2):
                    last = v.tensor_copy(k.onat[:, t, 512 * i:512 * i + 512], k.ps[:, 1 + i, :])
                last.then_inc(stored, 1)


def stage_attn_prompt(nc, k):
    with ExitStack() as ctx:
        sb = lambda n, s, d=F32: ctx.enter_context(nc.sbuf_tensor("ap_" + n, s, d))
        sem = lambda n: ctx.enter_context(nc.semaphore("ap_" + n))
        NPB = 3
        pbuf = sb("p", [P, NPB, SEQ])
        pT = sb("pT", [P, 2, SEQ])
        nmax = sb("nmax", [P, 4 * 2 * AH])
        ssum = sb("ssum", [P, 4 * 2 * AH])
        wgt = sb("wgt", [P, 4, HPK])
        o = sb("o", [P, 2, 512])
        NQ = NPAGES // 4
        ind = sb("ind", [P, NQ, 32])
        AHEAD = 2
        page_in = [sem("page_in0"), sem("page_in1")]
        scored, maxed, exped, turned, copied, valued, weighted, added, filled, emptied, own_s = (
            sem(n) for n in ("scored", "maxed", "exped", "turned", "copied", "valued", "weighted", "added", "filled",
                             "emptied", "own"))
        table_in, meant, ind_set, ind_done, passed, passed_pool = (
            sem(n) for n in ("table_in", "meant", "ind_set", "ind_done", "passed", "passed_pool"))
        block = ctx.enter_context(nc.Block())
        units = [(t, br, g, j) for t in range(4) for br in (1, 2) for g in range(KVH) for j in range(HPK)]
        U = len(units)
        bank7 = [(24, "mean", 0), (38, "mean", 1), (46, "turn", 0), (50, "turn", 1), (52, "mean", 2), (62, "mean", 3),
                 (71, "mean", 4), (78, "turn", 2), (80, "mean", 5), (83, "turn", 3), (89, "mean", 6), (97, "mean", 7),
                 (110, "turn", 4), (114, "turn", 5), (U + 1, "turn", 6), (U + 1, "turn", 7)]

        def load_samples(eng, half, passed):
            eng.wait_ge(table_in, 16)
            with eng.Fori(0, NB // 2) as pair:
                hold(eng, meant, pair * 2 + half - 1 + AHEAD, passed)
                load_pages(eng, k, k.cache_cmp_kv, half, pair * 2 + half, page_in[half])
            eng.wait_ge(meant, NB - 1 + half + AHEAD)
            load_pages(eng, k, k.cache_sel_kv, half, half, k.page_in[half])

        @block.sync
        def _(sp):
            sp.sem_inc(meant, AHEAD)
            sp.dma_start(k.page_row[:], k.page_table.rearrange("b n -> (b n)").rearrange("(a n) -> a n", a=1)).then_inc(table_in, 16)
            load_samples(sp, 0, passed)

        @block.gpsimd
        def _(pool):
            own = Link(pool, ind_set)
            own(nc.gpsimd.memset(ind[:], 1.0 / CMP))
            own(nc.gpsimd.affine_select(out=ind[:], in_=ind[:], compare_op=ALU.is_ge, fill=0.0, base=0,
                                        pattern=[[P, NQ], [-CMP, 32]], channel_multiplier=1))
            nc.gpsimd.affine_select(out=ind[:], in_=ind[:], compare_op=ALU.is_ge, fill=0.0, base=CMP - 1,
                                    pattern=[[-P, NQ], [CMP, 32]], channel_multiplier=-1).then_inc(ind_done, 1)
            load_samples(pool, 1, passed_pool)

        @block.tensor
        def _(pe):
            mm = nc.tensor.matmul

            def score(u):
                t, br, g, j = units[u]
                kT = k.ksT if br == 1 else k.kwT
                part = slice(HD * g, HD * g + HD)
                if u >= 3:
                    pe.wait_ge(exped, u - 2)
                n = P * (t + 1)
                mm(k.ps[:, u % 3, 0:n], k.qT[part, j, P * t:P * t + P], kT[part, 0:n], start=True, stop=False,
                   skip_group_check=True)
                mm(k.ps[:, u % 3, n - P:n], k.identb[:], k.causal[:], start=False, stop=True,
                   skip_group_check=True).then_inc(scored, 1)

            def turn(u):
                t = units[u][0]
                pe.wait_ge(exped, u + 1)
                if u >= 2:
                    pe.wait_ge(copied, u - 1)
                for kt in range(t + 1):
                    last = nc.tensor.transpose(k.ps[:, 3 + u % 2, kt * P:kt * P + P], pbuf[:, u % NPB, kt * P:kt * P + P],
                                               k.ident[:])
                last.then_inc(turned, 1)

            def value(u):
                t, br, g, j = units[u]
                pe.wait_ge(copied, u + 1)
                gr = u // HPK
                if j == 0 and gr >= 2:
                    pe.wait_ge(weighted, gr - 1)
                for kt in range(t + 1):
                    last = mm(k.ps[:, 5 + gr % 2, j * HD:j * HD + HD], pT[:, u % 2, kt * P:kt * P + P],
                              v_of(k.kv[:, kt, :], br, g), start=(kt == 0), stop=(kt == t))
                last.then_inc(valued, 1)

            def turn_out(n):
                t, i = n // 2, n % 2
                pe.wait_ge(added, 4 * t + 4)
                for j in range(4):
                    last = nc.tensor.transpose(k.ps[:, 7, j * P:j * P + P],
                                               k.onat[:, t, (4 * i + j) * P:(4 * i + j) * P + P], k.ident[:])
                last.then_inc(filled, 1)

            def average(b):
                pe.wait_ge(page_in[b % 2], 16 * NPAGES * (b // 2 + 1))
                if b == 0:
                    pe.wait_ge(ind_done, 1)
                for i in range(NQ):
                    for c in range(4):
                        last = mm(k.ps[32 * c:32 * c + 32, 7, 0:KVW], ind[:, i, :], k.pages[:, b % 2, NQ * c + i, :],
                                  start=(i == 0), stop=(i == NQ - 1))
                last.then_inc(filled, 1)

            for i in range(U + 2):
                if i < U:
                    score(i)
                if 1 <= i <= U:
                    turn(i - 1)
                if i >= 2:
                    value(i - 2)
                for n, (at, what, which) in enumerate(bank7):
                    if at == i:
                        if n:
                            pe.wait_ge(emptied, n)
                        (turn_out if what == "turn" else average)(which)

        @block.vector
        def _(dve):
            v = nc.vector
            own = Link(dve, own_s)

            def top(u):
                n = P * (units[u][0] + 1)
                dve.wait_ge(scored, u + 1)
                v.tensor_reduce(nmax[:, u:u + 1], k.ps[:, u % 3, 0:n], AX.X, ALU.max, negate=True).then_inc(maxed, 1)

            def copy(u):
                n = P * (units[u][0] + 1)
                dve.wait_ge(turned, u + 1)
                if u >= 2:
                    dve.wait_ge(valued, u - 1)
                v.tensor_copy(pT[:, u % 2, 0:n], k.ps[:, 3 + u % 2, 0:n]).then_inc(copied, 1)

            def weigh(gr):
                t, br, g, _ = units[gr * HPK]
                w = wgt[:, gr % 4, :]
                own(v.reciprocal(w, ssum[:, gr * HPK:gr * HPK + HPK]))
                own(v.tensor_tensor(w, w, k.gates[:, t, 3 * HPK * g + br:3 * HPK * (g + 1):3], ALU.mult))
                dve.wait_ge(valued, HPK * (gr + 1))
                oo = o[:, gr % 2, :].rearrange("p (j d) -> p j d", d=HD)
                v.tensor_tensor(oo, k.ps[:, 5 + gr % 2, :].rearrange("p (j d) -> p j d", d=HD), by_head(w, P),
                                ALU.mult).then_inc(weighted, 1)
                dve.wait_ge(weighted, gr + 1)
                dst = k.onat[:, t, :].rearrange("p (j g d) -> p j g d", g=KVH, d=HD)[:, :, g, :]
                if gr:
                    dve.wait_ge(added, gr)
                v.tensor_tensor(dst, dst, oo, ALU.add).then_inc(added, 1)

            for i in range(U + 4):
                if i < U:
                    top(i)
                if 1 <= i <= U:
                    copy(i - 1)
                if i >= 4 and (i - 4) % HPK == HPK - 1:
                    weigh((i - 4) // HPK)

        @block.scalar
        def _(act):
            def empty(n):
                _, what, which = bank7[n]
                act.wait_ge(filled, n + 1)
                if what == "turn":
                    t, i = which // 2, which % 2
                    nc.scalar.copy(k.oT[:, 4 * i:4 * i + 4, P * t:P * t + P],
                                   k.ps[:, 7, :].rearrange("p (j n) -> p j n", j=4)).then_inc(emptied, 1)
                else:
                    act.sem_inc(meant, 1)
                    nc.scalar.copy(k.means[:, which, :], k.ps[:, 7, 0:KVW]).then_inc(emptied, 1)

            for u in range(U):
                n = P * (units[u][0] + 1)
                act.wait_ge(maxed, u + 1)
                if u >= NPB:
                    act.wait_ge(turned, u - NPB + 1)
                nc.scalar.activation(pbuf[:, u % NPB, 0:n], k.ps[:, u % 3, 0:n], ACT.Exp, bias=nmax[:, u:u + 1],
                                     accum_out=ssum[:, u:u + 1]).then_inc(exped, 1)
                for n7, (at, _, _) in enumerate(bank7):
                    if at == u + 1:
                        empty(n7)
            for n7, (at, _, _) in enumerate(bank7):
                if at > U:
                    empty(n7)


def hold(eng, sem, value, passed):
    eng.wait_ge(sem, value)
    eng.sem_inc(passed, 1)


def page_buf(k, n):
    return k.pages[:, n] if n < 2 else k.onat[:].rearrange("p a b -> p (a b)").rearrange("p (i c) -> p i c", c=KVW)


def load_pages(sp, k, cache, buf, sample, page_in):
    rows_of = cache[0].rearrange("n p g c d -> n p (g c d)")
    with sp.Fori(0, NPAGES) as pg:
        page = sp.value_load(k.page_row[0:1, bass.ds(pg + sample * NPAGES, 1)], min_val=0, max_val=rows_of.shape[0] - 1)
        sp.dma_start(page_buf(k, buf)[:, bass.ds(pg, 1), :], rows_of[bass.ds(page, 1)].rearrange("a p c -> p a c")).then_inc(
            page_in, 16)


def stage_cmp_sample(nc, k):
    with ExitStack() as ctx:
        sb = lambda n, s, d=F32: ctx.enter_context(nc.sbuf_tensor("cs_" + n, s, d))
        sem = lambda n: ctx.enter_context(nc.semaphore("cs_" + n))
        N = NCMP_S
        kmean = sb("kmean", [P, NB, P])
        kcT = sb("kcT", [P, NB, N])
        wide_p = sb("wide_p", [P, NB, P])
        s = sb("s", [P, NB, N])
        m = sb("m", [P, NB])
        den = sb("den", [P, NB])
        pick = sb("pick", [P, NB, NSEL])
        force = sb("force", [P, NSEL])
        top = sb("top", [P, NB, 8])
        pT = sb("pT", [P, NB, P])
        group = sb("group", [P, 16, 8])
        gate_in, consts, pool_s, own_s, packed, turned, turned_copied, scored, exped, shifted = (
            sem(n) for n in ("gate_in", "consts", "pool", "own", "packed", "turned", "turned_copied", "scored", "exped",
                             "shifted"))
        weighed, imported, p_turned, p_copied, valued, qb_done = (
            sem(n) for n in ("weighed", "imported", "p_turned", "p_copied", "valued", "qb_done"))
        block = ctx.enter_context(nc.Block())

        @block.sync
        def _(sp):
            gates = k.gates_dram.rearrange("(b t) (h c) -> t h b c", t=DS, c=3)
            for g in range(KVH):
                for t in range(DS):
                    r0 = (g * DS + t) * HPK
                    sp.dma_start(k.grow[r0:r0 + HPK], gates[t, g * HPK:(g + 1) * HPK]).then_inc(gate_in, 16)
            load_pages(sp, k, k.cache_sel_kv, 2, 2, k.page_in[2])

        @block.gpsimd
        def _(pool):
            g = nc.gpsimd
            own = Link(pool, pool_s)
            own(g.memset(wide_p[:], 0.0))
            own(g.memset(group[:], 1.0))
            own(g.affine_select(out=group[:], in_=group[:], compare_op=ALU.is_ge, fill=0.0, base=0,
                                pattern=[[-8, 16], [0, 8]], channel_multiplier=1))
            own(g.affine_select(out=group[:], in_=group[:], compare_op=ALU.is_ge, fill=0.0, base=7,
                                pattern=[[8, 16], [0, 8]], channel_multiplier=-1))
            own(g.memset(force[:], 0.0))
            own(g.memset(force[:, 0:1], 1000.0))
            own(g.memset(force[:, NSEL - 2:NSEL], 1000.0))
            own(g.memset(k.step_mask[:], 0.0))
            own(g.memset(k.old_mask[:], 0.0))
            own(g.memset(k.new_mask[:], NEG))
            for lo in (0, HD):
                half = slice(lo, lo + HD)
                own(g.affine_select(out=k.step_mask[half], in_=k.step_mask[half], compare_op=ALU.is_ge, fill=NEG,
                                    base=0, pattern=[[-HPK, DS]], channel_multiplier=1))
                own(g.affine_select(out=k.old_mask[half], in_=k.old_mask[half], compare_op=ALU.is_ge, fill=NEG,
                                    base=HPK - 1, pattern=[[HPK, DS]], channel_multiplier=-1))
            for b in range(NB):
                own(g.tensor_copy(k.new_mask[:, b, DS * b:DS * b + DS], k.step_mask[:]))
            g.memset(k.qb[:], 0.0).then_inc(consts, 1)

        @block.tensor
        def _(pe):
            mm = nc.tensor.matmul
            pe.wait_ge(packed, 1)
            for b in range(NB):
                last = nc.tensor.transpose(k.ps[:, 2 + b // 4, (b % 4) * P:(b % 4) * P + P], kmean[:, b], k.ident[:])
                if b % 4 == 3:
                    last.then_inc(turned, 1)
            pe.wait_ge(consts, 1)
            pe.wait_ge(qb_done, 1)
            for b in range(NB):
                pe.wait_ge(turned_copied, b // 4 + 1)
                last = mm(k.ps[:, 4, b * N:b * N + N], k.qb[:, b], kcT[:, b, :], start=True, stop=True)
            last.then_inc(scored, 1)
            pe.wait_ge(weighed, 1)
            mm(k.ps[:, 5, 0:NB * N], group[:].rearrange("p a c -> p (a c)"), s[:].rearrange("p b n -> p (b n)"),
               start=True, stop=True).then_inc(imported, 1)
            pe.wait_ge(weighed, 2)
            for b in range(NB):
                last = nc.tensor.transpose(k.ps[:, 6 + b // 4, (b % 4) * P:(b % 4) * P + P], wide_p[:, b, :], k.ident[:])
            last.then_inc(p_turned, 1)
            pe.wait_ge(p_copied, 1)
            for b in range(NB):
                last = mm(k.ps[:, b // 4, (b % 4) * P:(b % 4) * P + P], pT[:, b, :],
                          k.means[:, b, :].rearrange("p (g c d) -> p g c d", g=KVH, c=2)[:, :, 1, :], start=True, stop=True)
            last.then_inc(valued, 1)

        @block.scalar
        def _(act):
            for i in range(2):
                act.wait_ge(turned, i + 1)
                nc.scalar.copy(kcT[:, 4 * i:4 * i + 4, :].rearrange("p b (c n) -> p b c n", c=4),
                               k.ps[:, 2 + i, :].rearrange("p (b c n) -> p b c n", b=4, c=4)[:, :, :, 0:8]).then_inc(
                    turned_copied, 1)
            act.wait_ge(shifted, 1)
            nc.scalar.activation(s[:], s[:], ACT.Exp).then_inc(exped, 1)

        @block.vector
        def _(dve):
            v = nc.vector
            own = Link(dve, own_s)
            for g in range(KVH):
                last = v.tensor_copy(kmean[:, :, HD * g:HD * g + HD], k.means[:, :, 2 * HD * g:2 * HD * g + HD])
            last.then_inc(packed, 1)
            dve.wait_ge(consts, 1)
            for g in range(KVH):
                part = slice(HD * g, HD * g + HD)
                for b in range(NB):
                    last = v.tensor_copy(k.qb[part, b].rearrange("p (g t j) -> p g t j", g=KVH, t=DS)[:, g],
                                         k.qT[part, :, SEQ + DS * b:SEQ + DS * b + DS].rearrange("p j t -> p t j"))
            last.then_inc(qb_done, 1)
            dve.wait_ge(scored, 1)
            sc = k.ps[:, 4, 0:NB * N].rearrange("p (b n) -> p b n", n=N)
            wide = lambda a: a.rearrange("p (b a) -> p b a", a=1).broadcast_to([P, NB, N])
            own(v.tensor_reduce(m[:], sc, AX.X, ALU.max))
            v.tensor_tensor(s[:], sc, wide(m[:]), ALU.subtract).then_inc(shifted, 1)
            dve.wait_ge(exped, 1)
            own(v.tensor_reduce(den[:], s[:], AX.X, ALU.add))
            own(v.reciprocal(den[:], den[:]))
            v.tensor_tensor(s[:], s[:], wide(den[:]), ALU.mult).then_inc(weighed, 1)
            dve.wait_ge(imported, 1)
            dve.wait_ge(gate_in, 16 * DS * KVH)
            gate = k.grow[:, :, 0].rearrange("p (b a) -> p b a", a=1).broadcast_to([P, NB, 8])
            for c in range(4):
                last = v.tensor_tensor(wide_p[:, :, 32 * c:32 * c + 8], s[:, :, 8 * c:8 * c + 8], gate, ALU.mult)
            last.then_inc(weighed, 1)
            over = force[:, 0:N].rearrange("p (a n) -> p a n", a=1).broadcast_to([P, NB, N])
            last_force = force[:, N:NSEL].rearrange("p (a n) -> p a n", a=1).broadcast_to([P, NB, 1])
            v.tensor_copy(pick[:, :, N:NSEL], last_force)
            own(v.tensor_tensor(pick[:, :, 0:N], k.ps[:, 5, 0:NB * N].rearrange("p (b n) -> p b n", n=N), over, ALU.add))
            for _ in range(TOPK // 8):
                for b in range(NB):
                    last = v.max(top[:, b, :], pick[:, b, :])
                own(last)
                for b in range(NB):
                    last = v.match_replace(out=pick[:, b, :], in_to_replace=top[:, b, :], in_values=pick[:, b, :],
                                           imm_value=NEG)
                own(last)
            own(v.tensor_scalar(k.sel_bias[:], pick[:], 0.1 * NEG, NEG, ALU.is_gt, ALU.mult))
            dve.wait_ge(p_turned, 1)
            for i in range(2):
                last = v.tensor_copy(pT[:, 4 * i:4 * i + 4, :], k.ps[:, 6 + i, :].rearrange("n (b p) -> n b p", b=4))
            last.then_inc(p_copied, 1)
            dve.wait_ge(valued, 1)
            for i in range(2):
                last = v.tensor_copy(k.acc[:, 4 * i:4 * i + 4, :], k.ps[:, i, :].rearrange("p (b c) -> p b c", b=4))
            own(last)


def stage_attn_sample(nc, k):
    with ExitStack() as ctx:
        sb = lambda n, s, d=F32: ctx.enter_context(nc.sbuf_tensor("as_" + n, s, d))
        sem = lambda n: ctx.enter_context(nc.semaphore("as_" + n))
        WPAGES = WINDOW // PAGE
        wpages = sb("wpages", [P, 2, WPAGES, KVW])
        kT = sb("kT", [P, 2, PAST])
        s = sb("s", [P, 2, PAST + NS])
        pT = k.qT[:].rearrange("p j n -> p (j n)")[:, 0:(NPAGES + 1) * P].rearrange("p (i n) -> p i n", n=P)
        nmax = sb("nmax", [P, 2 * NB])
        ssum = sb("ssum", [P, 2 * NB])
        wgt = sb("wgt", [P, 2 * NB])
        page_in = k.page_in
        wpage_in = [sem("wpage_in0"), sem("wpage_in1")]
        turned, k_copied, p_copied, scored, masked, maxed, exped, valued, added, own_s, acc_turned, stored, p_turned = (
            sem(n) for n in ("turned", "k_copied", "p_copied", "scored", "masked", "maxed", "exped", "valued", "added",
                             "own", "acc_turned", "stored", "p_turned"))
        block = ctx.enter_context(nc.Block())
        U = 2 * NB
        npg = lambda u: NPAGES if u % 2 == 0 else WPAGES

        def page(u, i):
            return page_buf(k, (u // 2) % 3)[:, i, :] if u % 2 == 0 else wpages[:, (u // 2) % 2, i, :]

        steps = [("keys", 0), ("scores", 0)]
        for u in range(0, U, 2):
            later = u + 2 < U
            steps += [("keys", u + 1), ("scores", u + 1)] + [("keys", u + 2)] * later
            steps += [("values", u), ("values", u + 1)] + [("scores", u + 2)] * later
        turns, index = [], {}
        for what, u in steps:
            todo = {"keys": [("k", u, i) for i in range(npg(u) // 4)], "scores": [],
                    "values": [("p", u, i) for i in range(npg(u) // 4 + 1)]}[what]
            for job in todo:
                index[job] = len(turns)
                turns.append(job)
        copies_before = lambda kind, n: sum(1 for j in turns[:n + 1] if j[0] == kind)

        def load_selected(eng, b):
            eng.wait_ge(valued, 2 * (b - 3) + 1)
            load_pages(eng, k, k.cache_sel_kv, b % 3, b, page_in[b % 3])

        @block.gpsimd
        def _(pool):
            for b in range(4, NB, 3):
                load_selected(pool, b)

        @block.sync
        def _(sp):
            old = k.cache_win_kv[0].rearrange("b (i p) g c d -> b p i (g c d)", p=P)

            for b in range(NB):
                if b >= 3 and b % 3 != 1:
                    load_selected(sp, b)
                if b >= 2:
                    sp.wait_ge(valued, 2 * (b - 2) + 2)
                sp.dma_start(wpages[:, b % 2], old[b]).then_inc(wpage_in[b % 2], 16)

        @block.tensor
        def _(pe):
            mm = nc.tensor.matmul

            def bank_free(n):
                if n >= 2:
                    kind = turns[n - 2][0]
                    pe.wait_ge(k_copied if kind == "k" else p_copied, copies_before(kind, n - 2))

            def keys(u):
                b = u // 2
                if u % 2 == 0:
                    pe.wait_ge(page_in[b % 3], 16 * NPAGES * (b // 3 + 1))
                else:
                    pe.wait_ge(wpage_in[b % 2], 16 * (b // 2 + 1))
                for i in range(npg(u) // 4):
                    n = index["k", u, i]
                    bank_free(n)
                    for q in range(4):
                        for g in range(KVH):
                            last = mm(k.ps[HD * g:HD * g + HD, n % 2, q * P:q * P + P],
                                      page(u, 4 * i + q)[:, 2 * HD * g:2 * HD * g + HD], k.ident[:], start=True, stop=True)
                    last.then_inc(turned, 1)

            def scores(u):
                b = u // 2
                if u:
                    pe.wait_ge(masked, u)
                for i in range(npg(u) // 4):
                    pe.wait_ge(k_copied, copies_before("k", index["k", u, i]))
                    mm(k.ps[:, 2 + i, :], k.qb[:, b], kT[:, u % 2, 512 * i:512 * i + 512], start=True, stop=True)
                new = k.ksT if u % 2 == 0 else k.kwT
                mm(k.ps[:, 6, 0:NS], k.qb[:, b], new[:, SEQ:T], start=True, stop=True).then_inc(scored, 1)

            def values(u):
                pe.wait_ge(exped, u + 1)
                for i in range(npg(u) // 4 + 1):
                    n = index["p", u, i]
                    bank_free(n)
                    if i < npg(u) // 4:
                        for q in range(4):
                            c = (4 * i + q) * P
                            last = nc.tensor.transpose(k.ps[:, n % 2, q * P:q * P + P], s[:, u % 2, c:c + P], k.ident[:])
                    else:
                        c = npg(u) * P
                        last = nc.tensor.transpose(k.ps[0:NS, n % 2, 0:P], s[:, u % 2, c:c + NS], k.ident[:])
                    last.then_inc(p_turned, 1)
                if u:
                    pe.wait_ge(added, u)
                for i in range(npg(u)):
                    if i % 4 == 0:
                        pe.wait_ge(p_copied, copies_before("p", index["p", u, i // 4]))
                    mm(k.ps[:, 7, 0:P], pT[:, i, :], page(u, i).rearrange("p (g c d) -> p g c d", g=KVH, c=2)[:, :, 1, :],
                       start=(i == 0), stop=False)
                pe.wait_ge(p_copied, copies_before("p", index["p", u, npg(u) // 4]))
                cols = slice((1 + u % 2) * KVW, (2 + u % 2) * KVW)
                mm(k.ps[:, 7, 0:P], pT[0:NS, NPAGES, :],
                   k.kv[0:NS, 4, cols].rearrange("p (g c d) -> p g c d", g=KVH, c=2)[:, :, 1, :], start=False,
                   stop=True).then_inc(valued, 1)

            for what, u in steps:
                if what == "keys":
                    keys(u)
                elif what == "scores":
                    scores(u)
                else:
                    values(u)
            pe.wait_ge(added, U)
            for i in range(2):
                for q in range(4):
                    last = nc.tensor.transpose(k.ps[:, 2 + i, q * P:q * P + P], k.acc[:, 4 * i + q, :], k.ident[:])
                last.then_inc(acc_turned, 1)

        @block.scalar
        def _(act):
            def copy_keys(u):
                for i in range(npg(u) // 4):
                    n = index["k", u, i]
                    act.wait_ge(turned, copies_before("k", n))
                    if u >= 2 and i == 0:
                        act.wait_ge(scored, u - 1)
                    nc.scalar.copy(kT[:, u % 2, 512 * i:512 * i + 512], k.ps[:, n % 2, :]).then_inc(k_copied, 1)

            def weights(u):
                w = npg(u) * P + NS
                act.wait_ge(maxed, u + 1)
                nc.scalar.activation(s[:, u % 2, 0:w], s[:, u % 2, 0:w], ACT.Exp, bias=nmax[:, u:u + 1],
                                     accum_out=ssum[:, u:u + 1]).then_inc(exped, 1)

            copy_keys(0)
            for u in range(0, U, 2):
                copy_keys(u + 1)
                if u + 2 < U:
                    copy_keys(u + 2)
                weights(u)
                weights(u + 1)

        @block.vector
        def _(dve):
            v = nc.vector
            own = Link(dve, own_s)

            def mask(u):
                b, n = u // 2, npg(u) * P
                dve.wait_ge(scored, u + 1)
                if u >= 2:
                    dve.wait_ge(valued, u - 1)
                for i in range(npg(u) // 4):
                    dst, src = s[:, u % 2, 512 * i:512 * i + 512], k.ps[:, 2 + i, :]
                    if u % 2 == 0:
                        v.tensor_tensor(dst.rearrange("p (n c) -> p n c", c=CMP), src.rearrange("p (n c) -> p n c", c=CMP),
                                        by_head(k.sel_bias[:, b, 8 * i:8 * i + 8], P, 8, CMP), ALU.add)
                    else:
                        v.tensor_tensor(dst[:, 0:DS], src[:, 0:DS], k.old_mask[:], ALU.add)
                        v.tensor_copy(dst[:, DS:], src[:, DS:])
                new = s[:, u % 2, n:n + NS]
                if u % 2 == 0:
                    last = v.scalar_tensor_tensor(out=new, in0=k.ps[:, 6, 0:NS], scalar=k.sel_bias[:, b, N_PAST:NSEL],
                                                  in1=k.new_mask[:, b, :], op0=ALU.add, op1=ALU.add)
                else:
                    last = v.tensor_tensor(new, k.ps[:, 6, 0:NS], k.new_mask[:, b, :], ALU.add)
                last.then_inc(masked, 1)
                dve.wait_ge(masked, u + 1)
                v.tensor_reduce(nmax[:, u:u + 1], s[:, u % 2, 0:n + NS], AX.X, ALU.max, negate=True).then_inc(maxed, 1)

            N_PAST = NCMP_S
            np_ = [0]

            def finish(u):
                b = u // 2
                for i in range(npg(u) // 4 + 1):
                    n = index["p", u, i]
                    np_[0] += 1
                    dve.wait_ge(p_turned, np_[0])
                    if u and i == 0:
                        dve.wait_ge(valued, u)
                    if i < npg(u) // 4:
                        v.tensor_copy(pT[:, 4 * i:4 * i + 4, :],
                                      k.ps[:, n % 2, :].rearrange("p (q c) -> p q c", q=4)).then_inc(p_copied, 1)
                    else:
                        v.tensor_copy(pT[0:NS, NPAGES, :], k.ps[0:NS, n % 2, 0:P]).then_inc(p_copied, 1)
                own(v.reciprocal(wgt[:, u:u + 1], ssum[:, u:u + 1]))
                own(v.tensor_tensor(wgt[:, u:u + 1], wgt[:, u:u + 1], k.grow[:, b, 1 + u % 2:2 + u % 2], ALU.mult))
                dve.wait_ge(valued, u + 1)
                if u:
                    dve.wait_ge(added, u)
                v.scalar_tensor_tensor(out=k.acc[:, b, :], in0=k.ps[:, 7, 0:P], scalar=wgt[:, u:u + 1],
                                       in1=k.acc[:, b, :], op0=ALU.mult, op1=ALU.add).then_inc(added, 1)

            mask(0)
            for u in range(0, U, 2):
                mask(u + 1)
                finish(u)
                finish(u + 1)
                if u + 2 < U:
                    mask(u + 2)
            for i in range(2):
                dve.wait_ge(acc_turned, i + 1)
                for q in range(4):
                    b = 4 * i + q
                    for g in range(KVH):
                        part = slice(HD * g, HD * g + HD)
                        c = q * P + g * NS
                        v.tensor_copy(k.oT[part, :, SEQ + DS * b:SEQ + DS * b + DS].rearrange("p j t -> p t j"),
                                      k.ps[part, 2 + i, c:c + NS].rearrange("p (t j) -> p t j", t=DS))
            v.tensor_copy(wgt[:, 0:1], ssum[:, 0:1]).then_inc(stored, 1)
            dve.wait_ge(stored, 1)


def stage_out(nc, k):
    with ExitStack() as ctx:
        sb = lambda n, s, d=F32: ctx.enter_context(nc.sbuf_tensor("o_" + n, s, d))
        sem = lambda n: ctx.enter_context(nc.semaphore("o_" + n))
        w = sb("w", [P, 2, KD, 512])
        x = sb("x", [P, TILES, D])
        h = sb("h", [P, TILES, D])
        rest = sb("rest", [P, TILES, D])
        part = sb("part", [P, 3, TILES, D], BF16)
        junk = sb("junk", [P, D])
        row = sb("row", [P, D])
        ss, mean, root, rstd = (sb(n, [P, TILES]) for n in ("ss", "mean", "root", "rstd"))
        first_in, w_in = [sem(f"first_in{j}") for j in range(PIECES)], sem("w_in")
        x_in = [sem(f"x_in{t}") for t in range(TILES)]
        row_in, projected, added, squared, averaged, rooted, normed, turned, copied, cast, left, parted, own_s, written = (
            sem(n) for n in ("row_in", "projected", "added", "squared", "averaged", "rooted", "normed", "turned",
                             "copied", "cast", "left", "parted", "own", "written"))
        block = ctx.enter_context(nc.Block())

        @block.sync
        def _(sp):
            load_pieces(sp, w[:, 0], w_view(k.w_out, 0, 512), first_in)
            sp.dma_start(w[:, 1], w_view(k.w_out, 512, 512)).then_inc(w_in, 16)
            for t in range(TILES):
                src = k.x_prompt[0, P * t:P * t + P, :] if t < 4 else k.x_sample.rearrange("b s d -> (b s) d")
                sp.dma_start(x[0:rows(t), t, :], src).then_inc(x_in[t], 16)
            sp.dma_start(row[:], k.norm_ffn_w.partition_broadcast(P)[:, 0, :]).then_inc(row_in, 16)
            for t in range(TILES):
                r = rows(t)
                sp.wait_ge(added, t + 1)
                sp.dma_start(k.x1_dram[P * t:P * t + r], x[0:r, t]).then_inc(written, 16)
            for t in range(TILES):
                r = rows(t)
                sp.wait_ge(parted, t + 1)
                sp.dma_start(k.parts_dram[:, P * t:P * t + r].rearrange("c p d -> p c d"), part[0:r, :, t]).then_inc(written, 16)
            sp.wait_ge(written, 32 * TILES)

        @block.tensor
        def _(pe):
            def project(t):
                r = rows(t)
                if t >= 2:
                    pe.wait_ge(added, t - 1)
                for i in range(2):
                    if t == 0 and i == 1:
                        pe.wait_ge(w_in, 16)
                    for f in range(KD):
                        if t == 0 and i == 0 and f % PIECE == 0:
                            pe.wait_ge(first_in[f // PIECE], 16)
                        last = nc.tensor.matmul(k.ps[0:r, 2 * (t % 2) + i, :], k.mT[:, f, P * t:P * t + r], w[:, i, f, :],
                                                start=(f == 0), stop=(f == KD - 1))
                last.then_inc(projected, 1)

            def turn(t):
                r = rows(t)
                pe.wait_ge(normed, t + 1)
                if t >= 2:
                    pe.wait_ge(copied, t - 1)
                for f in range(KD):
                    b, o = 4 + 2 * (t % 2) + f // 4, (f % 4) * P
                    last = nc.tensor.transpose(k.ps[:, b, o:o + r], h[0:r, t, f * P:f * P + P], k.ident[0:r, 0:r])
                last.then_inc(turned, 1)

            for t in range(TILES + 1):
                if t < TILES:
                    project(t)
                if t:
                    turn(t - 1)

        @block.scalar
        def _(act):
            def copy(t):
                r = rows(t)
                act.wait_ge(turned, t + 1)
                for i in range(2):
                    src = k.ps[:, 4 + 2 * (t % 2) + i, :].rearrange("p (f n) -> p f n", f=4)[:, :, 0:r]
                    last = nc.scalar.copy(k.hT[:, 4 * i:4 * i + 4, P * t:P * t + r], src)
                last.then_inc(copied, 1)

            for t in range(TILES):
                r = rows(t)
                act.wait_ge(added, t + 1)
                if t:
                    act.wait_ge(squared, t)
                nc.scalar.activation(junk[0:r], x[0:r, t], ACT.Square, accum_out=ss[0:r, t:t + 1]).then_inc(squared, 1)
                act.wait_ge(averaged, t + 1)
                nc.scalar.activation(root[0:r, t:t + 1], mean[0:r, t:t + 1], ACT.Sqrt).then_inc(rooted, 1)
                act.wait_ge(normed, t + 1)
                nc.scalar.copy(part[0:r, 0, t], h[0:r, t]).then_inc(cast, 1)
                act.wait_ge(left, 2 * t + 1)
                nc.scalar.copy(part[0:r, 1, t], rest[0:r, t]).then_inc(cast, 1)
                if t:
                    copy(t - 1)
                act.wait_ge(left, 2 * t + 2)
                nc.scalar.copy(part[0:r, 2, t], rest[0:r, t]).then_inc(parted, 1)
            copy(TILES - 1)

        @block.vector
        def _(dve):
            v = nc.vector
            own = Link(dve, own_s)
            dve.wait_ge(row_in, 16)
            for t in range(TILES):
                r = rows(t)
                dve.wait_ge(projected, t + 1)
                dve.wait_ge(x_in[t], 16)
                for i in range(2):
                    xx = x[0:r, t, 512 * i:512 * i + 512]
                    last = v.tensor_tensor(xx, xx, k.ps[0:r, 2 * (t % 2) + i, :], ALU.add)
                last.then_inc(added, 1)
                dve.wait_ge(squared, t + 1)
                v.tensor_scalar(mean[0:r, t:t + 1], ss[0:r, t:t + 1], 1.0 / D, EPS, ALU.mult, ALU.add).then_inc(averaged, 1)
                dve.wait_ge(rooted, t + 1)
                own(v.reciprocal(rstd[0:r, t:t + 1], root[0:r, t:t + 1]))
                v.scalar_tensor_tensor(out=h[0:r, t], in0=x[0:r, t], scalar=rstd[0:r, t:t + 1], in1=row[0:r],
                                       op0=ALU.mult, op1=ALU.mult).then_inc(normed, 1)
                for i, from_ in ((0, h), (1, rest)):
                    dve.wait_ge(cast, 2 * t + i + 1)
                    v.tensor_tensor(rest[0:r, t], from_[0:r, t], part[0:r, i, t], ALU.subtract).then_inc(left, 1)


class LoopLink:

    def __init__(self, eng, sem, it, per_body, passed):
        self.eng, self.sem, self.it, self.per_body, self.passed, self.n = eng, sem, it, per_body, passed, 0

    def __call__(self, ins):
        self.n += 1
        ins.then_inc(self.sem, 1)
        hold(self.eng, self.sem, self.it * self.per_body + self.n, self.passed)


def top16(v, own, values, tops, ats):
    n = len(values)
    for e in range(2):
        part = slice(8 * e, 8 * e + 8)
        for j in range(n):
            last = v.max(tops[j][:, part], values[j])
        own(last)
        for j in range(n):
            last = v.max_index(ats[j][:, part], tops[j][:, part], values[j])
        own(last)
        if e == 0:
            for j in range(n):
                last = v.match_replace(out=values[j], in_to_replace=tops[j][:, part], in_values=values[j], imm_value=NEG)
            own(last)


def rank_halves(v, own, k, scores):
    top16(v, own, scores, [k.top[:, c] for c in range(2)], [k.at[:, c] for c in range(2)])


def rank_sums(v, own, k, h):
    first = k.top[:, 0].rearrange("p (i a) -> p i a", a=1).broadcast_to([P, TOPK, TOPK])
    second = k.top[:, 1].rearrange("p (a j) -> p a j", a=1).broadcast_to([P, TOPK, TOPK])
    own(v.tensor_tensor(k.cand[:].rearrange("p (i j) -> p i j", i=TOPK), first, second, ALU.add))
    top16(v, own, [k.cand[:]], [k.best[:, h]], [k.pos[:]])


def name_experts(v, own, k, h):
    v.tensor_copy(k.atf[:], k.at[:])
    v.tensor_scalar(k.half[:, 0], k.pos[:], 4, None, ALU.logical_shift_right)
    own(v.tensor_scalar(k.half[:, 1], k.pos[:], TOPK - 1, None, ALU.bitwise_and))
    own(v.tensor_copy(k.halff[:], k.half[:]))
    for c in range(2):
        one = k.halff[:, c].rearrange("p (i a) -> p i a", a=1).broadcast_to([P, TOPK, TOPK])
        io = k.iotaf[:].rearrange("p (a j) -> p a j", a=1).broadcast_to([P, TOPK, TOPK])
        last = v.tensor_tensor(k.hit[:, c], one, io, ALU.is_equal)
    own(last)
    for c in range(2):
        where = k.atf[:, c].rearrange("p (a j) -> p a j", a=1).broadcast_to([P, TOPK, TOPK])
        last = v.tensor_tensor(k.hit[:, c], k.hit[:, c], where, ALU.mult)
    own(last)
    own(v.tensor_reduce(k.pick[:], k.hit[:], AX.X, ALU.add))
    own(v.scalar_tensor_tensor(out=k.expert[:, h, :], in0=k.pick[:, 0], scalar=float(PKEYS), in1=k.pick[:, 1],
                               op0=ALU.mult, op1=ALU.add))


def wide_den(k):
    return k.den[:].rearrange("p (h a) -> p h a", a=1).broadcast_to([P, PH, TOPK])


def shift_best(v, own, k):
    own(v.tensor_copy(k.den[:], k.best[:, :, 0:1].rearrange("p h a -> p (h a)")))
    return v.tensor_tensor(k.best[:], k.best[:], wide_den(k), ALU.subtract)


def share_best(v, own, k):
    own(v.tensor_reduce(k.den[:], k.best[:], AX.X, ALU.add))
    own(v.reciprocal(k.den[:], k.den[:]))
    return v.tensor_tensor(k.best[:], k.best[:], wide_den(k), ALU.mult)


def turn_routes(nc, k):
    for n, src in enumerate((k.expert, k.best)):
        last = nc.tensor.transpose(k.ps[:, 6, n * P:n * P + P], src[:].rearrange("p h k -> p (h k)"), k.ident[:])
    return last


def stage_query(nc, k):
    with ExitStack() as ctx:
        sb = lambda n, s, d=F32: ctx.enter_context(nc.sbuf_tensor("r_" + n, s, d))
        sem = lambda n: ctx.enter_context(nc.semaphore("r_" + n))
        NW, HC, NS_BUF = 6, 2 * PH, 4
        wbuf = sb("w", [P, NW, KD, P])
        sk = sb("sk", [P, HC, P])
        skT = sb("skT", [P, HC, P])
        qT = sb("qT", [P, 2, T])
        s = sb("s", [P, NS_BUF, TILES, P])
        iota = sb("iota", [P, TOPK], I32)
        w_in = [sem(f"w_in{i}") for i in range(NW)]
        s_out = [sem(f"s_out{i}") for i in range(NS_BUF)]
        (sk_in, sk_turned, sk_copied, projected, q_copied, scored, s_copied, ranked, own_s, pool_s, iota_done, shifted,
         exped, routed, routed_turned) = (
            sem(n) for n in ("sk_in", "sk_turned", "sk_copied", "projected", "q_copied", "scored", "s_copied", "ranked",
                             "own", "pool", "iota", "shifted", "exped", "routed", "routed_turned"))
        block = ctx.enter_context(nc.Block())

        @block.sync
        def _(sp):
            for i in range(HC):
                if i == 2:
                    sp.dma_start(sk[:], k.peer_sub_keys[0].rearrange("h c k d -> k (h c) d")).then_inc(sk_in, 16)
                if i >= NW:
                    sp.wait_ge(projected, i - NW + 1)
                sp.dma_start(wbuf[:, i % NW], w_view(k.peer_wq, P * i, P)).then_inc(w_in[i % NW], 16)

        @block.gpsimd
        def _(pool):
            own = Link(pool, pool_s)
            own(nc.gpsimd.iota(iota[:], pattern=[[1, TOPK]], base=0, channel_multiplier=0))
            own(nc.gpsimd.tensor_copy(k.iotaf[:], iota[:]))
            nc.gpsimd.memset(s[NS:P, :, TILES - 1, :], 0.0).then_inc(iota_done, 1)
            pool.wait_ge(iota_done, 1)
            own(nc.gpsimd.memset(k.sel[:], 1.0))
            for c in range(3):
                part = k.sel[HG * c:HG * c + HG]
                own(nc.gpsimd.affine_select(out=part, in_=part, compare_op=ALU.is_equal, fill=0.0, base=0,
                                            pattern=[[-1, HG], [0, P]], channel_multiplier=1))
            own(nc.gpsimd.memset(k.wz[:], 0.0))
            for i in range(HC):
                pool.wait_ge(s_copied, i + 1)
                pool.dma_start(k.scores_dram[:, :, i, :].rearrange("t p n -> p t n"), s[:, i % NS_BUF, 1:TILES, :]).then_inc(
                    s_out[i % NS_BUF], 16)
            for i in range(NS_BUF):
                pool.wait_ge(s_out[i], 16 * (HC // NS_BUF))

        @block.tensor
        def _(pe):
            mm = nc.tensor.matmul

            def turn_keys():
                pe.wait_ge(sk_in, 16)
                for q in range(HC // 4):
                    for i in range(4):
                        last = nc.tensor.transpose(k.ps[:, 4 + q, i * P:i * P + P], sk[:, 4 * q + i, :], k.ident[:])
                    last.then_inc(sk_turned, 1)

            def query(i):
                pe.wait_ge(w_in[i % NW], 16 * (i // NW + 1))
                if i >= 2:
                    pe.wait_ge(q_copied, i - 1)
                for bank, cols in ((k.ps[:, 2 * (i % 2), :], slice(0, SEQ)), (k.ps[:, 2 * (i % 2) + 1, 0:NS], slice(SEQ, T))):
                    for f in range(KD):
                        last = mm(bank, wbuf[:, i % NW, f, :], k.hT[:, f, cols], start=(f == 0), stop=(f == KD - 1))
                last.then_inc(projected, 1)

            def score(i):
                pe.wait_ge(q_copied, i + 1)
                if i >= 2:
                    pe.wait_ge(s_copied, i - 1)
                for t in range(TILES):
                    r = rows(t)
                    b, c = 4 + 2 * (i % 2) + t // 4, (t % 4) * P
                    last = mm(k.ps[0:r, b, c:c + P], qT[:, i % 2, P * t:P * t + r], skT[:, i, :], start=True, stop=True)
                last.then_inc(scored, 1)

            for i in range(HC + 1):
                if i < HC:
                    query(i)
                if i == 1:
                    turn_keys()
                    pe.wait_ge(sk_copied, 4)
                if i:
                    score(i - 1)
            pe.wait_ge(s_copied, HC)
            pe.wait_ge(routed, 1)
            turn_routes(nc, k).then_inc(routed_turned, 1)

        @block.scalar
        def _(act):
            a = nc.scalar
            def copy_keys(q):
                act.wait_ge(sk_turned, q + 1)
                a.copy(skT[:, 4 * q:4 * q + 4, :], k.ps[:, 4 + q, :].rearrange("p (i n) -> p i n", i=4)).then_inc(sk_copied, 1)

            def copy_s(i):
                act.wait_ge(scored, i + 1)
                if i >= NS_BUF:
                    act.wait_ge(s_out[i % NS_BUF], 16 * (i // NS_BUF))
                    act.wait_ge(ranked, (i - NS_BUF) // 2 + 1)
                else:
                    act.wait_ge(iota_done, 1)
                b = 4 + 2 * (i % 2)
                a.copy(s[:, i % NS_BUF, 0:4, :], k.ps[:, b, :].rearrange("p (t n) -> p t n", t=4))
                a.copy(s[0:NS, i % NS_BUF, 4, :], k.ps[0:NS, b + 1, 0:P]).then_inc(s_copied, 1)

            for i in range(HC + 1):
                if i < HC:
                    act.wait_ge(projected, i + 1)
                    if i >= 2:
                        act.wait_ge(scored, i - 1)
                    a.copy(qT[:, i % 2, 0:SEQ], k.ps[:, 2 * (i % 2), :])
                    a.copy(qT[:, i % 2, SEQ:T], k.ps[:, 2 * (i % 2) + 1, 0:NS]).then_inc(q_copied, 1)
                if i == 1:
                    for q in range(4):
                        copy_keys(q)
                if i:
                    copy_s(i - 1)
            act.wait_ge(shifted, 1)
            a.activation(k.best[:], k.best[:], ACT.Exp).then_inc(exped, 1)

        @block.vector
        def _(dve):
            v = nc.vector
            own = Link(dve, own_s)
            dve.wait_ge(iota_done, 1)
            for h in range(PH):
                dve.wait_ge(s_copied, 2 * h + 2)
                rank_halves(v, own, k, [s[:, (2 * h + c) % NS_BUF, 0, :] for c in range(2)])
                dve.sem_inc(ranked, 1)
                rank_sums(v, own, k, h)
                name_experts(v, own, k, h)
            shift_best(v, own, k).then_inc(shifted, 1)
            dve.wait_ge(exped, 1)
            share_best(v, own, k).then_inc(routed, 1)


def stage_experts(nc, k):
    with ExitStack() as ctx:
        sb = lambda n, s, d=F32: ctx.enter_context(nc.sbuf_tensor("e_" + n, s, d))
        sem = lambda n: ctx.enter_context(nc.semaphore("e_" + n))
        G, NU, NV, B = HG, 16, 16, 4
        BATCHES = P // B
        ubuf, vbuf = sb("u", [P, NU, D]), sb("v", [P, NV, D])
        hp = sb("hp", [3 * G, 2, D], BF16)
        x1, y, junk, row = (sb(n, [P, D]) for n in ("x1", "y", "junk", "row"))
        idx = sb("idx", [P, P], U32)
        rw = sb("rw", [P, P])
        dot, act_ = sb("dot", [P, P]), sb("act", [P, P])
        RING, sel, wz = WRING, k.sel, k.wz
        ss, mean, root, rstd = (sb(n, [P, 1]) for n in ("ss", "mean", "root", "rstd"))
        s_cur = k.mT[:].rearrange("p f t -> p (f t)")[:, 0:2 * PH * P].rearrange("p (i n) -> p i n", n=P)
        u_in = [sem(f"u_in{i}") for i in range(NU)]
        v_in = [sem(f"v_in{i}") for i in range(NV)]
        hp_in = [sem(f"hp_in{i}") for i in range(2)]
        (row_in, x1_in, s_in, y_out, staged, spread, dotted, gelud, weighed, summed, added, squared, averaged, rooted,
         scaled, y_done, own_s, shifted, exped, routed, routes_turned, passed_sp, passed_pool, passed_dve) = (
            sem(n) for n in ("row_in", "x1_in", "s_in", "y_out", "staged", "spread", "dotted", "gelud", "weighed",
                             "summed", "added", "squared", "averaged", "rooted", "scaled", "y_done", "own", "shifted",
                             "exped", "routed", "routes_turned", "passed_sp", "passed_pool", "passed_dve"))
        DOT0, SPREAD0, SUM0, ONE0 = NU, 2 * G, BATCHES, 1
        LATE = 20
        OWN = 17 * PH + 3
        block = ctx.enter_context(nc.Block())
        u_rows, v_rows = k.peer_u, k.peer_v

        def in_turn(eng, body):
            with eng.Fori(0, TILES - 1) as it:
                body(it, P)
            body(TILES - 1, NS)

        @block.sync
        def _(sp):
            sp.sem_inc(dotted, DOT0)
            sp.sem_inc(spread, SPREAD0)
            sp.sem_inc(summed, SUM0)
            for one in (added, y_done, routed, routes_turned):
                sp.sem_inc(one, ONE0)
            sp.sem_inc(y_out, 64)
            sp.dma_start(row[:], k.final_norm_w.rearrange("(a d) -> a d", a=1).partition_broadcast(P)[:, 0, :]).then_inc(row_in, 16)

            def load_h(it, g):
                for c in range(3):
                    sp.dma_start(hp[G * c:G * c + G, g % 2, :], k.parts_dram[c][bass.ds(it * P + g * G, G)]).then_inc(
                        hp_in[g % 2], 16)

            load_h(0, 0)
            load_h(0, 1)

            def body(it, n):
                quarter = lambda dram: dram.rearrange("(q b) d -> b q d", b=B)
                hold(sp, y_done, it + ONE0, passed_sp)
                for b in range(B):
                    sp.dma_start(x1[32 * b:32 * b + n // B], quarter(k.x1_dram[bass.ds(it * P, n)])[b]).then_inc(x1_in, 16)
                if n == P:
                    hold(sp, routed, it + ONE0, passed_sp)
                    sp.dma_start(s_cur, k.scores_dram[bass.ds(it, 1)].rearrange("a p i n -> p (a i) n")).then_inc(s_in, 16)
                    for g in range(2, 2 + P // G):
                        hold(sp, spread, it * P + G * (g - 1) + SPREAD0, passed_sp)
                        load_h(it, g)
                hold(sp, y_done, it + 1 + ONE0, passed_sp)
                dst = k.y_prompt[0][bass.ds(it * P, n)] if n == P else k.y_sample.rearrange("b t d -> (b t) d")
                for b in range(B):
                    sp.dma_start(quarter(dst)[b], y[32 * b:32 * b + n // B]).then_inc(y_out, 16)
            in_turn(sp, body)
            sp.wait_ge(y_out, 64 * (TILES + 1))

        @block.gpsimd
        def _(pool):
            g = nc.gpsimd

            def body(it, n):
                for t in range(n):
                    off = bass.IndirectOffsetOnAxis(ap=idx[:, t:t + 1], axis=0)
                    hold(pool, dotted, it * P + t + 1 - NU + DOT0, passed_pool)
                    if t % NS == 0:
                        hold(pool, staged, it * 2 + t // NS + 1, passed_pool)
                    g.indirect_dma_start(out=ubuf[:, t % NU, :], out_offset=None, in_=u_rows, in_offset=off).then_inc(
                        u_in[t % NU], 16)
                    if t % B == 0:
                        hold(pool, summed, it * BATCHES + (t - NV) // B + 1 + SUM0, passed_pool)
                    g.indirect_dma_start(out=vbuf[:, t % NV, :], out_offset=None, in_=v_rows, in_offset=off).then_inc(
                        v_in[t % NV], 16)
            in_turn(pool, body)

        @block.tensor
        def _(pe):
            mm = nc.tensor.matmul

            def spread_h(it, t):
                g, col = t // G, t % G
                if col == 0:
                    pe.wait_ge(hp_in[g % 2], it * 96 + 48 * (g // 2) + 48)
                pe.wait_ge(dotted, it * P + t - 1 + DOT0)
                for i in range(2):
                    last = mm(k.ps[:, 2 * (t % 2) + i, :], sel[:, col, :], hp[:, g % 2, 512 * i:512 * i + 512], start=True,
                              stop=True)
                last.then_inc(spread, 1)

            def sum_v(it, n, q):
                pe.wait_ge(weighed, it * BATCHES + q + 1)
                if q == 0:
                    pe.wait_ge(added, it + ONE0)
                for b in range(B):
                    t = B * q + b
                    pe.wait_ge(v_in[t % NV], 16 * (P // NV) * it + 16 * (t // NV + 1))
                for i in range(2):
                    for b in range(B):
                        t = B * q + b
                        at = 31 + 32 * (t % RING) - q
                        last = mm(k.ps[32 * b:32 * b + 32, 4 + i, :], wz[:, at:at + 32],
                                  vbuf[:, t % NV, 512 * i:512 * i + 512], start=(q == 0), stop=(q == n // B - 1),
                                  skip_group_check=True)
                last.then_inc(summed, 1)

            def body(it, n):
                for t in range(n + B):
                    if t < n:
                        spread_h(it, t)
                    if t % B == B - 1 and t > B:
                        sum_v(it, n, t // B - 1)
                    if n == P and t == 104:
                        pe.wait_ge(routed, it + 1 + ONE0)
                        pe.wait_ge(staged, it * 2 + 2)
                        turn_routes(nc, k).then_inc(routes_turned, 1)
            in_turn(pe, body)

        @block.vector
        def _(dve):
            v = nc.vector
            dve.wait_ge(row_in, 16)

            def weigh(it, q):
                dve.wait_ge(gelud, it * BATCHES + q + 1)
                dve.wait_ge(summed, it * BATCHES + q + 1 - RING // B + SUM0)
                at = 31 + 32 * (B * q % RING)
                v.tensor_tensor(wz[:, at:at + 32 * (B - 1) + 1:32], act_[:, q * B:q * B + B], rw[:, q * B:q * B + B],
                                ALU.mult).then_inc(weighed, 1)

            def finish(it, n):
                dve.wait_ge(summed, it * BATCHES + n // B + SUM0)
                dve.wait_ge(x1_in, it * 64 + 64)
                for i in range(2):
                    c = slice(512 * i, 512 * i + 512)
                    last = v.tensor_tensor(x1[:, c], x1[:, c], k.ps[:, 4 + i, :], ALU.add)
                last.then_inc(added, 1)
                dve.wait_ge(squared, it + 1)
                v.tensor_scalar(mean[:], ss[:], 1.0 / D, EPS, ALU.mult, ALU.add).then_inc(averaged, 1)
                dve.wait_ge(rooted, it + 1)
                v.reciprocal(rstd[:], root[:]).then_inc(scaled, 1)
                dve.wait_ge(y_out, it * 64 + 64)
                dve.wait_ge(scaled, it + 1)
                v.scalar_tensor_tensor(out=y[:], in0=x1[:], scalar=rstd[:], in1=row[:], op0=ALU.mult,
                                       op1=ALU.mult).then_inc(y_done, 1)

            def body(it, n):
                own = LoopLink(dve, own_s, it, OWN, passed_dve)
                for t in range(n):
                    dve.wait_ge(u_in[t % NU], 16 * (P // NU) * it + 16 * (t // NU + 1))
                    dve.wait_ge(spread, it * P + t + 1 + SPREAD0)
                    uu = ubuf[:, t % NU, :]
                    v.tensor_tensor_reduce(uu, uu, k.ps[:, 2 * (t % 2):2 * (t % 2) + 2, :].rearrange("p a b -> p (a b)"),
                                           1.0, 0.0, ALU.mult, ALU.add, dot[:, t:t + 1]).then_inc(dotted, 1)
                    if t % B == 1 and t > B:
                        weigh(it, t // B - 1)
                    if n < P:
                        continue
                    h, step = divmod(t - LATE, 9)
                    if t == LATE:
                        hold(dve, s_in, it * 16 + 16, passed_dve)
                        hold(dve, routes_turned, it + ONE0, passed_dve)
                    if 0 <= h < PH and step == 1:
                        rank_halves(v, own, k, [s_cur[:, 2 * h + c, :] for c in range(2)])
                    if 0 <= h < PH and step == 4:
                        rank_sums(v, own, k, h)
                    if 0 <= h < PH and step == 7:
                        name_experts(v, own, k, h)
                    if t == LATE + 9 * PH:
                        shift_best(v, own, k).then_inc(shifted, 1)
                    if t == LATE + 9 * PH + 5:
                        hold(dve, exped, it + 1, passed_dve)
                        share_best(v, own, k).then_inc(routed, 1)
                weigh(it, n // B - 1)
                assert n < P or own.n == OWN, own.n
                finish(it, n)
            in_turn(dve, body)

        @block.scalar
        def _(act):
            a = nc.scalar

            def stage(it, half):
                act.wait_ge(summed, it * BATCHES + (half - 1) * BATCHES // 2 + SUM0)
                act.wait_ge(routes_turned, it + ONE0)
                c = slice(NS * half, NS * half + NS)
                a.copy(idx[:, c], k.ps[:, 6, c])
                a.copy(rw[:, c], k.ps[:, 6, P + NS * half:P + NS * half + NS]).then_inc(staged, 1)

            def body(it, n):
                for q in range(n // B):
                    act.wait_ge(dotted, it * P + B * (q + 1) + DOT0)
                    a.activation(act_[:, B * q:B * q + B], dot[:, B * q:B * q + B], ACT.Gelu_apprx_tanh).then_inc(gelud, 1)
                    if n == P and q == 4:
                        stage(it, 1)
                    if n == P and q == 26:
                        stage(it + 1, 0)
                    if n == P and q == 22:
                        act.wait_ge(shifted, it + 1)
                        a.activation(k.best[:], k.best[:], ACT.Exp).then_inc(exped, 1)
                act.wait_ge(added, it + 1 + ONE0)
                a.activation(junk[:], x1[:], ACT.Square, accum_out=ss[:]).then_inc(squared, 1)
                act.wait_ge(averaged, it + 1)
                a.activation(root[:], mean[:], ACT.Sqrt).then_inc(rooted, 1)
            stage(0, 0)
            in_turn(act, body)




def build(nc, k):
    with ExitStack() as ctx:
        allocate(nc, k, ctx)
        stage_norm(nc, k)
        with ExitStack() as ssm:
            allocate_ssm(nc, k, ssm)
            stage_conv(nc, k)
            natural_projection(nc, k, "z", z_blocks(k))
            stage_decays(nc, k)
            stage_sample_state(nc, k)
            stage_ssd(nc, k)
            stage_gate(nc, k)
            stage_branch(nc, k, "bs", COL_BG, k.w_ssm_branch, 16, load_rows,
                         lambda f: k.xnat[:, 0:4, P * f:P * f + P], lambda f: yT(k, 4)[:, f, :], False)
        with ExitStack() as attn:
            allocate_attn(nc, k, attn)
            natural_projection(nc, k, "kv", kv_blocks(k))
            stage_qk(nc, k)
            stage_cmp_prompt(nc, k)
            stage_attn_prompt(nc, k)
            clear_semaphores(nc)
            stage_cmp_sample(nc, k)
            stage_attn_sample(nc, k)
            stage_branch(nc, k, "ba", COL_BG + D, k.w_attn_branch, HPK, load_head_rows,
                         lambda f: k.oT[:, f, 0:SEQ], lambda f: k.oT[:, f, SEQ:T], True)
        with ExitStack() as peer:
            allocate_peer(nc, k, peer)
            stage_out(nc, k)
            stage_query(nc, k)
            stage_experts(nc, k)


def clear_semaphores(nc):
    free = sorted(nc.free_semaphores)
    assert free == list(range(free[0], free[-1] + 1))
    with nc.Block() as block:
        @block.gpsimd
        def _(pool):
            pool.sem_clear(range(free[0], free[-1] + 1))


def allocate(nc, k, ctx):
    k.page_in = [ctx.enter_context(nc.semaphore(f"page_in{i}")) for i in range(3)]
    sb = lambda n, s, d=F32: ctx.enter_context(nc.sbuf_tensor(n, s, d))
    k.ps = ctx.enter_context(nc.psum_tensor("ps", [P, 8, 512], F32))
    k.ident, k.ones, k.cum = sb("ident", [P, P]), sb("ones", [P, P]), sb("cum", [P, P])
    k.identb, k.later, k.causal = sb("identb", [P, P], BF16), sb("later", [P, P], BF16), sb("causal", [P, P], BF16)
    k.same, k.cum_s, k.later_s = sb("same", [NS, NS]), sb("cum_s", [NS, NS]), sb("later_s", [NS, NS], BF16)
    k.dt_bias_row, k.a_row, k.dskip_row = (sb(n, [P, HEADS]) for n in ("dt_bias_row", "a_row", "dskip_row"))
    k.vcol = sb("vcol", [P, 152])
    k.norm_mix_col, k.norm_ffn_col, k.ssm_norm_col = k.vcol[:, 0:8], k.vcol[:, 8:16], k.vcol[:, 16:32]
    k.conv_b_col, k.conv_w_col = k.vcol[:, 32:56], k.vcol[:, 56:152]
    k.hT = sb("hT", [P, KD, T])
    k.mT = sb("mT", [P, KD, T])
    k.BT, k.CT = k.mT[:, 0:4, :], k.mT[:, 4:8, :]


def allocate_ssm(nc, k, ctx):
    sb = lambda n, s, d=F32: ctx.enter_context(nc.sbuf_tensor(n, s, d))
    k.xnat = sb("xnat", [P, TILES, D_INNER])
    k.znat = sb("znat", [P, TILES, D_INNER])
    k.Bnat = sb("Bnat", [P, TILES, GROUPS * STATE])
    k.dt, k.da, k.nacum, k.eacum, k.to_end, k.cdec = (
        sb(n, [P, TILES, HEADS]) for n in ("dt", "da", "nacum", "eacum", "to_end", "cdec"))
    k.tail_dec = sb("tail_dec", [P, 16, NB])
    k.yt = sb("yt", [P, 16, NS])
    k.ysq = sb("ysq", [P, TILES, GROUPS])


def allocate_attn(nc, k, ctx):
    sb = lambda n, s, d=F32: ctx.enter_context(nc.sbuf_tensor(n, s, d))
    k.qT = sb("qT", [P, HPK, T])
    k.ksT, k.kwT = sb("ksT", [P, T]), sb("kwT", [P, T])
    k.kv = sb("kv", [P, TILES, 3 * KVW])
    k.gates = sb("gates", [P, TILES, 3 * AH])
    k.oT = sb("oT", [P, HPK, T])
    k.onat = sb("onat", [P, 4, AH * HD])
    k.pages = sb("pages", [P, 2, NPAGES, KVW])
    k.means = sb("means", [P, NB, KVW])
    k.page_row = sb("page_row", [1, NB * NPAGES], I32)
    k.grow = sb("grow", [P, NB, 3])
    k.qb = sb("qb", [P, NB, P])
    k.acc = sb("acc", [P, NB, P])
    k.sel_bias = sb("sel_bias", [P, NB, NSEL])
    k.step_mask, k.old_mask = sb("step_mask", [P, DS]), sb("old_mask", [P, DS])
    k.new_mask = sb("new_mask", [P, NB, NS])
    k.gates_dram = nc.dram_tensor("gates_scratch", (NS, 3 * AH), F32).ap()


def allocate_peer(nc, k, ctx):
    sb = lambda n, s, d=F32: ctx.enter_context(nc.sbuf_tensor(n, s, d))
    k.top = sb("top", [P, 2, TOPK])
    k.at, k.atf = sb("at", [P, 2, TOPK], U32), sb("atf", [P, 2, TOPK])
    k.cand = sb("cand", [P, TOPK * TOPK])
    k.pos, k.half, k.halff = sb("pos", [P, TOPK], U32), sb("half", [P, 2, TOPK], U32), sb("halff", [P, 2, TOPK])
    k.iotaf, k.hit, k.pick = sb("iotaf", [P, TOPK]), sb("hit", [P, 2, TOPK, TOPK]), sb("pick", [P, 2, TOPK])
    k.best, k.expert = sb("best", [P, PH, TOPK]), sb("expert", [P, PH, TOPK])
    k.den = sb("den", [P, PH])
    k.sel = sb("sel", [3 * HG, HG, P], BF16)
    k.wz = sb("wz", [P, 32 * (WRING + 1)])
    k.scores_dram = nc.dram_tensor("scores_scratch", (TILES - 1, P, 2 * PH, P), F32).ap()
    k.x1_dram = nc.dram_tensor("x1_scratch", (T, D), F32).ap()
    k.parts_dram = nc.dram_tensor("h_parts_scratch", (3, T, D), BF16).ap()


def z_blocks(k):
    def z(i):
        return lambda t: k.znat[0:rows(t), t, 512 * i:512 * i + 512]
    return [(COL_Z + 512 * i, 512, z(i), ACT.Silu) for i in range(4)] + [
        (COL_DT, HEADS, lambda t: k.dt[0:rows(t), t, :], ACT.Copy)]


def kv_blocks(k):
    return [(COL_KV, 512, lambda t: k.kv[0:rows(t), t, 0:512], ACT.Copy),
            (COL_KV + 512, 256, lambda t: k.kv[0:rows(t), t, 512:768], ACT.Copy),
            (COL_NG, 3 * AH, lambda t: k.gates[0:rows(t), t, :], ACT.Sigmoid)]


INPUTS = ['x_prompt', 'x_sample', 'cache_cmp_kv', 'cache_sel_kv', 'cache_win_kv', 'state_ssm', 'state_conv',
          'page_table', 'norm_mix_w', 'w_in', 'conv_w', 'conv_b', 'dt_bias', 'a_log', 'd_skip', 'ssm_norm_w',
          'w_ssm_branch', 'w_attn_branch', 'w_out', 'norm_ffn_w', 'peer_wq', 'peer_sub_keys', 'peer_u', 'peer_v',
          'final_norm_w']
OUTPUTS = [('y_prompt', (1, SEQ, D)), ('y_sample', (NB, DS, D)),
           ('new_cmp_kv_prompt', (1, 1, SEQ, KVH, 2, HD)), ('new_cmp_kv_sample', (1, NB, DS, KVH, 2, HD)),
           ('new_sel_kv_prompt', (1, 1, SEQ, KVH, 2, HD)), ('new_sel_kv_sample', (1, NB, DS, KVH, 2, HD)),
           ('new_win_kv_prompt', (1, 1, WINDOW, KVH, 2, HD)), ('new_win_kv_sample', (1, NB, WINDOW, KVH, 2, HD)),
           ('new_ssm_prompt', (1, 1, HEADS, HP, STATE)), ('new_ssm_sample', (1, NB, HEADS, HP, STATE)),
           ('new_conv_prompt', (1, 1, CONV_W - 1, CONV_DIM)), ('new_conv_sample', (1, NB, CONV_W - 1, CONV_DIM))]
MATRICES = ('w_in', 'w_ssm_branch', 'w_attn_branch', 'w_out', 'peer_wq', 'peer_u', 'peer_v')


def name_tensors(k, aps):
    (k.x_prompt, k.x_sample, k.cache_cmp_kv, k.cache_sel_kv, k.cache_win_kv, k.state_ssm, k.state_conv,
     k.page_table, k.norm_mix_w, k.w_in, k.conv_w, k.conv_b, k.dt_bias, k.a_log, k.d_skip, k.ssm_norm_w,
     k.w_ssm_branch, k.w_attn_branch, k.w_out, k.norm_ffn_w, k.peer_wq, k.peer_sub_keys, k.peer_u, k.peer_v,
     k.final_norm_w) = (aps[name] for name in INPUTS)
    (k.y_prompt, k.y_sample, k.new_cmp_kv_prompt, k.new_cmp_kv_sample, k.new_sel_kv_prompt, k.new_sel_kv_sample,
     k.new_win_kv_prompt, k.new_win_kv_sample, k.new_ssm_prompt, k.new_ssm_sample, k.new_conv_prompt,
     k.new_conv_sample) = (aps[name] for name, _ in OUTPUTS)


def kernel(**inputs):
    import numpy as np
    import concourse.bacc as bacc
    from concourse.bass_utils import run_bass_kernel_spmd

    nc = bacc.Bacc("TRN2", target_bir_lowering=False, num_devices=1)
    arrays, aps = {}, {}
    for name in INPUTS:
        a = np.ascontiguousarray(inputs[name])
        arrays[f"in_{name}"] = a
        ap = nc.dram_tensor(f"in_{name}", a.shape, mybir.dt.from_np(a.dtype), kind="ExternalInput").ap()
        aps[name] = ap[0] if name in MATRICES else ap
    for name, shape in OUTPUTS:
        aps[name] = nc.dram_tensor(f"out_{name}", shape, F32, kind="ExternalOutput").ap()
    k = Shared()
    name_tensors(k, aps)
    build(nc, k)
    r = run_bass_kernel_spmd(nc, [arrays], core_ids=[0])
    return tuple(r.results[0][f"out_{name}"] for name, _ in OUTPUTS)
```
